# Optimizing a Trainium2 kernel written in Bass

```python
import jax, jax.numpy as jnp
from jax import lax
import numpy as np

D_MODEL = 1024
BATCH = 1
SEQ = 256
DEPTH = 2

D_MIX = D_MODEL
GLA_HEADS = 4
GLA_DV = D_MIX // 2 // GLA_HEADS
GLA_DK = GLA_DV // 2
GLA_RANK = 16
GLA_GATE_NORM = 16.0
HG_HEADS = 4
HG_DK = 128
HG_DV = D_MIX // 2 // HG_HEADS
CHUNK = 64
D_FF_DENSE = 2816
N_EXPERTS = 8
TOP_K = 2
D_FF_EXPERT = 3584
PLE_DIM = 256
EPS = 1e-6
HEAD_EPS = 1e-5
F_MIN = 1e-6

GLA_QK = GLA_HEADS * GLA_DK
GLA_V = GLA_HEADS * GLA_DV
HG_K = HG_HEADS * HG_DK
HG_V = HG_HEADS * HG_DV
IN_SPLIT_SIZES = (GLA_QK, GLA_QK, GLA_V, GLA_V, GLA_RANK, GLA_RANK,
                  HG_K, HG_K, HG_K, HG_V, HG_V)
D_IN_PROJ = sum(IN_SPLIT_SIZES)

kernel_name = "hybrid_gla_hgrn2_moe_bidir_encoder"

def rmsnorm(x, w, eps=EPS):
    xf = x.astype(jnp.float32)
    y = xf * lax.rsqrt(jnp.mean(xf * xf, axis=-1, keepdims=True) + eps)
    return (y * w.astype(jnp.float32)).astype(x.dtype)

def to_heads(a, n_heads):
    b, s, _ = a.shape
    return a.reshape(b, s, n_heads, -1).transpose(0, 2, 1, 3)

def chunk_gla(q, k, v, log_g):
    bn, h, t, dk = q.shape
    dv = v.shape[-1]
    n = t // CHUNK

    def to_chunks(a):
        return jnp.moveaxis(a.reshape(bn, h, n, CHUNK, a.shape[-1]), 2, 0)

    mask = jnp.tril(jnp.ones((CHUNK, CHUNK), dtype=bool))[:, :, None]
    mask_f = mask.astype(jnp.float32)

    def step(state, inp):
        q_c, k_c, v_c, g_c = inp
        b = jnp.cumsum(g_c, axis=-2)
        o_inter = jnp.einsum('bhck,bhkv->bhcv', q_c * jnp.exp(b), state)
        diff = b[:, :, :, None, :] - b[:, :, None, :, :]
        decay = jnp.exp(jnp.where(mask, diff, 0.0)) * mask_f
        scores = jnp.einsum('bhtsk,bhsk->bhts', q_c[:, :, :, None, :] * decay, k_c)
        o = o_inter + jnp.einsum('bhts,bhsv->bhtv', scores, v_c)
        b_last = b[:, :, -1:, :]
        state = (jnp.exp(b_last[:, :, 0, :])[..., None] * state
                 + jnp.einsum('bhsk,bhsv->bhkv', k_c * jnp.exp(b_last - b), v_c))
        return state, o

    s0 = jnp.zeros((bn, h, dk, dv), jnp.float32)
    _, o = lax.scan(step, s0, (to_chunks(q), to_chunks(k), to_chunks(v), to_chunks(log_g)))
    return jnp.moveaxis(o, 0, 2).reshape(bn, h, t, dv)

def bidir_gla(q, k_f, k_b, v, g_f, g_b):
    flip = lambda a: jnp.flip(a, axis=2)
    bsz = q.shape[0]
    o = chunk_gla(jnp.concatenate([q, flip(q)], 0),
                  jnp.concatenate([k_f, flip(k_b)], 0),
                  jnp.concatenate([v, flip(v)], 0),
                  jnp.concatenate([g_f, flip(g_b)], 0))
    return o[:bsz] + flip(o[bsz:])

def gated_head_norm(o, gate, w):
    o = o * lax.rsqrt(jnp.mean(o * o, axis=-1, keepdims=True) + HEAD_EPS) * w.astype(jnp.float32)
    b, h, s, dv = o.shape
    o = o.transpose(0, 2, 1, 3).reshape(b, s, h * dv)
    return o * jax.nn.silu(gate)

def hgrn_forget(z, lb):
    f = lb + (1.0 - lb) * jax.nn.sigmoid(z)
    log_f = jnp.log(jnp.maximum(f, F_MIN))
    k = (1.0 - lb) * jax.nn.sigmoid(-z)
    return log_f, k

def swiglu(v, wg, wu, wd):
    return (jax.nn.silu(v @ wg) * (v @ wu)) @ wd

def moe_swiglu(v, w_router, wg, wu, wd):
    logits = (v @ w_router).astype(jnp.float32)
    probs = jax.nn.softmax(logits, axis=-1)
    top_w, top_i = lax.top_k(probs, TOP_K)
    top_w = top_w / jnp.sum(top_w, axis=-1, keepdims=True)
    gates = jnp.sum(jax.nn.one_hot(top_i, N_EXPERTS, dtype=jnp.float32) * top_w[..., None], axis=-2)
    y = jnp.zeros(v.shape, jnp.float32)
    for e in range(N_EXPERTS):
        y = y + gates[..., e:e + 1] * swiglu(v, wg[e], wu[e], wd[e]).astype(jnp.float32)
    return y.astype(v.dtype)

def setup_inputs(seed: int = 0) -> dict:
    key = jax.random.key(seed)
    ks = jax.random.split(key, 24)
    f32 = jnp.float32

    def nrm(k, shape, fan_in):
        return jax.random.normal(k, shape, f32) * (fan_in ** -0.5)

    def gain(k, shape):
        return 1.0 + 0.05 * jax.random.normal(k, shape, f32)

    n_dense = (DEPTH + 1) // 2
    n_moe = DEPTH // 2
    return {
        "x": jax.random.normal(ks[0], (BATCH, SEQ, D_MODEL), f32),
        "p": jax.random.normal(ks[1], (DEPTH, BATCH, SEQ, PLE_DIM), f32),
        "w_in": nrm(ks[2], (DEPTH, D_MODEL, D_IN_PROJ), D_MODEL),
        "gla_wg2": nrm(ks[3], (DEPTH, 2, GLA_RANK, GLA_QK), GLA_RANK),
        "gla_bg": 0.1 * jax.random.normal(ks[4], (DEPTH, 2, GLA_QK), f32),
        "hg_lb_logits": jax.random.normal(ks[5], (DEPTH, 2, HG_K), f32),
        "gla_onorm": gain(ks[6], (DEPTH, GLA_DV)),
        "hg_onorm": gain(ks[7], (DEPTH, HG_DV)),
        "w_out": nrm(ks[8], (DEPTH, D_MIX, D_MODEL), D_MIX),
        "norm_mix": gain(ks[9], (DEPTH, D_MODEL)),
        "norm_ffn": gain(ks[10], (DEPTH, D_MODEL)),
        "w_dense_gate": nrm(ks[11], (n_dense, D_MODEL, D_FF_DENSE), D_MODEL),
        "w_dense_up": nrm(ks[12], (n_dense, D_MODEL, D_FF_DENSE), D_MODEL),
        "w_dense_down": nrm(ks[13], (n_dense, D_FF_DENSE, D_MODEL), D_FF_DENSE),
        "w_router": nrm(ks[14], (n_moe, D_MODEL, N_EXPERTS), D_MODEL),
        "w_exp_gate": nrm(ks[15], (n_moe, N_EXPERTS, D_MODEL, D_FF_EXPERT), D_MODEL),
        "w_exp_up": nrm(ks[16], (n_moe, N_EXPERTS, D_MODEL, D_FF_EXPERT), D_MODEL),
        "w_exp_down": nrm(ks[17], (n_moe, N_EXPERTS, D_FF_EXPERT, D_MODEL), D_FF_EXPERT),
        "w_ple_proj": nrm(ks[18], (DEPTH, PLE_DIM, D_MODEL), PLE_DIM),
        "w_ple_gate": nrm(ks[19], (DEPTH, D_MODEL, D_MODEL), D_MODEL),
        "norm_ple": gain(ks[20], (DEPTH, D_MODEL)),
        "norm_final": gain(ks[21], (D_MODEL,)),
    }

def reference(x, p, w_in, gla_wg2, gla_bg, hg_lb_logits, gla_onorm, hg_onorm, w_out,
              norm_mix, norm_ffn, w_dense_gate, w_dense_up, w_dense_down, w_router,
              w_exp_gate, w_exp_up, w_exp_down, w_ple_proj, w_ple_gate, norm_ple,
              norm_final):
    f32 = jnp.float32
    offsets = np.cumsum(IN_SPLIT_SIZES)[:-1].tolist()
    lb_p = jax.nn.softmax(hg_lb_logits.astype(f32), axis=0)
    lb_all = jnp.cumsum(lb_p, axis=0) - lb_p[0:1]

    h = x
    for i in range(DEPTH):
        u = rmsnorm(h, norm_mix[i])
        proj = (u @ w_in[i]).astype(f32)
        (gq, gk, gv, gr, glr_f, glr_b,
         hq, hf_f, hf_b, hv, hr) = jnp.split(proj, offsets, axis=-1)

        wg2 = gla_wg2[i].astype(f32)
        bg = gla_bg[i].astype(f32)
        g_f = jax.nn.log_sigmoid(glr_f @ wg2[0] + bg[0]) / GLA_GATE_NORM
        g_b = jax.nn.log_sigmoid(glr_b @ wg2[1] + bg[1]) / GLA_GATE_NORM
        k_gla = to_heads(gk, GLA_HEADS)
        o_gla = bidir_gla(to_heads(gq, GLA_HEADS) * (GLA_DK ** -0.5), k_gla, k_gla,
                          to_heads(gv, GLA_HEADS),
                          to_heads(g_f, GLA_HEADS), to_heads(g_b, GLA_HEADS))
        y_gla = gated_head_norm(o_gla, gr, gla_onorm[i])

        lb = lb_all[i]
        log_f_f, k_f = hgrn_forget(hf_f, lb[0])
        log_f_b, k_b = hgrn_forget(hf_b, lb[1])
        o_hg = bidir_gla(to_heads(jax.nn.silu(hq), HG_HEADS) * (HG_DK ** -0.5),
                         to_heads(k_f, HG_HEADS), to_heads(k_b, HG_HEADS),
                         to_heads(hv, HG_HEADS),
                         to_heads(log_f_f, HG_HEADS), to_heads(log_f_b, HG_HEADS))
        y_hg = gated_head_norm(o_hg, hr, hg_onorm[i])

        mixed = jnp.concatenate([y_gla, y_hg], axis=-1).astype(h.dtype) @ w_out[i]
        h = h + mixed

        v = rmsnorm(h, norm_ffn[i])
        j = i // 2
        if i % 2 == 0:
            ffn = swiglu(v, w_dense_gate[j], w_dense_up[j], w_dense_down[j])
        else:
            ffn = moe_swiglu(v, w_router[j], w_exp_gate[j], w_exp_up[j], w_exp_down[j])
        h = h + ffn

        gate = jax.nn.sigmoid(rmsnorm(h, norm_ple[i]) @ w_ple_gate[i])
        h = h + (p[i] @ w_ple_proj[i]) * gate

    return rmsnorm(h, norm_final)


_drawn_inputs = setup_inputs


def setup_inputs(seed=0):
    import zlib

    import numpy as np

    out = dict(_drawn_inputs(seed))
    spreads = {}
    factors = {}
    for name, (base, spread) in spreads.items():
        noise = np.random.default_rng([zlib.crc32(name.encode()), seed]).standard_normal(out[name].shape)
        drawn = base * np.exp(spread * noise) if base else spread * noise
        out[name] = __import__('jax').numpy.asarray(drawn.astype(out[name].dtype))
    for name, factor in factors.items():
        out[name] = (out[name] * factor).astype(out[name].dtype)
    return out
```

```python
from contextlib import ExitStack

import concourse.bass as bass
from concourse import mybir

F32 = mybir.dt.float32
BF16 = mybir.dt.bfloat16
I32 = mybir.dt.int32
U32 = mybir.dt.uint32
ACT = mybir.ActivationFunctionType
ALU = mybir.AluOpType

P = 128
D = 1024
T = 256
NT = T // P
KD = D // P
DEPTH = 2
EPS, HEAD_EPS, F_MIN = 1e-6, 1e-5, 1e-6
LN_F_MIN = -13.815510557964274
CHUNK = 64
RANK = 16
FF_DENSE, FF_EXPERT, NE, PLE = 2816, 3584, 8, 256
CAP = 128
NJMAX = NE + 3
FG = 256
RING = 6
SLOT = 2048
SUB = 8
SUB_SCALE = 2.0 ** -14
LEVELS = (8, 16, 32)

SPLIT = dict(gq=0, gk=256, gv=512, gr=1024, glr=1536, hq=1568, hff=2080, hfb=2592, hv=3104, hr=3616)
PROJ = [("gr", 0, "tok", "a"), ("gr", 1, "tok", "a"), ("hr", 0, "tok", "a"), ("hr", 1, "tok", "a"),
        ("hq", 0, "col", "a"), ("hq", 1, "col", "a"), ("hff", 0, "col", "a"), ("hff", 1, "col", "a"),
        ("hfb", 0, "col", "a"), ("hfb", 1, "col", "a"), ("glr", 0, "low", "v"), ("gq", 0, "col", "v"),
        ("gk", 0, "col", "v"), ("z", 0, "decay", "v"), ("z", 1, "decay", "v"), ("gv", 0, "tok", "v"),
        ("gv", 1, "tok", "v"), ("hv", 0, "tok", "v"), ("hv", 1, "tok", "v")]
PROJ_BANK = {(s[0], s[1]): (4 + n) % 8 for n, s in enumerate(PROJ)}

C_MIX, C_FFN, C_PLE, C_BG, C_LB, C_GON, C_HON, NROW = 0, 16, 32, 48, 56, 72, 74, 76

O_MASK = 0
O_ID = O_MASK + 11 * P
O_IOTA = O_ID + P
O_TRI = O_IOTA + P
O_ONE = O_TRI + P
O_RST = O_ONE + P
NCONST = O_RST + T

HEADS = [[(u, 64 * hh, 64, 2 * u + hh) for hh in range(2)] for u in range(2)] + \
        [[(u, 0, P, 4 + u - 2)] for u in range(2, 6)]
PAIRS = [[(hd, t) for hd in heads for t in range(NT)] for heads in HEADS]
GROUPS_OF = [3 * len(p) for p in PAIRS]
NGROUP = sum(GROUPS_OF)
GROUP0 = [sum(GROUPS_OF[:u]) for u in range(6)]


def shape_constants(np):
    c = np.zeros((P, NCONST), np.float32)
    s, t = np.arange(P)[:, None], np.arange(P)[None, :]
    same = lambda n: (s // n) == (t // n)
    fwd = [same(SUB) * (s <= t) / SUB_SCALE ** 2]
    bwd = [same(SUB) * (s >= t) / SUB_SCALE ** 2]
    for m in LEVELS + (CHUNK,):
        lo, hi = (s % (2 * m)) < m, (t % (2 * m)) >= m
        fwd.append(same(2 * m) * lo * hi)
        bwd.append(same(2 * m) * ((s % (2 * m)) >= m) * ((t % (2 * m)) < m))
    for n, m in enumerate(fwd[:4] + bwd[:4] + [fwd[4], bwd[4], np.ones((P, P))]):
        c[:, O_MASK + n * P:O_MASK + (n + 1) * P] = m
    c[:, O_ID:O_ID + P] = np.eye(P)
    c[:, O_IOTA:O_IOTA + P] = t
    c[:, O_TRI:O_TRI + P] = s < t
    c[:, O_ONE:O_ONE + P] = 1.0
    c[:, O_RST:O_RST + T] = (np.arange(T) % CHUNK != 0)[None, :]
    return c


def product_order():
    order = [("rows", "v")]
    for L in range(DEPTH):
        order += [(("normT", 3 * L, b), "av"[b % 2]) for b in range(4)]
        order += [((part, piece, L), engine) for part, piece, _, engine in PROJ]
        order += [(("yT", L, b), "av"[b % 2]) for b in range(4)]
        order += [(("mix", L, n), "v") for n in range(4)]
        order += [(("normT", 3 * L + 1, b), "av"[b % 2]) for b in range(4)]
        if L == 1:
            order += [("logits", "v"), ("rank", "v")]
        order += [(("pT", L), "v")]
        order += [(("normT", 3 * L + 2, b), "av"[b % 2]) for b in range(4)]
        order += [(("pp", L, n), "v") for n in range(4)]
        order += [(("pg", L, n), "a") for n in range(4)]
    return order


def numbered(order):
    taken, out = {"a": 0, "v": 0}, {}
    for n, (name, engine) in enumerate(order):
        taken[engine] += 1
        out[name] = (n + 1, engine, taken[engine])
    return out


def trunk_kernel(nc, x, p, w_in, gla_wg2, gla_bg, hg_lb_logits, gla_onorm, hg_onorm, w_out, norm_mix,
                 norm_ffn, w_dense_gate, w_dense_up, w_dense_down, w_router, w_exp_gate, w_exp_up,
                 w_exp_down, w_ple_proj, w_ple_gate, norm_ple, norm_final, consts, out):
    ctx = ExitStack()
    with ctx:
        def sb(name, shape, dt=F32):
            return ctx.enter_context(nc.sbuf_tensor(name, shape, dt))

        def sem(name):
            return ctx.enter_context(nc.semaphore(name))

        ring = sb("ring", [P, RING, SLOT])
        h = sb("h", [P, NT, D])
        hn = sb("hn", [P, NT, D])
        xT = sb("xT", [P, KD, T])
        V = sb("V", [P, NT, D])
        SR = sb("SR", [P, NT, D])
        Q = sb("Q", [P, 6, T])
        K = sb("K", [P, 2, 6, T])
        G = sb("G", [P, 2, 6, T])
        B = sb("B", [P, 2, 6, T])
        X = sb("X", [P, 2, 8, 2, T])
        A = sb("A", [P, 4, 512])
        CST = sb("CST", [P, NCONST])
        RV = sb("RV", [NROW, P])
        RC = sb("RC", [P, NROW])
        LB = sb("LB", [P, 4, 8])
        LBX = sb("LBX", [P, 6, 8])
        TOT = sb("TOT", [P, 2, 6, 4])
        EF = sb("EF", [P, 2, 6, 4])
        WGLR = sb("WGLR", [P, DEPTH, KD, 2 * RANK])
        WG2 = sb("WG2", [2 * RANK, DEPTH, 2, T])
        GLT = sb("GLT", [2 * RANK, T])
        PIN = sb("PIN", [P, DEPTH, NT, PLE])
        PT_ = sb("PT_", [P, 2, T])
        NF = sb("NF", [P, D])
        WR = sb("WR", [P, KD, NE])
        STAT = sb("STAT", [P, 3, 7, NT])
        HST = sb("HST", [P, 3, 16])
        ZB = sb("ZB", [1, 512], BF16)
        RT = sb("RT", [P, 24, 16])
        IDX = sb("IDX", [P, NT, 8], U32)
        JC = sb("JC", [P, NJMAX, 4])
        JF = sb("JF", [P, 16])
        JT = sb("JT", [P, 16], I32)
        CUR = sb("CUR", [P, 2, 4])

        psum = [ctx.enter_context(nc.psum_tensor(f"bank{i}", [P, 512], F32)) for i in range(8)]

        Xf = X[:, :, :, :, :].rearrange("p a b c d -> p (a b c d)")
        SG = Xf[:, 0:1024].rearrange("p (b n) -> p b n", b=2)
        HT = Xf[:, 1024:2048].rearrange("p (b n) -> p b n", b=2)
        HS = Xf[:, 2048:2560].rearrange("p (b n) -> p b n", b=2)
        VG = Xf[:, 2560:3584].rearrange("p (k c) -> p k c", k=KD)
        YS = Xf[:, 3584:4608]
        PICK = Xf[:, 4608:4864].rearrange("p (t c) -> p t c", t=NT)
        PICKT = Xf[:, 4864:5120]

        ident = CST[:, O_ID:O_ID + P]
        iota = CST[:, O_IOTA:O_IOTA + P]
        iota8 = CST[:, O_IOTA:O_IOTA + NE]
        tri = CST[:, O_TRI:O_TRI + P]
        ones = CST[:, O_ONE:O_ONE + P]
        one_col = CST[:, O_ONE:O_ONE + 1]
        reset = CST[:, O_RST:O_RST + T]

        x_in = sem("x_in")
        small_in = sem("small_in")
        slot_full = [sem(f"slot_full{i}") for i in range(RING)]
        filled = sem("filled")
        emptied = {"a": sem("emptied_by_scalar"), "v": sem("emptied_by_vector")}
        dve_step = sem("dve_step")
        zeroed = sem("zeroed")
        lb_shifted = sem("lb_shifted")
        lb_exp = sem("lb_exp")
        squares = sem("squares")
        mean_ready = sem("mean_ready")
        root_ready = sem("root_ready")
        hn_ready = sem("hn_ready")
        h_ready = sem("h_ready")
        forget_ready = sem("forget_ready")
        logf_ready = sem("logf_ready")
        softplus_step = sem("softplus_step")
        sums_ready = sem("sums_ready")
        edge_ready = sem("edge_ready")
        diff_ready = sem("diff_ready")
        exp_ready = sem("exp_ready")
        diag_ready = sem("diag_ready")
        decayed_ready = sem("decayed_ready")
        score_full = sem("score_full")
        masked = sem("masked")
        av_done = sem("av_done")
        osq = sem("head_squares")
        omean = sem("head_mean")
        oroot = sem("head_root")
        y_ready = sem("y_ready")
        gu_full = [sem("gate_full"), sem("up_full")]
        silu_ready = sem("silu_ready")
        hidden_ready = sem("hidden_ready")
        down_done = sem("down_done")
        rt_shift = sem("router_shifted")
        rt_exp = sem("router_exp")
        rt_mask = sem("router_mask")
        table_ready = sem("table_ready")
        cur_ready = sem("cur_ready")
        pick_ready = sem("pick_ready")
        gather_full = sem("gather_full")
        gathered_a = sem("gathered_by_scalar")
        gathered_v = sem("gathered_by_vector")
        pickT_full = sem("pickT_full")
        pickT_ready = sem("pickT_ready")
        e_gate = sem("exp_gate_full")
        e_up = sem("exp_up_full")
        e_silu = sem("exp_silu")
        e_hid = sem("exp_hidden")
        e_ht_full = sem("exp_hiddenT_full")
        e_ht = sem("exp_hiddenT")
        e_down = sem("exp_down_done")
        ys_a = sem("exp_y_by_scalar")
        ys_v = sem("exp_y_by_vector")
        scat_full = sem("scatter_full")
        scat_done = sem("scatter_done")
        out_done = sem("out_done")

        number = numbered(product_order())
        ND = FF_DENSE // FG
        NG = FF_EXPERT // FG
        assert ND % 2 == 1 and NG % 2 == 0 and (3 * NG) % RING == 0
        TURNS = 3 * NG // RING
        UNITS = []
        for L in range(DEPTH):
            UNITS += [("in", L, part, piece) for part, piece, form, _ in PROJ if form in ("col", "tok")]
            UNITS += [("out", L, n) for n in range(4)]
            if L == 0:
                UNITS += [("dg", 0), ("du", 0)]
                for f in range(1, ND):
                    UNITS += [("dg", f), ("du", f), ("dd", f - 1)]
                UNITS += [("dd", ND - 1), ("pp", L)] + [("pg", L, n) for n in range(4)]
        U0 = {u: n for n, u in enumerate(UNITS)}
        UE = len(UNITS)
        TAIL = [("pp", 1)] + [("pg", 1, n) for n in range(4)]
        NSMALL = 10 + 4 * DEPTH

        def col_view(w):
            return w.rearrange("(k p) n -> p k n", p=P)

        def slot_cols(s):
            return ring[:, s, :].rearrange("p (k n) -> p k n", k=KD)

        def slot_rows(s):
            return ring[:, s, :].rearrange("p (k n) -> p k n", k=2)

        def part_of(t, offset, dims):
            a = t[:, :, :, :] if len(t.shape) == 4 else (t[:, :, :] if len(t.shape) == 3 else t[:, :, :, :, :])
            return bass.AP(a.tensor, offset, [a.ap[0]] + [[s, n] for s, n in dims])

        block = ctx.enter_context(nc.Block())

        @block.sync
        def _(sp):
            sp.dma_start(h[:, :, :], x[0].rearrange("(t p) d -> p t d", p=P)).then_inc(x_in, 16)
            small = [
                (CST[:, :], consts),
                (RV[C_MIX:C_MIX + 16, :], norm_mix.rearrange("l (k p) -> (l k) p", p=P)),
                (RV[C_FFN:C_FFN + 16, :], norm_ffn.rearrange("l (k p) -> (l k) p", p=P)),
                (RV[C_PLE:C_PLE + 16, :], norm_ple.rearrange("l (k p) -> (l k) p", p=P)),
                (RV[C_BG:C_BG + 8, :], gla_bg.rearrange("l d (u p) -> (l d u) p", p=P)),
                (RV[C_LB:C_LB + 16, :], hg_lb_logits.rearrange("l d (u p) -> (l d u) p", p=P)),
                (RV[C_GON:C_GON + 2, :], gla_onorm),
                (RV[C_HON:C_HON + 2, :], hg_onorm),
                (WR[:, :, :], w_router[0].rearrange("(k p) e -> p k e", p=P)),
                (NF[:, :], norm_final.rearrange("(a d) -> a d", a=1).to_broadcast([P, D])),
            ]
            for L in range(DEPTH):
                small.append((WGLR[:, L, :, :], col_view(w_in[L])[:, :, SPLIT["glr"]:SPLIT["glr"] + 2 * RANK]))
                small.append((PIN[:, L, :, :], p[L, 0].rearrange("(t p) d -> p t d", p=P)))
            for dst, src in small:
                sp.dma_start(dst, src).then_inc(small_in, 16)
            sp.wait_ge(zeroed, 1)
            for L in range(DEPTH):
                for d in range(2):
                    sp.dma_start(WG2[RANK * d:RANK * (d + 1), L, d, :], gla_wg2[L, d]).then_inc(small_in, 16)

            def load(slot, src):
                dst = slot_cols(slot) if src.shape[1] == KD else slot_rows(slot)
                sp.dma_start(dst, src).then_inc(slot_full[slot], 16)

            def source(u):
                if u[0] == "in":
                    c = SPLIT[u[2]] + u[3] * FG
                    return col_view(w_in[u[1]])[:, :, c:c + FG]
                if u[0] == "out":
                    return col_view(w_out[u[1]])[:, :, u[2] * FG:(u[2] + 1) * FG]
                if u[0] in ("dg", "du"):
                    w = w_dense_gate if u[0] == "dg" else w_dense_up
                    return col_view(w[0])[:, :, u[1] * FG:(u[1] + 1) * FG]
                if u[0] == "dd":
                    return w_dense_down[0, u[1] * FG:(u[1] + 1) * FG, :].rearrange("(k p) n -> p k n", p=P)
                if u[0] == "pp":
                    return w_ple_proj[u[1]].rearrange("(k p) n -> p k n", p=P)
                return col_view(w_ple_gate[u[1]])[:, :, u[2] * FG:(u[2] + 1) * FG]

            def wait_used(u):
                if u[0] == "in":
                    sp.wait_ge(filled, number[(u[2], u[3], u[1])][0])
                elif u[0] == "out":
                    sp.wait_ge(filled, number[("mix", u[1], u[2])][0])
                elif u[0] == "dg":
                    sp.wait_ge(gu_full[0], u[1] + 1)
                elif u[0] == "du":
                    sp.wait_ge(gu_full[1], u[1] + 1)
                elif u[0] == "dd":
                    sp.wait_ge(down_done, u[1] + 1)
                elif u[0] == "pp":
                    sp.wait_ge(filled, number[("pp", u[1], 3)][0])
                else:
                    sp.wait_ge(filled, number[("pg", u[1], u[2])][0])

            for n, u in enumerate(UNITS):
                if n >= RING:
                    wait_used(UNITS[n - RING])
                load(n % RING, source(u))

            gate_v = w_exp_gate[0].rearrange("e (k p) f -> p e k f", p=P)
            up_v = w_exp_up[0].rearrange("e (k p) f -> p e k f", p=P)
            down_v = w_exp_down[0].rearrange("e (g k p) n -> p e g k n", p=P, k=2)

            def job_loads(e, j):
                base = NG * j

                def gate(f, at):
                    load(at % RING, gate_v[:, bass.ds(e, 1), :, bass.ds(f * FG, FG)].rearrange("p e k f -> p (e k) f"))

                def up(f, at):
                    load(at % RING, up_v[:, bass.ds(e, 1), :, bass.ds(f * FG, FG)].rearrange("p e k f -> p (e k) f"))

                def down(f, at):
                    load(at % RING, down_v[:, bass.ds(e, 1), bass.ds(f, 1), :, :].rearrange("p e g k n -> p (e g k) n"))

                if isinstance(j, int):
                    before = [lambda n=n: wait_used(UNITS[UE - RING + n]) for n in range(RING)]
                else:
                    before = [lambda: sp.wait_ge(e_up, base - 1), lambda: sp.wait_ge(e_down, base - 2),
                              lambda: sp.wait_ge(e_gate, base), lambda: sp.wait_ge(e_up, base),
                              lambda: sp.wait_ge(e_down, base - 1), lambda: sp.wait_ge(e_down, base)]
                for n, (what, f) in enumerate([(gate, 0), (up, 0), (gate, 1), (up, 1), (down, 0), (gate, 2)]):
                    before[n]()
                    what(f, UE + n)
                sp.wait_ge(e_gate, base + 1)
                up(2, UE)
                sp.wait_ge(e_up, base + 1)
                down(1, UE + 1)
                with sp.Fori(1, NG // 2 - 1) as i:
                    for c in range(2):
                        f = 2 * i + 1 + c
                        sp.wait_ge(e_gate, base + f - 1)
                        gate(f, UE + 2 + 3 * c)
                        sp.wait_ge(e_up, base + f - 1)
                        up(f, UE + 3 + 3 * c)
                        sp.wait_ge(e_down, base + f - 2)
                        down(f - 1, UE + 4 + 3 * c)
                sp.wait_ge(e_gate, base + NG - 2)
                gate(NG - 1, UE + 2)
                sp.wait_ge(e_up, base + NG - 2)
                up(NG - 1, UE + 3)
                sp.wait_ge(e_down, base + NG - 3)
                down(NG - 2, UE + 4)
                sp.wait_ge(e_gate, base + NG - 1)
                down(NG - 1, UE + 5)

            job_loads(0, 0)
            sp.wait_ge(table_ready, 1)
            nj = NE + nc.sync.value_load(JT[0:1, 15:16], min_val=0, max_val=NJMAX - NE)
            with sp.Fori(1, nj) as j:
                job_loads(nc.sync.value_load(JT[0:1, bass.ds(j, 1)], min_val=0, max_val=NE - 1), j)
            used = [(e_up, -1), (e_down, -2), (e_gate, 0), (e_up, 0), (e_down, -1)]
            for n, u in enumerate(TAIL):
                sp.wait_ge(used[n][0], NG * nj + used[n][1])
                load((UE + n) % RING, source(u))
            sp.wait_ge(h_ready, 7)
            sp.dma_start(out[0].rearrange("(t p) d -> p t d", p=P), hn[:, :, :]).then_inc(out_done, 16)
            sp.wait_ge(out_done, 16)

        def data(eng, name):
            _, engine, n = number[name]
            eng.wait_ge(emptied[engine], n)

        @block.tensor
        def _(pe):
            mm = nc.tensor.matmul

            def arrived(n, turns=0):
                pe.wait_ge(slot_full[n % RING], 16 * (n // RING + 1) + 16 * turns)
                return n % RING

            def transposes(bank, src):
                for kk in range(2):
                    for t in range(NT):
                        last = nc.tensor.transpose(bank[:, kk * T + t * P:kk * T + (t + 1) * P], src(kk, t), ident)
                last.then_inc(filled, 1)

            def turn_tokens(name, first_bank, before=None):
                for b in range(4):
                    if before is not None and before[b] is not None:
                        data(pe, before[b])
                    transposes(psum[first_bank + b],
                               lambda kk, t: hn[:, t, (2 * b + kk) * P:(2 * b + kk + 1) * P])
                for b in range(4):
                    data(pe, name + (b,))

            def columns(bank, w):
                for c in range(2):
                    for k in range(KD):
                        last = mm(bank[:, c * T:(c + 1) * T], w[:, k, c * P:(c + 1) * P], xT[:, k, :],
                                  start=(k == 0), stop=(k == KD - 1))
                return last

            def tokens(bank, w, act, kt=KD, cols=slice(0, FG)):
                for t in range(NT):
                    for k in range(kt):
                        last = mm(bank[:, t * FG:(t + 1) * FG], act[:, k, t * P:(t + 1) * P], w[:, k, cols],
                                  start=(k == 0), stop=(k == kt - 1))
                return last

            pe.wait_ge(small_in, 16 * NSMALL)
            nc.tensor.transpose(psum[7][:, 0:NROW], RV[:, :], ident[0:NROW, 0:NROW]).then_inc(filled, 1)

            def project(L):
                pe.wait_ge(hn_ready, 3 * L + 1)
                turn_tokens(("normT", 3 * L), 0, [("pp", 0, b) for b in range(4)] if L else None)
                held = [("pg", 0, b) for b in range(4)] if L else [None, None, None, "rows"]
                held += [("normT", 3 * L, b) for b in range(4)]
                for i, (part, piece, form, _) in enumerate(PROJ):
                    before = held[i] if i < 8 else PROJ[i - 8][:2] + (L,)
                    if before is not None:
                        data(pe, before)
                    bank = psum[PROJ_BANK[part, piece]]
                    if form == "low":
                        for k in range(KD):
                            last = mm(bank[0:2 * RANK, 0:T], WGLR[:, L, k, :], xT[:, k, :],
                                      start=(k == 0), stop=(k == KD - 1))
                    elif form == "decay":
                        data(pe, ("glr", 0, L))
                        for u in range(2):
                            last = mm(bank[:, u * T:(u + 1) * T], WG2[:, L, piece, u * P:(u + 1) * P], GLT[:, :],
                                      start=True, stop=True)
                    else:
                        w = slot_cols(arrived(U0[("in", L, part, piece)]))
                        last = columns(bank, w) if form == "col" else tokens(bank, w, xT)
                    last.then_inc(filled, 1)

            def scan(L):
                data(pe, ("hfb", 1, L))
                data(pe, ("hv", 1, L))
                waiting = []

                def scores(g, ins):
                    n = L * NGROUP + g
                    if n >= 4:
                        pe.wait_ge(masked, n - 3)
                    for c, (k_ap, q_ap) in enumerate(ins):
                        last = mm(psum[4 + n % 4][:, c * P:(c + 1) * P], k_ap, q_ap, start=True, stop=True)
                    last.then_inc(score_full, 1)

                def weighted(g, sources, head, t, first, final):
                    n = L * NGROUP + g
                    pe.wait_ge(masked, n + 1)
                    o = psum[t + 2 * (head // 4)][:, (head % 4) * P:(head % 4 + 1) * P]
                    for c, s in enumerate(sources):
                        last = mm(o, A[:, n % 4, c * P:(c + 1) * P], V[:, s, head * P:(head + 1) * P],
                                  start=(first and c == 0), stop=(final and c == len(sources) - 1),
                                  skip_group_check=True)
                    last.then_inc(av_done, 1)

                g = 0
                for u in range(6):
                    b, n = (L * 6 + u) % 2, L * 6 + u
                    pe.wait_ge(diag_ready, 2 * n + 2)
                    pe.wait_ge(decayed_ready, 10 * n + 10)
                    for (_, p0, kd, head), t in PAIRS[u]:
                        rows, cols = slice(p0, p0 + kd), slice(t * P, (t + 1) * P)
                        groups = [[(X[rows, b, 1, d, cols], X[rows, b, 0, d, cols])] +
                                  [(X[rows, b, 2 + m, d, cols],) * 2 for m in range(3)] for d in range(2)]
                        cross = 1 - t
                        groups.append([(X[rows, b, 6, d, cols], X[rows, b, 5, d, cols]) for d in range(2)] +
                                      [(X[rows, b, 7, cross, 0:P], X[rows, b, 7, cross, P:2 * P])])
                        for i, ins in enumerate(groups):
                            scores(g, ins)
                            waiting.append((g, [t] * 4 if i < 2 else [t, t, 1 - t], head, t, i == 0, i == 2))
                            g += 1
                            if len(waiting) > 2:
                                weighted(*waiting.pop(0))
                for w in waiting:
                    weighted(*w)

            def mix_out(L):
                pe.wait_ge(y_ready, L + 1)
                turn_tokens(("yT", L), 4)
                for n in range(4):
                    w = slot_cols(arrived(U0[("out", L, n)]))
                    tokens(psum[n], w, xT).then_inc(filled, 1)

            def dense():
                for n in range(4):
                    data(pe, ("mix", 0, n))
                for b in range(4):
                    mm(psum[b][:, :], ZB[0:1, 0:P], ZB[0:1, :], start=True, stop=False, skip_group_check=True)
                first = U0[("dg", 0)]

                def gate_up(half, n, turns, free):
                    for c in range(2):
                        if free is not None:
                            pe.wait_ge((silu_ready, hidden_ready)[c], free)
                        columns(psum[4 + c + 2 * half], slot_cols(arrived(n + c, turns))).then_inc(gu_full[c], 1)

                def down(half, n, turns, ready, final=False):
                    pe.wait_ge(hidden_ready, ready)
                    w = slot_rows(arrived(n, turns))
                    for k in range(2):
                        for t in range(NT):
                            for c in range(2):
                                last = mm(psum[2 * t + c][:, :], HT[:, half, k * T + t * P:k * T + (t + 1) * P],
                                          w[:, k, c * 512:(c + 1) * 512], start=False, stop=final and k == 1,
                                          skip_group_check=True)
                    last.then_inc(down_done, 1)

                gate_up(0, first, 0, None)
                gate_up(1, first + 2, 0, None)
                down(0, first + 4, 0, 1)
                gate_up(0, first + 5, 0, 1)
                down(1, first + 7, 0, 2)
                with pe.Fori(1, ND // 2) as i:
                    gate_up(1, first + 2, i, 2 * i)
                    down(0, first + 4, i, 2 * i + 1)
                    gate_up(0, first + 5, i, 2 * i + 1)
                    down(1, first + 7, i, 2 * i + 2)
                down(0, first + 3 * ND - 1, 0, ND, final=True)

            def route():
                data(pe, ("normT", 4, 0))
                bank = psum[4]
                for t in range(NT):
                    for k in range(KD):
                        last = mm(bank[:, t * NE:(t + 1) * NE], xT[:, k, t * P:(t + 1) * P], WR[:, k, :],
                                  start=(k == 0), stop=(k == KD - 1))
                last.then_inc(filled, 1)
                data(pe, ("normT", 4, 1))
                bank = psum[5]
                pe.wait_ge(rt_mask, 1)
                m = RT[:, 8, :]
                mm(bank[:, 0:8], tri, m[:, 0:8], start=True, stop=True)
                mm(bank[:, 8:16], ones, m[:, 0:8], start=True, stop=False)
                mm(bank[:, 8:16], tri, m[:, 8:16], start=False, stop=True)
                mm(bank[:, 16:24], ones, m[:, 0:8], start=True, stop=False)
                mm(bank[:, 16:24], ones, m[:, 8:16], start=False, stop=True).then_inc(filled, 1)

            def job(j):
                base = NG * j
                pe.wait_ge(pick_ready, 2 * j + 2)
                pe.wait_ge(scat_done, 4 * j + 1)
                for k in range(KD):
                    for t in range(NT):
                        last = mm(psum[4 + k // 4][:, (k % 4) * P:(k % 4 + 1) * P], hn[:, t, k * P:(k + 1) * P],
                                  PICK[:, t, :], start=(t == 0), stop=(t == NT - 1))
                    if k % 4 == 3:
                        last.then_inc(gather_full, 1)
                for t in range(NT):
                    last = nc.tensor.transpose(psum[2][:, t * P:(t + 1) * P], PICK[:, t, :], ident)
                last.then_inc(pickT_full, 1)
                pe.wait_ge(gathered_a, j + 1)
                pe.wait_ge(gathered_v, j + 1)

                def half_of(f, half, which, n, turns, wait):
                    if wait:
                        pe.wait_ge((e_silu, e_hid)[which], base + f - 1)
                    w = slot_cols(arrived(n, turns))
                    for k in range(KD):
                        last = mm(psum[4 + 2 * half + which][:, 0:FG], VG[:, k, :], w[:, k, :],
                                  start=(k == 0), stop=(k == KD - 1))
                    last.then_inc((e_gate, e_up)[which], 1)

                def turn(f, half, wait):
                    pe.wait_ge(e_hid, base + f + 1)
                    if wait:
                        pe.wait_ge(e_ht, base + f - 1)
                    for k in range(2):
                        last = nc.tensor.transpose(psum[2 + half][:, k * P:(k + 1) * P],
                                                   HS[:, half, k * P:(k + 1) * P], ident)
                    last.then_inc(e_ht_full, 1)

                def down(f, half, n, turns, first=False, final=False):
                    pe.wait_ge(e_ht, base + f + 1)
                    w = slot_rows(arrived(n, turns))
                    for k in range(2):
                        for c in range(2):
                            last = mm(psum[c][:, :], HT[:, half, k * P:(k + 1) * P], w[:, k, c * 512:(c + 1) * 512],
                                      start=(first and k == 0), stop=(final and k == 1), skip_group_check=True)
                    last.then_inc(e_down, 1)

                def step(f, half, n, turns, wait, **flags):
                    half_of(f, half, 0, n, turns, wait)
                    turn(f - 1, 1 - half, flags.get("turn_wait", True))
                    half_of(f, half, 1, n + 1, turns, wait)
                    down(f - 1, 1 - half, n + 2, turns, flags.get("first", False))

                jt = TURNS * j
                half_of(0, 0, 0, UE, jt, False)
                half_of(0, 0, 1, UE + 1, jt, False)
                pe.wait_ge(pickT_ready, j + 1)
                step(1, 1, UE + 2, jt, False, turn_wait=False, first=True)
                step(2, 0, UE + 5, jt, True, turn_wait=False)
                with pe.Fori(1, NG // 2 - 1) as i:
                    step(2 * i + 1, 1, UE + 2, jt + i, True)
                    step(2 * i + 2, 0, UE + 5, jt + i, True)
                last_turn = jt + NG // 2 - 1
                half_of(NG - 1, 1, 0, UE + 2, last_turn, True)
                turn(NG - 2, 0, True)
                half_of(NG - 1, 1, 1, UE + 3, last_turn, True)
                down(NG - 2, 0, UE + 4, last_turn)
                turn(NG - 1, 1, True)
                down(NG - 1, 1, UE + 5, last_turn, final=True)
                pe.wait_ge(ys_a, j + 1)
                pe.wait_ge(ys_v, j + 1)
                for t in range(NT):
                    for c in range(2):
                        mm(psum[4 + 2 * t + c][:, :], PICKT[:, t * P:(t + 1) * P], YS[:, c * 512:(c + 1) * 512],
                           start=True, stop=True).then_inc(scat_full, 1)

            def ple(L, base, turns):
                pe.wait_ge(hn_ready, 3 * L + 3)
                transposes(psum[7], lambda kk, t: PIN[:, L, t, kk * P:(kk + 1) * P])
                turn_tokens(("normT", 3 * L + 2), 3)
                data(pe, ("pT", L))
                w = slot_rows(arrived(base, turns))
                for n in range(4):
                    tokens(psum[n], w, PT_, 2, slice(n * FG, (n + 1) * FG)).then_inc(filled, 1)
                for n in range(4):
                    w = slot_cols(arrived(base + 1 + n, turns))
                    tokens(psum[4 + n], w, xT).then_inc(filled, 1)

            for L in range(DEPTH):
                project(L)
                scan(L)
                mix_out(L)
                pe.wait_ge(hn_ready, 3 * L + 2)
                turn_tokens(("normT", 3 * L + 1), 4, [("yT", L, b) for b in range(4)])
                if L == 0:
                    dense()
                    ple(0, U0[("pp", 0)], 0)
                else:
                    route()
                    pe.wait_ge(table_ready, 1)
                    nj = NE + nc.tensor.value_load(JT[0:1, 15:16], min_val=0, max_val=NJMAX - NE)
                    with pe.Fori(0, nj) as j:
                        job(j)
                    ple(1, UE, TURNS * nj)

        def level(b, i, m, keys, what=None, u=0):
            off = 0 if keys else m
            turn = m if keys else -m
            if what is None:
                return part_of(X, (b * 8 + 2 + i) * 2 * T + off, [[T + turn, 2], [2 * m, T // (2 * m)], [1, m]])
            if what is K:
                return part_of(K, u * T + off, [[6 * T + turn, 2], [2 * m, T // (2 * m)], [1, m]])
            return part_of(Q, u * T + off, [[turn, 2], [2 * m, T // (2 * m)], [1, m]])

        @block.scalar
        def _(act):
            fn = nc.scalar.activation

            def take(name, bank):
                act.wait_ge(filled, number[name][0])
                return psum[bank]

            def scaled(dst, bank, cols):
                for c, col in enumerate(cols):
                    last = fn(dst(c), bank[:, c * T:(c + 1) * T], ACT.Copy, scale=RC[:, col:col + 1])
                last.then_inc(emptied["a"], 1)

            act.wait_ge(lb_shifted, 1)
            fn(LBX[:, 3:5, :], LBX[:, 1:3, :], ACT.Exp).then_inc(lb_exp, 1)

            def norm(r, col, first_bank=None):
                if r == 0:
                    act.wait_ge(x_in, 16)
                else:
                    act.wait_ge(h_ready, r)
                for t in range(NT):
                    fn(hn[:, t, :], h[:, t, :], ACT.Square, accum_out=STAT[:, 0, r, t:t + 1]).then_inc(squares, 1)
                act.wait_ge(mean_ready, r + 1)
                fn(STAT[:, 2, r, :], STAT[:, 1, r, :], ACT.Sqrt).then_inc(root_ready, 1)
                if col is not None:
                    data(act, "rows")
                    for b in (0, 2):
                        scaled(lambda c: xT[:, 2 * b + c, :], take(("normT", r, b), first_bank + b), [col + 2 * b, col + 2 * b + 1])

            def mixer(L):
                for part, piece, form, reader in PROJ:
                    if reader != "a":
                        continue
                    bank = take((part, piece, L), PROJ_BANK[part, piece])
                    two = bank[:, :].rearrange("p (a n) -> p a n", a=2)
                    if form == "tok":
                        c = piece * FG + (512 if part == "hr" else 0)
                        fn(SR[:, :, c:c + FG], two, ACT.Silu).then_inc(emptied["a"], 1)
                    elif part == "hq":
                        fn(Q[:, 2 + 2 * piece:4 + 2 * piece, :], two, ACT.Silu).then_inc(emptied["a"], 1)
                    else:
                        d, u = (0 if part == "hff" else 1), 2 + 2 * piece
                        fn(G[:, d, u:u + 2, :], two, ACT.Sigmoid)
                        fn(K[:, d, u:u + 2, :], two, ACT.Sigmoid, scale=-1.0).then_inc(emptied["a"], 1)
                act.wait_ge(forget_ready, L + 1)
                fn(G[:, :, 2:6, :], G[:, :, 2:6, :], ACT.Ln).then_inc(logf_ready, 1)
                data(act, ("z", 1, L))
                sp_ = A[:, 0:2, :].rearrange("p d (u t) -> p d u t", u=2)
                fn(sp_, G[:, :, 0:2, :], ACT.Abs).then_inc(softplus_step, 1)
                act.wait_ge(softplus_step, 3 * L + 1)
                fn(sp_, sp_, ACT.Exp, scale=-1.0).then_inc(softplus_step, 1)
                act.wait_ge(softplus_step, 3 * L + 2)
                fn(sp_, sp_, ACT.Ln, bias=1.0).then_inc(softplus_step, 1)
                act.wait_ge(sums_ready, L + 1)
                for d, place, c in ((0, 0, 1), (0, 3, 2), (1, 1, 2), (1, 2, 1)):
                    fn(EF[:, d, :, place], TOT[:, d, :, c], ACT.Exp).then_inc(edge_ready, 1)
                for u in range(6):
                    n, b = L * 6 + u, (L * 6 + u) % 2
                    act.wait_ge(diff_ready, 5 * n + 1)
                    fn(X[:, b, 1, :, :], X[:, b, 0, :, :], ACT.Exp, scale=-1.0).then_inc(exp_ready, 1)
                    fn(X[:, b, 0, :, :], X[:, b, 0, :, :], ACT.Exp).then_inc(exp_ready, 1)
                    for i, m in enumerate(LEVELS):
                        act.wait_ge(diff_ready, 5 * n + 2 + i)
                        for keys in (True, False):
                            v = level(b, i, m, keys)
                            fn(v, v, ACT.Exp, scale=-1.0 if keys else 1.0).then_inc(exp_ready, 1)
                    fn(X[:, b, 5, :, :], B[:, :, u, :], ACT.Exp).then_inc(exp_ready, 1)
                    act.wait_ge(diff_ready, 5 * n + 5)
                    fn(X[:, b, 6, :, :], X[:, b, 6, :, :], ACT.Exp).then_inc(exp_ready, 1)
                act.wait_ge(av_done, (L + 1) * NGROUP)
                for g in range(2):
                    for t in range(NT):
                        for hd in range(4):
                            n = 8 * g + 4 * t + hd
                            fn(A[:, 2 * g + t, hd * P:(hd + 1) * P], psum[2 * g + t][:, hd * P:(hd + 1) * P], ACT.Square,
                               accum_out=HST[:, 0, n:n + 1]).then_inc(osq, 1)
                act.wait_ge(omean, L + 1)
                fn(HST[:, 2, :], HST[:, 1, :], ACT.Sqrt).then_inc(oroot, 1)
                for b in (0, 2):
                    col = C_GON + L if b < 2 else C_HON + L
                    scaled(lambda c: xT[:, 2 * b + c, :], take(("yT", L, b), 4 + b), [col, col])

            def dense():
                def silu(half, n):
                    act.wait_ge(gu_full[0], n)
                    fn(SG[:, half, :], psum[4 + 2 * half][:, :], ACT.Silu).then_inc(silu_ready, 1)
                silu(0, 1)
                silu(1, 2)
                with act.Fori(1, ND // 2) as i:
                    act.wait_ge(hidden_ready, 2 * i - 1)
                    silu(0, 2 * i + 1)
                    act.wait_ge(hidden_ready, 2 * i)
                    silu(1, 2 * i + 2)
                act.wait_ge(hidden_ready, ND - 2)
                silu(0, ND)

            def job(j):
                base = NG * j
                act.wait_ge(gather_full, 2 * j + 1)
                for k in range(4):
                    last = fn(VG[:, k, :], psum[4][:, k * P:(k + 1) * P], ACT.Copy,
                              scale=RC[:, C_FFN + KD + k:C_FFN + KD + k + 1])
                last.then_inc(gathered_a, 1)
                act.wait_ge(pickT_full, j + 1)
                fn(PICKT, psum[2][:, 0:T], ACT.Copy).then_inc(pickT_ready, 1)

                def silu(f, half, wait):
                    act.wait_ge(e_gate, base + f + 1)
                    if wait:
                        act.wait_ge(e_hid, base + f - 1)
                    fn(SG[:, half, 0:FG], psum[4 + 2 * half][:, 0:FG], ACT.Silu).then_inc(e_silu, 1)

                def turned(f, half, wait):
                    act.wait_ge(e_ht_full, base + f + 1)
                    if wait:
                        act.wait_ge(e_down, base + f - 1)
                    fn(HT[:, half, 0:FG], psum[2 + half][:, 0:FG], ACT.Copy).then_inc(e_ht, 1)

                silu(0, 0, False)
                silu(1, 1, False)
                turned(0, 0, False)
                silu(2, 0, True)
                turned(1, 1, False)
                with act.Fori(1, NG // 2 - 1) as i:
                    silu(2 * i + 1, 1, True)
                    turned(2 * i, 0, True)
                    silu(2 * i + 2, 0, True)
                    turned(2 * i + 1, 1, True)
                silu(NG - 1, 1, True)
                turned(NG - 2, 0, True)
                turned(NG - 1, 1, True)
                act.wait_ge(e_down, base + NG)
                fn(YS[:, 0:512], psum[0][:, :], ACT.Copy).then_inc(ys_a, 1)

            def ple(L):
                for n in range(4):
                    bank = take(("pg", L, n), 4 + n)
                    if n >= 2:
                        data(act, ("pp", L, n - 2))
                    fn(SG[:, n % 2, :], bank[:, :], ACT.Sigmoid).then_inc(emptied["a"], 1)

            for L in range(DEPTH):
                norm(3 * L, C_MIX + KD * L, 0)
                mixer(L)
                norm(3 * L + 1, C_FFN + KD * L, 4)
                if L == 0:
                    dense()
                else:
                    for t in range(NT):
                        act.wait_ge(rt_shift, t + 1)
                        fn(RT[:, 2, t * 8:(t + 1) * 8], RT[:, 1, t * 8:(t + 1) * 8], ACT.Exp,
                           accum_out=RT[:, 3, t:t + 1]).then_inc(rt_exp, 1)
                    act.wait_ge(table_ready, 1)
                    nj = NE + nc.scalar.value_load(JT[0:1, 15:16], min_val=0, max_val=NJMAX - NE)
                    with act.Fori(0, nj) as j:
                        job(j)
                norm(3 * L + 2, C_PLE + KD * L, 3)
                ple(L)
            norm(6, None)

        @block.gpsimd
        def _(pool):
            for L in range(DEPTH):
                for u in range(6):
                    n, b = L * 6 + u, (L * 6 + u) % 2

                    def times(dst, src, other, ready):
                        pool.wait_ge(exp_ready, 10 * n + ready)
                        nc.gpsimd.tensor_tensor(dst, src, other, ALU.mult).then_inc(decayed_ready, 1)

                    for i, m in enumerate(LEVELS):
                        v = level(b, i, m, True)
                        times(v, v, level(b, i, m, True, K, u), 3 + 2 * i)
                        v = level(b, i, m, False)
                        times(v, v, level(b, i, m, False, Q, u), 4 + 2 * i)
                    times(X[:, b, 5, :, :], X[:, b, 5, :, :], part_of(Q, u * T, [[0, 2], [1, T]]), 9)
                    times(X[:, b, 6, :, :], X[:, b, 6, :, :], K[:, :, u, :], 10)
                    pool.wait_ge(edge_ready, 4 * L + 4)
                    pool.wait_ge(decayed_ready, 10 * n + 8)
                    o5, o6, o7 = ((b * 8 + a) * 2 * T for a in (5, 6, 7))
                    ef = u * 4
                    times(part_of(X, o7, [[T, 2], [CHUNK, 2], [1, CHUNK]]),
                          part_of(X, o6, [[T + P, 2], [CHUNK, 2], [1, CHUNK]]),
                          part_of(EF, ef, [[24, 2], [1, 2], [0, CHUNK]]), 10)
                    times(part_of(X, o7 + P, [[T, 2], [CHUNK, 2], [1, CHUNK]]),
                          part_of(X, o5 + P, [[T - P, 2], [CHUNK, 2], [1, CHUNK]]),
                          part_of(EF, ef + 2, [[24, 2], [1, 2], [0, CHUNK]]), 10)

        @block.vector
        def _(dve):
            tt, ts, stt = nc.vector.tensor_tensor, nc.vector.tensor_scalar, nc.vector.scalar_tensor_tensor
            steps = [0]

            def link(ins):
                steps[0] += 1
                ins.then_inc(dve_step, 1)
                dve.wait_ge(dve_step, steps[0])

            def take(name, bank):
                dve.wait_ge(filled, number[name][0])
                return psum[bank]

            nc.vector.memset(WG2[:, :, :, :], 0.0).then_inc(zeroed, 1)
            nc.vector.memset(ZB[:, :], 0.0)
            nc.vector.memset(JF[:, :], 0.0)
            link(nc.vector.memset(EF[:, :, :, :], 1.0))
            nc.vector.tensor_copy(RC[:, :], take("rows", 7)[:, 0:NROW]).then_inc(emptied["v"], 1)
            data(dve, "rows")
            l0, l1 = RC[:, C_LB:C_LB + 8], RC[:, C_LB + 8:C_LB + 16]
            link(tt(LBX[:, 0, :], l0, l1, ALU.max))
            tt(LBX[:, 1, :], l0, LBX[:, 0, :], ALU.subtract)
            tt(LBX[:, 2, :], l1, LBX[:, 0, :], ALU.subtract).then_inc(lb_shifted, 1)
            dve.wait_ge(lb_exp, 1)
            link(tt(LBX[:, 5, :], LBX[:, 3, :], LBX[:, 4, :], ALU.add))
            link(nc.vector.reciprocal(LBX[:, 0, :], LBX[:, 5, :]))
            tt(LBX[:, 1, :], LBX[:, 3, :], LBX[:, 0, :], ALU.mult)
            link(tt(LBX[:, 2, :], LBX[:, 4, :], LBX[:, 0, :], ALU.mult))
            tt(LB[:, 0, :], LBX[:, 1, :], LBX[:, 1, :], ALU.subtract)
            link(tt(LBX[:, 5, :], LBX[:, 1, :], LBX[:, 2, :], ALU.add))
            link(tt(LB[:, 1, :], LBX[:, 5, :], LBX[:, 1, :], ALU.subtract))
            link(ts(LB[:, 2:4, :], LB[:, 0:2, :], -1.0, 1.0, ALU.mult, ALU.add))

            def scaled(dst, bank, cols):
                for c, col in enumerate(cols):
                    last = ts(dst(c), bank[:, c * T:(c + 1) * T], RC[:, col:col + 1], None, ALU.mult)
                last.then_inc(emptied["v"], 1)

            def norm(r, col):
                dve.wait_ge(squares, 2 * r + 2)
                ts(STAT[:, 1, r, :], STAT[:, 0, r, :], 1.0 / D, EPS, ALU.mult, ALU.add).then_inc(mean_ready, 1)
                dve.wait_ge(root_ready, r + 1)
                link(nc.vector.reciprocal(STAT[:, 0, r, :], STAT[:, 2, r, :]))
                for t in range(NT):
                    last = ts(hn[:, t, :], h[:, t, :], STAT[:, 0, r, t:t + 1], None, ALU.mult)
                if col is None:
                    link(last)
                    tt(hn[:, :, :], hn[:, :, :], NF[:, :].unsqueeze(1).to_broadcast([P, NT, D]),
                       ALU.mult).then_inc(h_ready, 1)
                    return
                last.then_inc(hn_ready, 1)

            def norm_turned(r, col, first_bank):
                for b in (1, 3):
                    scaled(lambda c: xT[:, 2 * b + c, :], take(("normT", r, b), first_bank + b), [col + 2 * b, col + 2 * b + 1])

            def mixer(L):
                data(dve, ("hq", 1, L))
                ts(Q[:, 2:6, :], Q[:, 2:6, :], float(P) ** -0.5, None, ALU.mult)
                data(dve, ("hfb", 1, L))
                for d in range(2):
                    for u in range(4):
                        c = 4 * d + u
                        ts(K[:, d, 2 + u, :], K[:, d, 2 + u, :], LB[:, 2 + L, c:c + 1], None, ALU.mult)
                        last = ts(G[:, d, 2 + u, :], G[:, d, 2 + u, :], LB[:, 2 + L, c:c + 1], LB[:, L, c:c + 1],
                                  ALU.mult, ALU.add)
                link(last)
                ts(G[:, :, 2:6, :], G[:, :, 2:6, :], F_MIN, None, ALU.max).then_inc(forget_ready, 1)
                nc.vector.tensor_copy(GLT[:, :], take(("glr", 0, L), PROJ_BANK["glr", 0])[0:2 * RANK, 0:T]).then_inc(emptied["v"], 1)
                two = take(("gq", 0, L), PROJ_BANK["gq", 0])[:, :].rearrange("p (a n) -> p a n", a=2)
                ts(Q[:, 0:2, :], two, float(P // 2) ** -0.5, None, ALU.mult).then_inc(emptied["v"], 1)
                two = take(("gk", 0, L), PROJ_BANK["gk", 0])[:, :].rearrange("p (a n) -> p a n", a=2)
                nc.vector.tensor_copy(K[:, 0, 0:2, :], two)
                nc.vector.tensor_copy(K[:, 1, 0:2, :], two).then_inc(emptied["v"], 1)
                for d in range(2):
                    bank = take(("z", d, L), PROJ_BANK["z", d])
                    for u in range(2):
                        c = C_BG + 4 * L + 2 * d + u
                        last = ts(G[:, d, u, :], bank[:, u * T:(u + 1) * T], RC[:, c:c + 1], None, ALU.add)
                    last.then_inc(emptied["v"], 1)
                for part, c0 in (("gv", 0), ("hv", 512)):
                    for piece in range(2):
                        two = take((part, piece, L), PROJ_BANK[part, piece])[:, :].rearrange("p (a n) -> p a n", a=2)
                        c = c0 + piece * FG
                        nc.vector.tensor_copy(V[:, :, c:c + FG], two).then_inc(emptied["v"], 1)
                dve.wait_ge(softplus_step, 3 * L + 3)
                data(dve, ("z", 1, L))
                g2 = G[:, :, 0:2, :].rearrange("p d u t -> p d (u t)")
                link(stt(g2, g2, 0.0, A[:, 0:2, :], ALU.min, ALU.subtract))
                link(ts(g2, g2, 1.0 / 16.0, LN_F_MIN, ALU.mult, ALU.max))
                dve.wait_ge(logf_ready, L + 1)
                for d in range(2):
                    for u in range(6):
                        last = nc.vector.tensor_tensor_scan(B[:, d, u, :], reset, G[:, d, u, :], 0.0,
                                                            ALU.mult, ALU.add)
                link(last)
                link(nc.vector.tensor_copy(TOT[:, :, :, :], B[:, :, :, CHUNK - 1:T:CHUNK]))
                back = B[:, 1, :, :]
                link(tt(back, G[:, 1, :, :], back, ALU.subtract))
                chunks = part_of(B, 6 * T, [[T, 6], [CHUNK, 4], [1, CHUNK]])
                tt(chunks, chunks, part_of(TOT, 24, [[4, 6], [1, 4], [0, CHUNK]]), ALU.add).then_inc(sums_ready, 1)
                dve.wait_ge(sums_ready, L + 1)

                def differences(u):
                    n, b = L * 6 + u, (L * 6 + u) % 2
                    if n >= 2:
                        dve.wait_ge(score_full, ((n - 1) // 6) * NGROUP + GROUP0[(n - 1) % 6])
                    x0 = b * 8 * 2 * T
                    tt(part_of(X, x0, [[T, 2], [SUB, T // SUB], [1, SUB]]),
                       part_of(B, u * T, [[6 * T, 2], [SUB, T // SUB], [1, SUB]]),
                       part_of(B, u * T + SUB // 2 - 1, [[6 * T, 2], [SUB, T // SUB], [0, SUB]]),
                       ALU.subtract).then_inc(diff_ready, 1)
                    for i, m in enumerate(LEVELS):
                        w = 2 * m
                        tt(part_of(X, x0 + (2 + i) * 2 * T, [[T, 2], [w, T // w], [1, w]]),
                           part_of(B, u * T, [[6 * T, 2], [w, T // w], [1, w]]),
                           part_of(B, u * T + m - 1, [[6 * T + 1, 2], [w, T // w], [0, w]]),
                           ALU.subtract).then_inc(diff_ready, 1)
                    tt(part_of(X, x0 + 6 * 2 * T, [[T, 2], [CHUNK, 4], [1, CHUNK]]),
                       part_of(TOT, u * 4, [[24, 2], [1, 4], [0, CHUNK]]),
                       part_of(B, u * T, [[6 * T, 2], [CHUNK, 4], [1, CHUNK]]),
                       ALU.subtract).then_inc(diff_ready, 1)

                def diagonal(u):
                    n, b = L * 6 + u, (L * 6 + u) % 2
                    dve.wait_ge(exp_ready, 10 * n + 2)
                    stt(X[:, b, 0, :, :], X[:, b, 0, :, :], SUB_SCALE, part_of(Q, u * T, [[0, 2], [1, T]]),
                        ALU.mult, ALU.mult).then_inc(diag_ready, 1)
                    stt(X[:, b, 1, :, :], X[:, b, 1, :, :], SUB_SCALE, K[:, :, u, :],
                        ALU.mult, ALU.mult).then_inc(diag_ready, 1)

                def mask(g):
                    n = L * NGROUP + g
                    w = 384 if g % 3 == 2 else 512
                    dve.wait_ge(score_full, n + 1)
                    if n >= 4:
                        dve.wait_ge(av_done, n - 3)
                    tt(A[:, n % 4, 0:w], psum[4 + n % 4][:, 0:w], CST[:, O_MASK + (g % 3) * 512:][:, 0:w],
                       ALU.mult).then_inc(masked, 1)

                differences(0)
                diagonal(0)
                for u in range(6):
                    if u < 5:
                        differences(u + 1)
                    for g in range(GROUPS_OF[u]):
                        mask(GROUP0[u] + g)
                        if g == 1 and u < 5:
                            diagonal(u + 1)
                dve.wait_ge(osq, 16 * L + 16)
                ts(HST[:, 1, :], HST[:, 0, :], 1.0 / P, HEAD_EPS, ALU.mult, ALU.add).then_inc(omean, 1)
                dve.wait_ge(oroot, L + 1)
                link(nc.vector.reciprocal(HST[:, 0, :], HST[:, 2, :]))
                for g in range(2):
                    for t in range(NT):
                        for hd in range(4):
                            n, c = 8 * g + 4 * t + hd, 512 * g + hd * P
                            last = stt(hn[:, t, c:c + P], psum[2 * g + t][:, hd * P:(hd + 1) * P],
                                       HST[:, 0, n:n + 1], SR[:, t, c:c + P], ALU.mult, ALU.mult)
                last.then_inc(y_ready, 1)
                for b in (1, 3):
                    col = C_GON + L if b < 2 else C_HON + L
                    scaled(lambda c: xT[:, 2 * b + c, :], take(("yT", L, b), 4 + b), [col, col])
                for n in range(4):
                    two = take(("mix", L, n), n)[:, :].rearrange("p (a n) -> p a n", a=2)
                    hv = h[:, :, n * FG:(n + 1) * FG]
                    tt(hv, two, hv, ALU.add).then_inc(emptied["v"], 1)
                data(dve, ("mix", L, 3))
                nc.vector.memset(LBX[:, 0, 0:1], 0.0).then_inc(h_ready, 1)

            def dense():
                def hidden(half, n):
                    dve.wait_ge(silu_ready, n)
                    dve.wait_ge(gu_full[1], n)
                    tt(HT[:, half, :], psum[5 + 2 * half][:, :], SG[:, half, :], ALU.mult).then_inc(hidden_ready, 1)
                hidden(0, 1)
                hidden(1, 2)
                with dve.Fori(1, ND // 2) as i:
                    dve.wait_ge(down_done, 2 * i - 1)
                    hidden(0, 2 * i + 1)
                    dve.wait_ge(down_done, 2 * i)
                    hidden(1, 2 * i + 2)
                dve.wait_ge(down_done, ND - 2)
                hidden(0, ND)
                dve.wait_ge(down_done, ND)
                for t in range(NT):
                    for c in range(2):
                        hv = h[:, t, c * 512:(c + 1) * 512]
                        last = tt(hv, psum[2 * t + c][:, :], hv, ALU.add)
                last.then_inc(h_ready, 1)

            def route():
                lg, sh, pr = RT[:, 0, :], RT[:, 1, :], RT[:, 4, :]
                nc.vector.tensor_copy(lg, take("logits", 4)[:, 0:16]).then_inc(emptied["v"], 1)
                data(dve, "logits")
                for t in range(NT):
                    w = slice(8 * t, 8 * t + 8)
                    link(nc.vector.max(RT[:, 5, w], lg[:, w]))
                    ts(sh[:, w], lg[:, w], RT[:, 5, 8 * t:8 * t + 1], None, ALU.subtract).then_inc(rt_shift, 1)
                dve.wait_ge(rt_exp, 2)
                link(nc.vector.reciprocal(RT[:, 3, 2:4], RT[:, 3, 0:2]))
                for t in range(NT):
                    w = slice(8 * t, 8 * t + 8)
                    link(ts(pr[:, w], RT[:, 2, w], RT[:, 3, 2 + t:3 + t], None, ALU.mult))
                    link(nc.vector.max(RT[:, 6, w], pr[:, w]))
                    link(nc.vector.max_index(IDX[:, t, :], RT[:, 6, w], pr[:, w]))
                    link(nc.vector.tensor_copy(RT[:, 7, w], IDX[:, t, :]))
                    ts(RT[:, 9, w], iota8, RT[:, 7, 8 * t:8 * t + 1], None, ALU.is_equal)
                    link(ts(RT[:, 10, w], iota8, RT[:, 7, 8 * t + 1:8 * t + 2], None, ALU.is_equal))
                    link(tt(RT[:, 3, 4 + t:5 + t], RT[:, 6, 8 * t:8 * t + 1], RT[:, 6, 8 * t + 1:8 * t + 2], ALU.add))
                    link(nc.vector.reciprocal(RT[:, 3, 6 + t:7 + t], RT[:, 3, 4 + t:5 + t]))
                    link(ts(RT[:, 11, w], RT[:, 6, w], RT[:, 3, 6 + t:7 + t], None, ALU.mult))
                    link(ts(RT[:, 12, w], RT[:, 9, w], RT[:, 11, 8 * t:8 * t + 1], None, ALU.mult))
                    link(stt(RT[:, 13, w], RT[:, 10, w], RT[:, 11, 8 * t + 1:8 * t + 2], RT[:, 12, w],
                             ALU.mult, ALU.add))
                gates, picks = RT[:, 13, :], RT[:, 8, :]
                tt(picks, RT[:, 9, :], RT[:, 10, :], ALU.add).then_inc(rt_mask, 1)
                bank = take("rank", 5)
                nc.vector.tensor_copy(RT[:, 14, 0:8], bank[:, 16:24])
                link(stt(RT[:, 15, :], bank[:, 0:16], 1.0, picks, ALU.add, ALU.mult))
                nc.vector.memset(LBX[:, 0, 0:1], 0.0).then_inc(emptied["v"], 1)
                place = RT[:, 16, :]
                link(ts(place, RT[:, 15, :], -1.0, None, ALU.add))
                for t in range(NT):
                    nc.vector.tensor_copy(JC[:, 0:NE, t], place[:, 8 * t:8 * t + 8])
                    nc.vector.tensor_copy(JC[:, 0:NE, 2 + t], gates[:, 8 * t:8 * t + 8])
                over, upto, rank = RT[:, 17, 0:8], RT[:, 18, 0:8], RT[:, 19, 0:8]
                link(ts(over, RT[:, 14, 0:8], CAP + 0.5, None, ALU.is_gt))
                link(nc.vector.tensor_tensor_scan(upto, ones[:, 0:8], over, 0.0, ALU.mult, ALU.add))
                tt(rank, upto, over, ALU.subtract)
                nc.vector.tensor_copy(JF[:, 0:NE], iota8)
                link(nc.vector.tensor_copy(JF[:, 15:16], upto[:, 7:8]))
                for e in range(NJMAX - NE):
                    sel, scr = RT[:, 20, 0:8], RT[:, 21, 0:8]
                    link(stt(sel, rank, float(e), over, ALU.is_equal, ALU.mult))
                    link(stt(scr, sel, 1.0, iota8, ALU.mult, ALU.mult, accum_out=JF[:, NE + e:NE + e + 1]))
                    for t in range(NT):
                        w = slice(8 * t, 8 * t + 8)
                        link(stt(scr, sel, 1.0, place[:, w], ALU.mult, ALU.mult, accum_out=RT[:, 22, t:t + 1]))
                        link(stt(scr, sel, 1.0, gates[:, w], ALU.mult, ALU.mult, accum_out=JC[:, NE + e, 2 + t:3 + t]))
                    link(ts(JC[:, NE + e, 0:2], RT[:, 22, 0:2], -float(CAP), None, ALU.add))
                nc.vector.memset(LBX[:, 0, 0:1], 0.0).then_inc(scat_done, 1)
                nc.vector.tensor_copy(JT[:, :], JF[:, :]).then_inc(table_ready, 1)
                dve.wait_ge(table_ready, 1)

            def job(j):
                base = NG * j
                cur = CUR[:, 0, :]
                dve.wait_ge(scat_done, 4 * j + 1)
                nc.vector.tensor_copy(cur, JC[:, bass.ds(j, 1), :].rearrange("p a c -> p (a c)")).then_inc(cur_ready, 1)
                dve.wait_ge(cur_ready, j + 1)
                for t in range(NT):
                    ts(PICK[:, t, :], iota, cur[:, t:t + 1], None, ALU.is_equal).then_inc(pick_ready, 1)
                dve.wait_ge(gather_full, 2 * j + 2)
                for k in range(4, 8):
                    c = C_FFN + KD + k
                    last = ts(VG[:, k, :], psum[5][:, (k - 4) * P:(k - 3) * P], RC[:, c:c + 1], None, ALU.mult)
                last.then_inc(gathered_v, 1)

                def hidden(f, half, wait):
                    dve.wait_ge(e_silu, base + f + 1)
                    dve.wait_ge(e_up, base + f + 1)
                    if wait:
                        dve.wait_ge(e_ht_full, base + f - 1)
                    tt(HS[:, half, :], psum[5 + 2 * half][:, 0:FG], SG[:, half, 0:FG], ALU.mult).then_inc(e_hid, 1)

                hidden(0, 0, False)
                hidden(1, 1, False)
                with dve.Fori(1, NG // 2) as i:
                    hidden(2 * i, 0, True)
                    hidden(2 * i + 1, 1, True)
                dve.wait_ge(e_down, base + NG)
                nc.vector.tensor_copy(YS[:, 512:1024], psum[1][:, :]).then_inc(ys_v, 1)
                for t in range(NT):
                    for c in range(2):
                        dve.wait_ge(scat_full, 4 * j + 2 * t + c + 1)
                        hv = h[:, t, c * 512:(c + 1) * 512]
                        stt(hv, psum[4 + 2 * t + c][:, :], cur[:, 2 + t:3 + t], hv,
                            ALU.mult, ALU.add).then_inc(scat_done, 1)

            def ple(L):
                for n in range(4):
                    two = take(("pp", L, n), n)
                    data(dve, ("pg", L, n))
                    tt(HT[:, n % 2, :], two[:, :], SG[:, n % 2, :], ALU.mult).then_inc(emptied["v"], 1)
                    data(dve, ("pp", L, n))
                    hv = h[:, :, n * FG:(n + 1) * FG]
                    last = tt(hv, hv, HT[:, n % 2, :].rearrange("p (a n) -> p a n", a=2), ALU.add)
                last.then_inc(h_ready, 1)

            for L in range(DEPTH):
                norm(3 * L, 0)
                norm_turned(3 * L, C_MIX + KD * L, 0)
                mixer(L)
                norm(3 * L + 1, 0)
                norm_turned(3 * L + 1, C_FFN + KD * L, 4)
                if L == 0:
                    dense()
                else:
                    route()
                    nj = NE + nc.vector.value_load(JT[0:1, 15:16], min_val=0, max_val=NJMAX - NE)
                    with dve.Fori(0, nj) as j:
                        job(j)
                    dve.wait_ge(scat_done, 4 * nj + 1)
                    nc.vector.memset(LBX[:, 0, 0:1], 0.0).then_inc(h_ready, 1)
                norm(3 * L + 2, 0)
                bank = take(("pT", L), 7)
                nc.vector.tensor_copy(PT_[:, :, :], bank[:, :].rearrange("p (a n) -> p a n", a=2))\
                    .then_inc(emptied["v"], 1)
                norm_turned(3 * L + 2, C_PLE + KD * L, 3)
                ple(L)
            norm(6, None)


_INS = ["x", "p", "w_in", "gla_wg2", "gla_bg", "hg_lb_logits", "gla_onorm", "hg_onorm", "w_out", "norm_mix",
        "norm_ffn", "w_dense_gate", "w_dense_up", "w_dense_down", "w_router", "w_exp_gate", "w_exp_up",
        "w_exp_down", "w_ple_proj", "w_ple_gate", "norm_ple", "norm_final"]
_OUTS = [((1, T, D), "float32")]


def kernel(**inputs):
    import numpy as _np
    import concourse.bacc as _bacc
    from concourse import mybir as _mybir
    from concourse.bass_utils import run_bass_kernel_spmd as _run

    nc = _bacc.Bacc("TRN2", target_bir_lowering=False, num_devices=1)
    arrays, args = {}, []
    for name in _INS + ["consts"]:
        a = shape_constants(_np) if name == "consts" else _np.ascontiguousarray(inputs[name])
        arrays[f"in_{name}_dram"] = a
        args.append(nc.dram_tensor(f"in_{name}_dram", a.shape, _mybir.dt.from_np(a.dtype), kind="ExternalInput").ap())
    for i, (shape, dtype) in enumerate(_OUTS):
        dt = _mybir.dt.from_np(_np.dtype(dtype))
        args.append(nc.dram_tensor(f"out_{i}_dram", shape, dt, kind="ExternalOutput").ap())
    trunk_kernel(nc, *args)
    r = _run(nc, [arrays], core_ids=[0])
    got = tuple(r.results[0][f"out_{i}_dram"] for i in range(len(_OUTS)))
    return got[0]
```

```python
from contextlib import ExitStack

import concourse.bass as bass
import numpy as np
from concourse import mybir

F32 = mybir.dt.float32
BF16 = mybir.dt.bfloat16
F32R = mybir.dt.float32r
I32 = mybir.dt.int32
U32 = mybir.dt.uint32
ACT = mybir.ActivationFunctionType
ALU = mybir.AluOpType

P = 128
D = 1024
T = 256
NT = T // P
KD = D // P
DEPTH = 2
EPS, HEAD_EPS, F_MIN = 1e-6, 1e-5, 1e-6
LN_F_MIN = -13.815510557964274
CHUNK = 64
RANK = 16
FF_DENSE, FF_EXPERT, NE, PLE = 2816, 3584, 8, 256
CAP = 128
NJMAX = NE + 3
FG = 256
RING = 6
SLOT = 2048
SPLIT_RING = 3
SUB = 8
SUB_SCALE = 2.0 ** -14
LEVELS = (8, 16, 32)

SPLIT = dict(gq=0, gk=256, gv=512, gr=1024, glr=1536, hq=1568, hff=2080, hfb=2592, hv=3104, hr=3616)
PROJ = [("gr", 0, "tok", "a"), ("gr", 1, "tok", "a"), ("hr", 0, "tok", "a"), ("hr", 1, "tok", "a"),
        ("hq", 0, "col", "a"), ("hq", 1, "col", "a"), ("hff", 0, "col", "a"), ("hff", 1, "col", "a"),
        ("hfb", 0, "col", "a"), ("hfb", 1, "col", "a"), ("glr", 0, "low", "v"), ("gq", 0, "col", "v"),
        ("gk", 0, "col", "v"), ("z", 0, "decay", "v"), ("z", 1, "decay", "v"), ("gv", 0, "tok", "v"),
        ("gv", 1, "tok", "v"), ("hv", 0, "tok", "v"), ("hv", 1, "tok", "v")]
PROJ_BANK = {(s[0], s[1]): (4 + n) % 8 for n, s in enumerate(PROJ)}

C_MIX, C_FFN, C_PLE, C_BG, C_LB, C_GON, C_HON, NROW = 0, 16, 32, 48, 56, 72, 74, 76

O_MASK = 0
O_ID = O_MASK + 7 * P
O_IOTA = O_ID + P
O_TRI = O_IOTA + P
O_ONE = O_TRI + P
O_RST = O_ONE + P
NCONST = O_RST + T

HEADS = [[(u, 64 * hh, 64, 2 * u + hh) for hh in range(2)] for u in range(2)] + \
        [[(u, 0, P, 4 + u - 2)] for u in range(2, 6)]
PAIRS = [[(hd, t) for hd in heads for t in range(NT)] for heads in HEADS]
GROUPS_OF = [2 * len(p) for p in PAIRS]
NGROUP = sum(GROUPS_OF)
GROUP0 = [sum(GROUPS_OF[:u]) for u in range(6)]


def shape_constants(np):
    c = np.zeros((P, NCONST), np.float32)
    s, t = np.arange(P)[:, None], np.arange(P)[None, :]
    same = lambda n: (s // n) == (t // n)
    masks = [same(SUB) * (s <= t) / SUB_SCALE ** 2, same(SUB) * (s >= t) / SUB_SCALE ** 2]
    for m in LEVELS + (CHUNK,):
        masks.append(same(2 * m) * ((s // m) != (t // m)))
    for n, m in enumerate(masks + [np.ones((P, P))]):
        c[:, O_MASK + n * P:O_MASK + (n + 1) * P] = m
    c[:, O_ID:O_ID + P] = np.eye(P)
    c[:, O_IOTA:O_IOTA + P] = t
    c[:, O_TRI:O_TRI + P] = s < t
    c[:, O_ONE:O_ONE + P] = 1.0
    c[:, O_RST:O_RST + T] = (np.arange(T) % CHUNK != 0)[None, :]
    return c


def product_order():
    order = [("rows", "v")]
    for L in range(DEPTH):
        order += [(("normT", 3 * L, b), "v") for b in range(4)]
        order += [((part, piece, L), engine) for part, piece, _, engine in PROJ]
        order += [(("yT", L, b), "v") for b in range(4)]
        order += [(("mix", L, n), "v") for n in range(4)]
        order += [(("normT", 3 * L + 1, b), "v") for b in range(4)]
        if L == 1:
            order += [("logits", "v"), ("rank", "v")]
        order += [(("pT", L), "v")]
        order += [(("normT", 3 * L + 2, b), "v") for b in range(4)]
        order += [(("pp", L, n), "v") for n in range(4)]
        order += [(("pg", L, n), "a") for n in range(4)]
    return order


def numbered(order):
    taken, out = {"a": 0, "v": 0}, {}
    for n, (name, engine) in enumerate(order):
        taken[engine] += 1
        out[name] = (n + 1, engine, taken[engine])
    return out


def trunk_kernel(nc, x, p, w_in, gla_wg2, gla_bg, hg_lb_logits, gla_onorm, hg_onorm, w_out, norm_mix,
                 norm_ffn, w_dense_gate, w_dense_up, w_dense_down, w_router, w_exp_gate, w_exp_up,
                 w_exp_down, w_ple_proj, w_ple_gate, norm_ple, norm_final, consts, out):
    ctx = ExitStack()
    with ctx:
        def sb(name, shape, dt=F32):
            return ctx.enter_context(nc.sbuf_tensor(name, shape, dt))

        def sem(name):
            return ctx.enter_context(nc.semaphore(name))

        def shared(first, second):
            places = []
            for tiles in (first, second):
                with ExitStack() as scope:
                    places.append([scope.enter_context(nc.sbuf_tensor(name, shape, dt)) for name, shape, dt in tiles])
            size = max(sum(4 * int(np.prod(shape[1:])) for _, shape, _ in tiles) for tiles in (first, second))
            ctx.enter_context(nc.sbuf_tensor("place_of_" + first[0][0], [P, size // 4], F32))
            return places

        ring = sb("ring", [P, RING, SLOT])
        h = sb("h", [P, NT, D])
        hn = sb("hn", [P, NT, D])
        (XH, XL), (X2,) = shared([("XH", [P, KD, T], F32R), ("XL", [P, KD, T], F32R)],
                                 [("X2", [P, 8, 2, T], F32)])
        (W,), (X,) = shared([("W", [P, SPLIT_RING, 2, SLOT], F32R)], [("X", [P, SPLIT_RING, 8, 2, T], F32)])
        assert 8 * 2 * T == 2 * SLOT
        (V, SR, Q, K, G), (SG, HS, HH, HL, VH, VL, YH, YL, PICK, PICKT) = shared(
            [("V", [P, NT, D], F32), ("SR", [P, NT, D], F32), ("Q", [P, 6, T], F32), ("K", [P, 2, 6, T], F32),
             ("G", [P, 2, 6, T], F32)],
            [("SG", [P, 2, 512], F32), ("HS", [P, 2, 512], F32), ("HH", [P, 2, 512], F32R),
             ("HL", [P, 2, 512], F32R), ("VH", [P, KD, CAP], F32R), ("VL", [P, KD, CAP], F32R),
             ("YH", [P, D], F32R), ("YL", [P, D], F32R), ("PICK", [P, NT, CAP], F32), ("PICKT", [P, T], F32R)])
        NF = G[:, 0, 0:4, :].rearrange("p a b -> p (a b)")
        CST = sb("CST", [P, NCONST])
        RV = sb("RV", [NROW, P])
        RC = sb("RC", [P, NROW])
        LB = sb("LB", [P, 4, 8])
        LBX = sb("LBX", [P, 6, 8])
        TOT = sb("TOT", [P, 2, 6, 4])
        EF = sb("EF", [P, 2, 6, 4])
        WG2 = sb("WG2", [2 * RANK, DEPTH, 2, T])
        GLT = sb("GLT", [2 * RANK, T])
        PIN = sb("PIN", [P, DEPTH, NT, PLE])
        PH = sb("PH", [P, 2, T], F32R)
        PL = sb("PL", [P, 2, T], F32R)
        WR = sb("WR", [P, KD, NE])
        WRH = sb("WRH", [P, KD, NE], F32R)
        WRL = sb("WRL", [P, KD, NE], F32R)
        STAT = sb("STAT", [P, 3, 7, NT])
        HST = sb("HST", [P, 3, 16])
        ZB = sb("ZB", [1, 512], BF16)
        RT = sb("RT", [P, 24, 16])
        IDX = sb("IDX", [P, NT, 8], U32)
        JC = sb("JC", [P, NJMAX + 1, 4])
        JF = sb("JF", [P, 16])
        JT = sb("JT", [P, 16], I32)
        PLACE = sb("PLACE", [P, NT])
        GATE = sb("GATE", [P, NT])

        psum = [ctx.enter_context(nc.psum_tensor(f"bank{i}", [P, 512], F32)) for i in range(8)]

        ident = CST[:, O_ID:O_ID + P]
        iota = CST[:, O_IOTA:O_IOTA + P]
        iota8 = CST[:, O_IOTA:O_IOTA + NE]
        tri = CST[:, O_TRI:O_TRI + P]
        ones = CST[:, O_ONE:O_ONE + P]
        one_col = CST[:, O_ONE:O_ONE + 1]
        reset = CST[:, O_RST:O_RST + T]

        x_in = sem("x_in")
        small_in = sem("small_in")
        last_in = sem("last_in")
        high_ready = sem("high_ready")
        split_ready = sem("split_ready")
        xh_ready = sem("xh_ready")
        router_high = sem("router_high")
        router_ready = sem("router_split")
        hh_ready = sem("hidden_high")
        slot_full = [sem(f"slot_full{i}") for i in range(RING)]
        filled = sem("filled")
        emptied = {"a": sem("emptied_by_scalar"), "v": sem("emptied_by_vector")}
        dve_step = sem("dve_step")
        zeroed = sem("zeroed")
        lb_shifted = sem("lb_shifted")
        lb_exp = sem("lb_exp")
        squares = sem("squares")
        mean_ready = sem("mean_ready")
        root_ready = sem("root_ready")
        hn_ready = sem("hn_ready")
        h_ready = sem("h_ready")
        forget_ready = sem("forget_ready")
        logf_ready = sem("logf_ready")
        softplus_step = sem("softplus_step")
        sums_ready = sem("sums_ready")
        edge_ready = sem("edge_ready")
        diff_ready = sem("diff_ready")
        exp_ready = sem("exp_ready")
        diag_ready = sem("diag_ready")
        decayed_ready = sem("decayed_ready")
        score_full = sem("score_full")
        masked = sem("masked")
        summed = sem("summed")
        av_done = sem("av_done")
        osq = sem("head_squares")
        omean = sem("head_mean")
        oroot = sem("head_root")
        y_ready = sem("y_ready")
        gu_full = [sem("gate_full"), sem("up_full")]
        silu_ready = sem("silu_ready")
        hs_ready = sem("hidden_rows")
        hidden_ready = sem("hidden_ready")
        down_done = sem("down_done")
        rt_shift = sem("router_shifted")
        rt_exp = sem("router_exp")
        rt_mask = sem("router_mask")
        table_ready = sem("table_ready")
        place_ready = sem("place_ready")
        pick_ready = sem("pick_ready")
        gather_full = sem("gather_full")
        vh_ready = sem("gathered_high")
        gathered = sem("gathered")
        gate_ready = sem("gate_ready")
        pickT_full = sem("pickT_full")
        pickT_ready = sem("pickT_ready")
        e_gate = sem("exp_gate_full")
        e_up = sem("exp_up_full")
        e_silu = sem("exp_silu")
        e_hid = sem("exp_hidden")
        e_ht_full = sem("exp_hiddenT_full")
        e_hh = sem("exp_hiddenT_high")
        e_ht = sem("exp_hiddenT")
        e_down = sem("exp_down_done")
        yh_ready = sem("exp_y_high")
        ys_ready = sem("exp_y_split")
        scat_full = sem("scatter_full")
        scat_done = sem("scatter_done")
        out_done = sem("out_done")

        number = numbered(product_order())
        ND = FF_DENSE // FG
        NG = FF_EXPERT // FG
        assert ND % 2 == 1 and NG % 2 == 0 and (3 * NG) % RING == 0
        UNITS = []
        for L in range(DEPTH):
            UNITS += [("in", L, part, piece) for part, piece, form, _ in PROJ if form != "decay"]
            UNITS += [("out", L, n) for n in range(4)]
            if L == 0:
                UNITS += [("dg", 0), ("du", 0)]
                for f in range(1, ND):
                    UNITS += [("dg", f), ("du", f), ("dd", f - 1)]
                UNITS += [("dd", ND - 1), ("pp", L)] + [("pg", L, n) for n in range(4)]
        U0 = {u: n for n, u in enumerate(UNITS)}
        UE = len(UNITS)
        TAIL = [("pp", 1)] + [("pg", 1, n) for n in range(4)]
        NSMALL = 9 + 3 * DEPTH

        def col_view(w):
            return w.rearrange("(k p) n -> p k n", p=P)

        def cols(s):
            return [W[:, s, i, :].rearrange("p (k n) -> p k n", k=KD) for i in range(2)]

        def rows(s):
            return [W[:, s, i, :].rearrange("p (k n) -> p k n", k=2) for i in range(2)]

        def decayed(L, u):
            last = U0[("in", L, "hv", 1)]
            return X2[:, :, :, :] if u % 3 == 2 else X[:, (last - 2 + u % 3) % SPLIT_RING, :, :, :]

        def masked_scores(L, n):
            slot = U0[("in", L, "hv", 1)] % SPLIT_RING
            return X[:, slot, 0:4, :, :].rearrange("p a d t -> p a (d t)")[:, n % 4, :]

        def head_output(head, t):
            c = 2 * t + head % 2
            return psum[head // 2][:, c * P:(c + 1) * P]

        def part_of(t, offset, dims):
            a = t[(slice(None),) * len(t.shape)]
            return bass.AP(a.tensor, a.offset + offset, [a.ap[0]] + [[s, n] for s, n in dims])

        block = ctx.enter_context(nc.Block())

        @block.sync
        def _(sp):
            sp.dma_start(h[:, :, :], x[0].rearrange("(t p) d -> p t d", p=P)).then_inc(x_in, 16)
            small = [
                (CST[:, :], consts),
                (RV[C_MIX:C_MIX + 16, :], norm_mix.rearrange("l (k p) -> (l k) p", p=P)),
                (RV[C_FFN:C_FFN + 16, :], norm_ffn.rearrange("l (k p) -> (l k) p", p=P)),
                (RV[C_PLE:C_PLE + 16, :], norm_ple.rearrange("l (k p) -> (l k) p", p=P)),
                (RV[C_BG:C_BG + 8, :], gla_bg.rearrange("l d (u p) -> (l d u) p", p=P)),
                (RV[C_LB:C_LB + 16, :], hg_lb_logits.rearrange("l d (u p) -> (l d u) p", p=P)),
                (RV[C_GON:C_GON + 2, :], gla_onorm),
                (RV[C_HON:C_HON + 2, :], hg_onorm),
                (WR[:, :, :], w_router[0].rearrange("(k p) e -> p k e", p=P)),
            ]
            for L in range(DEPTH):
                small.append((PIN[:, L, :, :], p[L, 0].rearrange("(t p) d -> p t d", p=P)))
            for dst, src in small:
                sp.dma_start(dst, src).then_inc(small_in, 16)
            sp.wait_ge(zeroed, 1)
            for L in range(DEPTH):
                for d in range(2):
                    sp.dma_start(WG2[RANK * d:RANK * (d + 1), L, d, :], gla_wg2[L, d]).then_inc(small_in, 16)

            def load(n, src, further=0):
                if not isinstance(further, int) or n + further >= RING:
                    sp.wait_ge(split_ready, further + n - RING + 1)
                dst = ring[:, n % RING, :].rearrange("p (k n) -> p k n", k=src.shape[1])
                sp.dma_start(dst, src).then_inc(slot_full[n % RING], 16)

            def source(u):
                if u[0] == "in":
                    c = SPLIT[u[2]] + u[3] * FG
                    return col_view(w_in[u[1]])[:, :, c:c + FG]
                if u[0] == "out":
                    return col_view(w_out[u[1]])[:, :, u[2] * FG:(u[2] + 1) * FG]
                if u[0] in ("dg", "du"):
                    w = w_dense_gate if u[0] == "dg" else w_dense_up
                    return col_view(w[0])[:, :, u[1] * FG:(u[1] + 1) * FG]
                if u[0] == "dd":
                    return w_dense_down[0, u[1] * FG:(u[1] + 1) * FG, :].rearrange("(k p) n -> p k n", p=P)
                if u[0] == "pp":
                    return w_ple_proj[u[1]].rearrange("(k p) n -> p k n", p=P)
                return col_view(w_ple_gate[u[1]])[:, :, u[2] * FG:(u[2] + 1) * FG]

            for n, u in enumerate(UNITS):
                load(n, source(u))

            gate_v = w_exp_gate[0].rearrange("e (k p) f -> p e k f", p=P)
            up_v = w_exp_up[0].rearrange("e (k p) f -> p e k f", p=P)
            down_v = w_exp_down[0].rearrange("e (g k p) n -> p e g k n", p=P, k=2)

            def job_loads(e, j):
                def gate(f, n, i):
                    load(UE + n, gate_v[:, bass.ds(e, 1), :, bass.ds(f * FG, FG)].rearrange("p e k f -> p (e k) f"),
                         3 * NG * j + RING * i)

                def up(f, n, i):
                    load(UE + n, up_v[:, bass.ds(e, 1), :, bass.ds(f * FG, FG)].rearrange("p e k f -> p (e k) f"),
                         3 * NG * j + RING * i)

                def down(f, n, i):
                    load(UE + n, down_v[:, bass.ds(e, 1), bass.ds(f, 1), :, :].rearrange("p e g k n -> p (e g k) n"),
                         3 * NG * j + RING * i)

                gate(0, 0, 0)
                up(0, 1, 0)
                with sp.Fori(0, NG // 2 - 1) as i:
                    for c in range(2):
                        f = 2 * i + 1 + c
                        gate(f, 2 + 3 * c, i)
                        up(f, 3 + 3 * c, i)
                        down(f - 1, 4 + 3 * c, i)
                gate(NG - 1, 3 * NG - 4, 0)
                up(NG - 1, 3 * NG - 3, 0)
                down(NG - 2, 3 * NG - 2, 0)
                down(NG - 1, 3 * NG - 1, 0)

            job_loads(0, 0)
            sp.wait_ge(table_ready, 1)
            nj = NE + nc.sync.value_load(JT[0:1, 15:16], min_val=0, max_val=NJMAX - NE)
            with sp.Fori(1, nj) as j:
                job_loads(nc.sync.value_load(JT[0:1, bass.ds(j, 1)], min_val=0, max_val=NE - 1), j)
            for n, u in enumerate(TAIL):
                load(UE + n, source(u), 3 * NG * nj)
            sp.dma_start(NF, norm_final.rearrange("(a d) -> a d", a=1).to_broadcast([P, D])).then_inc(last_in, 16)
            sp.wait_ge(h_ready, 7)
            sp.dma_start(out[0].rearrange("(t p) d -> p t d", p=P), hn[:, :, :]).then_inc(out_done, 16)
            sp.wait_ge(out_done, 16)

        def used(eng, u):
            if u[0] in ("dg", "du"):
                eng.wait_ge(gu_full[u[0] == "du"], u[1] + 1)
            elif u[0] == "dd":
                eng.wait_ge(down_done, u[1] + 1)
            else:
                name = {"in": lambda: (u[2], u[3], u[1]), "out": lambda: ("mix", u[1], u[2]),
                        "pp": lambda: ("pp", u[1], 3), "pg": lambda: ("pg", u[1], u[2])}[u[0]]()
                eng.wait_ge(filled, number[name][0])

        def data(eng, name):
            _, engine, n = number[name]
            eng.wait_ge(emptied[engine], n)

        @block.tensor
        def _(pe):
            mm = nc.tensor.matmul

            def split(n, further=0):
                pe.wait_ge(split_ready, n + 1 + further)
                return n % SPLIT_RING

            def three(out, left, right, start, stop):
                mm(out, left[0], right[0], start=start, stop=False, skip_group_check=True)
                mm(out, left[0], right[1], start=False, stop=False, skip_group_check=True)
                return mm(out, left[1], right[0], start=False, stop=stop, skip_group_check=True)

            def parts(pair, *at):
                return [x[at] for x in pair]

            ALL = slice(None)
            def transposes(bank, src):
                for kk in range(2):
                    for t in range(NT):
                        last = nc.tensor.transpose(bank[:, kk * T + t * P:kk * T + (t + 1) * P], src(kk, t), ident)
                last.then_inc(filled, 1)

            def turn_tokens(name, first_bank, before=None):
                for b in range(4):
                    if before is not None and before[b] is not None:
                        data(pe, before[b])
                    transposes(psum[first_bank + b],
                               lambda kk, t: hn[:, t, (2 * b + kk) * P:(2 * b + kk + 1) * P])
                for b in range(4):
                    data(pe, name + (b,))

            def columns(bank, w, count=2):
                for c in range(count):
                    for k in range(KD):
                        last = three(bank[:, c * T:(c + 1) * T], parts(w, ALL, k, slice(c * P, (c + 1) * P)),
                                     [XH[:, k, :], XL[:, k, :]], k == 0, k == KD - 1)
                return last

            def tokens(bank, w, act, kt=KD, at=slice(0, FG)):
                for t in range(NT):
                    for k in range(kt):
                        last = three(bank[:, t * FG:(t + 1) * FG], parts(act, ALL, k, slice(t * P, (t + 1) * P)),
                                     parts(w, ALL, k, at), k == 0, k == kt - 1)
                return last

            pe.wait_ge(small_in, 16 * NSMALL)
            nc.tensor.transpose(psum[7][:, 0:NROW], RV[:, :], ident[0:NROW, 0:NROW]).then_inc(filled, 1)

            def project(L):
                pe.wait_ge(hn_ready, 3 * L + 1)
                turn_tokens(("normT", 3 * L), 0, [("pp", 0, b) for b in range(4)] if L else None)
                held = [("pg", 0, b) for b in range(4)] if L else [None, None, None, "rows"]
                held += [("normT", 3 * L, b) for b in range(4)]
                for i, (part, piece, form, _) in enumerate(PROJ):
                    before = held[i] if i < 8 else PROJ[i - 8][:2] + (L,)
                    if before is not None:
                        data(pe, before)
                    bank = psum[PROJ_BANK[part, piece]]
                    if form == "low":
                        last = columns(bank, cols(split(U0[("in", L, part, piece)])), 1)
                    elif form == "decay":
                        data(pe, ("glr", 0, L))
                        for u in range(2):
                            last = mm(bank[:, u * T:(u + 1) * T], WG2[:, L, piece, u * P:(u + 1) * P], GLT[:, :],
                                      start=True, stop=True)
                    else:
                        w = cols(split(U0[("in", L, part, piece)]))
                        last = columns(bank, w) if form == "col" else tokens(bank, w, (XH, XL))
                    last.then_inc(filled, 1)

            def scan(L):
                data(pe, ("hfb", 1, L))
                data(pe, ("hv", 1, L))
                waiting = []

                def scores(g, ins):
                    n = L * NGROUP + g
                    if n >= 4:
                        pe.wait_ge(masked, n - 3)
                    c = 0
                    for keys, k_ap, q_ap in ins:
                        last = mm(psum[4 + n % 4][keys, c * P:(c + 1) * P], k_ap, q_ap, start=True, stop=True)
                        c += keys.stop == P
                    last.then_inc(score_full, 1)

                def weighted(g, sources, head, t, first, final):
                    n = L * NGROUP + g
                    if g % 2:
                        pe.wait_ge(masked, n + 1)
                    else:
                        pe.wait_ge(summed, n // 2 + 1)
                    o = head_output(head, t)
                    for c, s in enumerate(sources):
                        last = mm(o, masked_scores(L, n)[:, c * P:(c + 1) * P], V[:, s, head * P:(head + 1) * P],
                                  start=(first and c == 0), stop=(final and c == len(sources) - 1),
                                  skip_group_check=True)
                    last.then_inc(av_done, 1)

                g = 0
                for u in range(6):
                    xb, n = decayed(L, u), L * 6 + u
                    pe.wait_ge(diag_ready, 2 * n + 2)
                    pe.wait_ge(decayed_ready, 10 * n + 4)
                    for (_, p0, kd, head), t in PAIRS[u]:
                        dims, at = slice(p0, p0 + kd), slice(t * P, (t + 1) * P)

                        cross = 1 - t
                        half = [slice(t * P, t * P + CHUNK), slice(t * P + CHUNK, (t + 1) * P)]
                        whole = slice(0, P)
                        groups = [[(whole, xb[dims, 1, d, at], xb[dims, 0, d, at]) for d in range(2)] +
                                  [(whole, xb[dims, s, 0, at], xb[dims, s, 1, at]) for s in (2, 3)],
                                  [(whole, xb[dims, 4, 0, at], xb[dims, 4, 1, at])] +
                                  [(slice(d * CHUNK, (d + 1) * CHUNK), xb[dims, 6, d, half[d]], xb[dims, 5, d, at])
                                   for d in range(2)] +
                                  [(whole, xb[dims, 7, cross, 0:P], xb[dims, 7, cross, P:2 * P])]]
                        for i, ins in enumerate(groups):
                            if i == 1:
                                pe.wait_ge(decayed_ready, 10 * n + 10)
                            scores(g, ins)
                            waiting.append((g, [[t, t], [t, t, 1 - t]][i], head, t, i == 0, i == 1))
                            g += 1
                            if len(waiting) > 2:
                                weighted(*waiting.pop(0))
                for w in waiting:
                    weighted(*w)

            def mix_out(L):
                pe.wait_ge(y_ready, L + 1)
                turn_tokens(("yT", L), 4)
                for n in range(4):
                    tokens(psum[n], cols(split(U0[("out", L, n)])), (XH, XL)).then_inc(filled, 1)

            def dense():
                for n in range(4):
                    data(pe, ("mix", 0, n))
                for b in range(4):
                    mm(psum[b][:, :], ZB[0:1, 0:P], ZB[0:1, :], start=True, stop=False, skip_group_check=True)
                first = U0[("dg", 0)]

                def gate_up(half, n, further, free):
                    for c in range(2):
                        if free is not None:
                            pe.wait_ge((silu_ready, hs_ready)[c], free)
                        columns(psum[4 + c + 2 * half], cols(split(n + c, further))).then_inc(gu_full[c], 1)

                def down(half, n, further, ready, final=False):
                    pe.wait_ge(hidden_ready, ready)
                    w = rows(split(n, further))
                    for k in range(2):
                        for t in range(NT):
                            for c in range(2):
                                last = three(psum[2 * t + c][:, :],
                                             parts((HH, HL), ALL, half, slice(k * T + t * P, k * T + (t + 1) * P)),
                                             parts(w, ALL, k, slice(c * 512, (c + 1) * 512)), False, final and k == 1)
                    last.then_inc(down_done, 1)

                gate_up(0, first, 0, None)
                gate_up(1, first + 2, 0, None)
                down(0, first + 4, 0, 1)
                gate_up(0, first + 5, 0, 1)
                down(1, first + 7, 0, 2)
                with pe.Fori(1, ND // 2) as i:
                    gate_up(1, first + 2, RING * i, 2 * i)
                    down(0, first + 4, RING * i, 2 * i + 1)
                    gate_up(0, first + 5, RING * i, 2 * i + 1)
                    down(1, first + 7, RING * i, 2 * i + 2)
                down(0, first + 3 * ND - 1, 0, ND, final=True)

            def route():
                data(pe, ("normT", 4, 0))
                bank = psum[4]
                pe.wait_ge(router_ready, 1)
                for t in range(NT):
                    for k in range(KD):
                        last = three(bank[:, t * NE:(t + 1) * NE], parts((XH, XL), ALL, k, slice(t * P, (t + 1) * P)),
                                     parts((WRH, WRL), ALL, k), k == 0, k == KD - 1)
                last.then_inc(filled, 1)
                data(pe, ("normT", 4, 1))
                bank = psum[5]
                pe.wait_ge(rt_mask, 1)
                m = RT[:, 8, :]
                mm(bank[:, 0:8], tri, m[:, 0:8], start=True, stop=True)
                mm(bank[:, 8:16], ones, m[:, 0:8], start=True, stop=False)
                mm(bank[:, 8:16], tri, m[:, 8:16], start=False, stop=True)
                mm(bank[:, 16:24], ones, m[:, 0:8], start=True, stop=False)
                mm(bank[:, 16:24], ones, m[:, 8:16], start=False, stop=True).then_inc(filled, 1)

            def gather(j):
                pe.wait_ge(pick_ready, 2 * j + 2)
                for k in range(KD):
                    for t in range(NT):
                        last = mm(psum[2 + k // 4][:, (k % 4) * P:(k % 4 + 1) * P], hn[:, t, k * P:(k + 1) * P],
                                  PICK[:, t, :], start=(t == 0), stop=(t == NT - 1))
                    if k % 4 == 3:
                        last.then_inc(gather_full, 1)

            def job(j):
                base = NG * j
                further = 3 * NG * j
                pe.wait_ge(gathered, 2 * j + 2)
                for t in range(NT):
                    last = nc.tensor.transpose(psum[2][:, t * P:(t + 1) * P], PICK[:, t, :], ident)
                last.then_inc(pickT_full, 1)

                def gate_or_up(f, half, which, n, on, wait):
                    if wait:
                        pe.wait_ge((e_silu, e_hid)[which], base + f - 1)
                    w = cols(split(n, on))
                    for k in range(KD):
                        last = three(psum[4 + 2 * half + which][:, 0:FG], parts((VH, VL), ALL, k), parts(w, ALL, k),
                                     k == 0, k == KD - 1)
                    last.then_inc((e_gate, e_up)[which], 1)

                def turn(f, half, wait):
                    pe.wait_ge(e_hid, base + f + 1)
                    if wait:
                        pe.wait_ge(e_ht, base + f - 1)
                    for k in range(2):
                        last = nc.tensor.transpose(psum[2 + half][:, k * P:(k + 1) * P],
                                                   HS[:, half, k * P:(k + 1) * P], ident)
                    last.then_inc(e_ht_full, 1)

                def down(f, half, n, on, first=False, final=False):
                    pe.wait_ge(e_ht, base + f + 1)
                    w = rows(split(n, on))
                    for k in range(2):
                        for c in range(2):
                            last = three(psum[c][:, :], parts((HH, HL), ALL, half, slice(k * P, (k + 1) * P)),
                                         parts(w, ALL, k, slice(c * 512, (c + 1) * 512)),
                                         first and k == 0, final and k == 1)
                    last.then_inc(e_down, 1)

                def step(f, half, n, on, wait, turn_wait=True, first=False):
                    gate_or_up(f, half, 0, n, on, wait)
                    turn(f - 1, 1 - half, turn_wait)
                    gate_or_up(f, half, 1, n + 1, on, wait)
                    down(f - 1, 1 - half, n + 2, on, first)

                pe.wait_ge(scat_done, 4 * j + 1)
                gate_or_up(0, 0, 0, UE, further, False)
                pe.wait_ge(scat_done, 4 * j + 2)
                gate_or_up(0, 0, 1, UE + 1, further, False)
                pe.wait_ge(scat_done, 4 * j + 4)
                pe.wait_ge(pickT_ready, j + 1)
                step(1, 1, UE + 2, further, False, turn_wait=False, first=True)
                step(2, 0, UE + 5, further, True, turn_wait=False)
                with pe.Fori(1, NG // 2 - 1) as i:
                    step(2 * i + 1, 1, UE + 2, further + RING * i, True)
                    step(2 * i + 2, 0, UE + 5, further + RING * i, True)
                gate_or_up(NG - 1, 1, 0, UE + 3 * NG - 4, further, True)
                turn(NG - 2, 0, True)
                gate_or_up(NG - 1, 1, 1, UE + 3 * NG - 3, further, True)
                down(NG - 2, 0, UE + 3 * NG - 2, further)
                turn(NG - 1, 1, True)
                down(NG - 1, 1, UE + 3 * NG - 1, further, final=True)
                gather(j + 1)
                pe.wait_ge(ys_ready, j + 1)
                for t in range(NT):
                    for c in range(2):
                        bank, place = psum[4 + 2 * t + c][:, :], PICKT[:, t * P:(t + 1) * P]
                        mm(bank, place, YH[:, c * 512:(c + 1) * 512], start=True, stop=False)
                        mm(bank, place, YL[:, c * 512:(c + 1) * 512], start=False, stop=True).then_inc(scat_full, 1)

            def ple(L, base, further):
                pe.wait_ge(hn_ready, 3 * L + 3)
                transposes(psum[7], lambda kk, t: PIN[:, L, t, kk * P:(kk + 1) * P])
                turn_tokens(("normT", 3 * L + 2), 3)
                data(pe, ("pT", L))
                w = rows(split(base, further))
                for n in range(4):
                    tokens(psum[n], w, (PH, PL), 2, slice(n * FG, (n + 1) * FG)).then_inc(filled, 1)
                for n in range(4):
                    tokens(psum[4 + n], cols(split(base + 1 + n, further)), (XH, XL)).then_inc(filled, 1)

            for L in range(DEPTH):
                project(L)
                scan(L)
                mix_out(L)
                pe.wait_ge(hn_ready, 3 * L + 2)
                turn_tokens(("normT", 3 * L + 1), 4, [("yT", L, b) for b in range(4)])
                if L == 0:
                    dense()
                    ple(0, U0[("pp", 0)], 0)
                else:
                    route()
                    pe.wait_ge(table_ready, 1)
                    nj = NE + nc.tensor.value_load(JT[0:1, 15:16], min_val=0, max_val=NJMAX - NE)
                    gather(0)
                    with pe.Fori(0, nj) as j:
                        job(j)
                    ple(1, UE, 3 * NG * nj)

        def both_ways(t, offset, m, step):
            return part_of(t, offset, [[step + m, 2], [2 * m, T // (2 * m)], [1, m]])

        @block.scalar
        def _(act):
            fn = nc.scalar.activation

            def take(name, bank):
                act.wait_ge(filled, number[name][0])
                return psum[bank]

            def high(n, turns=0):
                act.wait_ge(slot_full[n % RING], 16 * (n // RING + 1) + 16 * turns)
                fn(W[:, n % SPLIT_RING, 0, :], ring[:, n % RING, :], ACT.Copy).then_inc(high_ready, 1)

            def follow(u):
                used(act, u)
                high(U0[u] + SPLIT_RING)

            def scaled_high(name, first_bank, column):
                for b in range(4):
                    bank = take(name + (b,), first_bank + b)
                    for c in range(2):
                        col = column(2 * b + c)
                        last = fn(XH[:, 2 * b + c, :], bank[:, c * T:(c + 1) * T], ACT.Copy, scale=RC[:, col:col + 1])
                    last.then_inc(xh_ready, 1)

            for n in range(SPLIT_RING):
                high(n)
            act.wait_ge(lb_shifted, 1)
            fn(LBX[:, 3:5, :], LBX[:, 1:3, :], ACT.Exp).then_inc(lb_exp, 1)
            fn(WRH[:, :, :], WR[:, :, :], ACT.Copy).then_inc(router_high, 1)

            def norm(r):
                if r == 0:
                    act.wait_ge(x_in, 16)
                else:
                    act.wait_ge(h_ready, r)
                for t in range(NT):
                    fn(hn[:, t, :], h[:, t, :], ACT.Square, accum_out=STAT[:, 0, r, t:t + 1]).then_inc(squares, 1)
                act.wait_ge(mean_ready, r + 1)
                fn(STAT[:, 2, r, :], STAT[:, 1, r, :], ACT.Sqrt).then_inc(root_ready, 1)
                data(act, "rows")

            def head_squares(L, bank, unit):
                act.wait_ge(av_done, L * NGROUP + GROUP0[unit] + GROUPS_OF[unit])
                for head in (2 * bank, 2 * bank + 1):
                    for t in range(NT):
                        n = 8 * (head // 4) + 4 * t + head % 4
                        fn(hn[:, t, head * P:(head + 1) * P], head_output(head, t), ACT.Square,
                           accum_out=HST[:, 0, n:n + 1]).then_inc(osq, 1)

            def mixer(L):
                last_unit = U0[("in", L, "hv", 1)]
                for part, piece, form, engine in PROJ:
                    if engine == "a":
                        bank = take((part, piece, L), PROJ_BANK[part, piece])
                        two = bank[:, :].rearrange("p (a n) -> p a n", a=2)
                        if form == "tok":
                            c = piece * FG + (512 if part == "hr" else 0)
                            fn(SR[:, :, c:c + FG], two, ACT.Silu).then_inc(emptied["a"], 1)
                        elif part == "hq":
                            fn(Q[:, 2 + 2 * piece:4 + 2 * piece, :], two, ACT.Silu).then_inc(emptied["a"], 1)
                        else:
                            d, u = (0 if part == "hff" else 1), 2 + 2 * piece
                            fn(G[:, d, u:u + 2, :], two, ACT.Sigmoid)
                            fn(K[:, d, u:u + 2, :], two, ACT.Sigmoid, scale=-1.0).then_inc(emptied["a"], 1)
                    if form != "decay" and U0[("in", L, part, piece)] + SPLIT_RING <= last_unit:
                        follow(("in", L, part, piece))
                    if part == "gk":
                        act.wait_ge(forget_ready, L + 1)
                        fn(G[:, :, 2:6, :], G[:, :, 2:6, :], ACT.Ln).then_inc(logf_ready, 1)
                    if (part, piece) == ("z", 1):
                        data(act, ("z", 1, L))
                        soft = hn[:, 0, :].rearrange("p (d u t) -> p d u t", d=2, u=2)
                        fn(soft, G[:, :, 0:2, :], ACT.Abs).then_inc(softplus_step, 1)
                        act.wait_ge(softplus_step, 3 * L + 1)
                        fn(soft, soft, ACT.Exp, scale=-1.0).then_inc(softplus_step, 1)
                        act.wait_ge(softplus_step, 3 * L + 2)
                        fn(soft, soft, ACT.Ln, bias=1.0).then_inc(softplus_step, 1)
                act.wait_ge(sums_ready, L + 1)
                for d, place, c in ((0, 0, 1), (0, 3, 2), (1, 1, 2), (1, 2, 1)):
                    fn(EF[:, d, :, place], TOT[:, d, :, c], ACT.Exp).then_inc(edge_ready, 1)
                for u in range(6):
                    n, xb = L * 6 + u, decayed(L, u)
                    act.wait_ge(diff_ready, 5 * n + 1)
                    fn(xb[:, 1, :, :], xb[:, 0, :, :], ACT.Exp, scale=-1.0).then_inc(exp_ready, 1)
                    fn(xb[:, 0, :, :], xb[:, 0, :, :], ACT.Exp).then_inc(exp_ready, 1)
                    for i, m in enumerate(LEVELS):
                        act.wait_ge(diff_ready, 5 * n + 2 + i)
                        for role in range(2):
                            v = xb[:, 2 + i, role, :]
                            fn(v, v, ACT.Exp, scale=1.0 if role else -1.0).then_inc(exp_ready, 1)
                    fn(xb[:, 5, :, :], G[:, :, u, :], ACT.Exp).then_inc(exp_ready, 1)
                    act.wait_ge(diff_ready, 5 * n + 5)
                    fn(xb[:, 6, :, :], xb[:, 6, :, :], ACT.Exp).then_inc(exp_ready, 1)
                    if u > 3:
                        head_squares(L, u - 4, u - 4)
                head_squares(L, 2, 3)
                head_squares(L, 3, 5)
                act.wait_ge(omean, L + 1)
                fn(HST[:, 2, :], HST[:, 1, :], ACT.Sqrt).then_inc(oroot, 1)
                high(last_unit + 1)
                high(last_unit + 2)
                scaled_high(("yT", L), 4, lambda k: (C_GON if k < 4 else C_HON) + L)
                high(last_unit + 3)
                for n in range(4):
                    follow(("out", L, n))

            def dense():
                first = U0[("dg", 0)]

                def step(f, half, turns, wait):
                    n = first + 3 * (f if isinstance(f, int) else 2 - half) + 2
                    act.wait_ge(gu_full[0], f + 1)
                    if wait:
                        act.wait_ge(hs_ready, f - 1)
                    fn(SG[:, half, :], psum[4 + 2 * half][:, :], ACT.Silu).then_inc(silu_ready, 1)
                    if not isinstance(f, int) or f:
                        high(n, turns)
                    else:
                        high(first + 3)
                    act.wait_ge(gu_full[1], f + 1)
                    high(n + 1 if not isinstance(f, int) or f else first + 4, turns)
                    act.wait_ge(hs_ready, f + 1)
                    if wait:
                        act.wait_ge(down_done, f - 1)
                    fn(HH[:, half, :], HS[:, half, :], ACT.Copy).then_inc(hh_ready, 1)
                    if not isinstance(f, int) or f:
                        act.wait_ge(down_done, f)
                        high(n + 2, turns)

                step(0, 0, 0, False)
                step(1, 1, 0, False)
                step(2, 0, 0, True)
                with act.Fori(1, ND // 2) as i:
                    step(2 * i + 1, 1, i, True)
                    step(2 * i + 2, 0, i, True)
                act.wait_ge(down_done, ND)
                high(first + 3 * ND + 2)

            def gather_high(j):
                for b in range(2):
                    act.wait_ge(gather_full, 2 * j + b + 1)
                    for k in range(4 * b, 4 * b + 4):
                        c = C_FFN + KD + k
                        last = fn(VH[:, k, :], psum[2 + b][:, (k % 4) * P:(k % 4 + 1) * P], ACT.Copy,
                                  scale=RC[:, c:c + 1])
                    last.then_inc(vh_ready, 1)

            def job(j):
                base, jt = NG * j, 3 * NG // RING * j

                def silu(f, half, wait):
                    act.wait_ge(e_gate, base + f + 1)
                    if wait:
                        act.wait_ge(e_hid, base + f - 1)
                    fn(SG[:, half, 0:FG], psum[4 + 2 * half][:, 0:FG], ACT.Silu).then_inc(e_silu, 1)

                def turned(f, half, wait):
                    act.wait_ge(e_ht_full, base + f + 1)
                    if wait:
                        act.wait_ge(e_down, base + f - 1)
                    fn(HH[:, half, 0:FG], psum[2 + half][:, 0:FG], ACT.Copy).then_inc(e_hh, 1)

                def step(f, half, n, turns, wait, turned_wait):
                    silu(f, half, wait)
                    turned(f - 1, 1 - half, turned_wait)
                    high(UE + n, turns)
                    act.wait_ge(e_up, base + f + 1)
                    high(UE + n + 1, turns)
                    act.wait_ge(e_down, base + f)
                    high(UE + n + 2, turns)

                act.wait_ge(pickT_full, j + 1)
                fn(PICKT[:, :], psum[2][:, 0:T], ACT.Copy).then_inc(pickT_ready, 1)
                silu(0, 0, False)
                high(UE + 3, jt)
                act.wait_ge(e_up, base + 1)
                high(UE + 4, jt)
                step(1, 1, 5, jt, False, False)
                step(2, 0, 8, jt, True, False)
                with act.Fori(1, NG // 2 - 1) as i:
                    step(2 * i + 1, 1, 5, jt + i, True, True)
                    step(2 * i + 2, 0, 8, jt + i, True, True)
                silu(NG - 1, 1, True)
                turned(NG - 2, 0, True)
                high(UE + 3 * NG - 1, jt)
                act.wait_ge(e_up, base + NG)
                high(UE + 3 * NG, jt)
                turned(NG - 1, 1, True)
                act.wait_ge(e_down, base + NG - 1)
                high(UE + 3 * NG + 1, jt)
                act.wait_ge(e_down, base + NG)
                for c in range(2):
                    fn(YH[:, c * 512:(c + 1) * 512], psum[c][:, :], ACT.Copy).then_inc(yh_ready, 1)
                gather_high(j + 1)
                high(UE + 3 * NG + 2, jt)

            def ple(L, base, turns):
                fn(PH[:, :, :], take(("pT", L), 7)[:, :].rearrange("p (a n) -> p a n", a=2),
                   ACT.Copy).then_inc(xh_ready, 1)
                scaled_high(("normT", 3 * L + 2), 3, lambda k: C_PLE + KD * L + k)
                act.wait_ge(filled, number[("pp", L, 3)][0])
                high(base + SPLIT_RING, turns)
                for n in range(4):
                    bank = take(("pg", L, n), 4 + n)
                    if n >= 2:
                        data(act, ("pp", L, n - 2))
                    fn(SG[:, n % 2, :], bank[:, :], ACT.Sigmoid).then_inc(emptied["a"], 1)
                    if L == 0 or n < 1:
                        high(base + SPLIT_RING + 1 + n, turns)

            for L in range(DEPTH):
                norm(3 * L)
                scaled_high(("normT", 3 * L), 0, lambda k: C_MIX + KD * L + k)
                mixer(L)
                norm(3 * L + 1)
                scaled_high(("normT", 3 * L + 1), 4, lambda k: C_FFN + KD * L + k)
                if L == 0:
                    dense()
                    further = 0
                else:
                    for t in range(NT):
                        act.wait_ge(rt_shift, t + 1)
                        fn(RT[:, 2, t * 8:(t + 1) * 8], RT[:, 1, t * 8:(t + 1) * 8], ACT.Exp,
                           accum_out=RT[:, 3, t:t + 1]).then_inc(rt_exp, 1)
                    gather_high(0)
                    act.wait_ge(table_ready, 1)
                    nj = NE + nc.scalar.value_load(JT[0:1, 15:16], min_val=0, max_val=NJMAX - NE)
                    with act.Fori(0, nj) as j:
                        job(j)
                    further = 3 * NG // RING * nj
                norm(3 * L + 2)
                ple(L, U0[("pp", 0)] if L == 0 else UE, further)
            norm(6)

        @block.gpsimd
        def _(pool):
            for L in range(DEPTH):
                for u in range(6):
                    n, xb = L * 6 + u, decayed(L, u)

                    def times(dst, src, other, ready):
                        pool.wait_ge(exp_ready, 10 * n + ready)
                        nc.gpsimd.tensor_tensor(dst, src, other, ALU.mult).then_inc(decayed_ready, 1)

                    for i, m in enumerate(LEVELS):
                        v = both_ways(xb, (2 + i) * 2 * T, m, 0)
                        times(v, v, both_ways(K, u * T, m, 6 * T), 3 + 2 * i)
                        v = xb[:, 2 + i, 1, :]
                        times(v, v, Q[:, u, :], 4 + 2 * i)
                    times(xb[:, 5, :, :], xb[:, 5, :, :], part_of(Q, u * T, [[0, 2], [1, T]]), 9)
                    times(xb[:, 6, :, :], xb[:, 6, :, :], K[:, :, u, :], 10)
                    pool.wait_ge(edge_ready, 4 * L + 4)
                    pool.wait_ge(decayed_ready, 10 * n + 8)
                    o5, o6, o7 = (a * 2 * T for a in (5, 6, 7))
                    ef = u * 4
                    times(part_of(xb, o7, [[T, 2], [CHUNK, 2], [1, CHUNK]]),
                          part_of(xb, o6, [[T + P, 2], [CHUNK, 2], [1, CHUNK]]),
                          part_of(EF, ef, [[24, 2], [1, 2], [0, CHUNK]]), 10)
                    times(part_of(xb, o7 + P, [[T, 2], [CHUNK, 2], [1, CHUNK]]),
                          part_of(xb, o5 + P, [[T - P, 2], [CHUNK, 2], [1, CHUNK]]),
                          part_of(EF, ef + 2, [[24, 2], [1, 2], [0, CHUNK]]), 10)

        @block.vector
        def _(dve):
            tt, ts, stt = nc.vector.tensor_tensor, nc.vector.tensor_scalar, nc.vector.scalar_tensor_tensor
            steps = [0]

            def link(ins):
                steps[0] += 1
                ins.then_inc(dve_step, 1)
                dve.wait_ge(dve_step, steps[0])

            def take(name, bank):
                dve.wait_ge(filled, number[name][0])
                return psum[bank]

            def low(n, further=0):
                dve.wait_ge(high_ready, n + 1 + further)
                s = n % SPLIT_RING
                tt(W[:, s, 1, :], ring[:, n % RING, :], W[:, s, 0, :].bitcast(F32), ALU.subtract).then_inc(split_ready, 1)

            nc.vector.memset(WG2[:, :, :, :], 0.0).then_inc(zeroed, 1)
            nc.vector.memset(ZB[:, :], 0.0)
            nc.vector.memset(JF[:, :], 0.0)
            nc.vector.memset(JC[:, :, :], 0.0)
            link(nc.vector.memset(EF[:, :, :, :], 1.0))
            for n in range(SPLIT_RING):
                low(n)
            nc.vector.tensor_copy(RC[:, :], take("rows", 7)[:, 0:NROW]).then_inc(emptied["v"], 1)
            data(dve, "rows")
            l0, l1 = RC[:, C_LB:C_LB + 8], RC[:, C_LB + 8:C_LB + 16]
            link(tt(LBX[:, 0, :], l0, l1, ALU.max))
            tt(LBX[:, 1, :], l0, LBX[:, 0, :], ALU.subtract)
            tt(LBX[:, 2, :], l1, LBX[:, 0, :], ALU.subtract).then_inc(lb_shifted, 1)
            dve.wait_ge(lb_exp, 1)
            link(tt(LBX[:, 5, :], LBX[:, 3, :], LBX[:, 4, :], ALU.add))
            link(nc.vector.reciprocal(LBX[:, 0, :], LBX[:, 5, :]))
            tt(LBX[:, 1, :], LBX[:, 3, :], LBX[:, 0, :], ALU.mult)
            link(tt(LBX[:, 2, :], LBX[:, 4, :], LBX[:, 0, :], ALU.mult))
            tt(LB[:, 0, :], LBX[:, 1, :], LBX[:, 1, :], ALU.subtract)
            link(tt(LBX[:, 5, :], LBX[:, 1, :], LBX[:, 2, :], ALU.add))
            link(tt(LB[:, 1, :], LBX[:, 5, :], LBX[:, 1, :], ALU.subtract))
            link(ts(LB[:, 2:4, :], LB[:, 0:2, :], -1.0, 1.0, ALU.mult, ALU.add))

            dve.wait_ge(router_high, 1)
            tt(WRL[:, :, :], WR[:, :, :], WRH[:, :, :].bitcast(F32), ALU.subtract).then_inc(router_ready, 1)

            def scaled_low(name, first_bank, column, high_count):
                for b in range(4):
                    dve.wait_ge(xh_ready, high_count + b + 1)
                    bank = take(name + (b,), first_bank + b)
                    for c in range(2):
                        col = column(2 * b + c)
                        last = stt(XL[:, 2 * b + c, :], bank[:, c * T:(c + 1) * T], RC[:, col:col + 1],
                                   XH[:, 2 * b + c, :].bitcast(F32), ALU.mult, ALU.subtract)
                    last.then_inc(emptied["v"], 1)

            def norm(r, col):
                dve.wait_ge(squares, 2 * r + 2)
                ts(STAT[:, 1, r, :], STAT[:, 0, r, :], 1.0 / D, EPS, ALU.mult, ALU.add).then_inc(mean_ready, 1)
                dve.wait_ge(root_ready, r + 1)
                link(nc.vector.reciprocal(STAT[:, 0, r, :], STAT[:, 2, r, :]))
                for t in range(NT):
                    last = ts(hn[:, t, :], h[:, t, :], STAT[:, 0, r, t:t + 1], None, ALU.mult)
                if col is None:
                    link(last)
                    dve.wait_ge(last_in, 16)
                    tt(hn[:, :, :], hn[:, :, :], NF[:, :].unsqueeze(1).to_broadcast([P, NT, D]),
                       ALU.mult).then_inc(h_ready, 1)
                    return
                last.then_inc(hn_ready, 1)

            def mixer(L):
                last_unit = U0[("in", L, "hv", 1)]
                g2 = G[:, :, 0:2, :].rearrange("p d u t -> p d (u t)")
                soft = hn[:, 0, :].rearrange("p (d n) -> p d n", d=2)

                def chunk_sums(units):
                    for u in units:
                        nc.vector.tensor_tensor_scan(G[:, 0, u, :], reset, G[:, 0, u, :], 0.0, ALU.mult, ALU.add)
                        back = part_of(G, (6 + u) * T + T - 1, [[-1, T]])
                        last = nc.vector.tensor_tensor_scan(back, reset, back, 0.0, ALU.mult, ALU.add)
                    return last

                def difference(u, part):
                    n, xb = L * 6 + u, decayed(L, u)
                    if part == 0:
                        if u >= 3:
                            dve.wait_ge(score_full, L * NGROUP + GROUP0[u - 2])
                        tt(part_of(xb, 0, [[T, 2], [SUB, T // SUB], [1, SUB]]),
                           part_of(G, u * T, [[6 * T, 2], [SUB, T // SUB], [1, SUB]]),
                           part_of(G, u * T + SUB // 2 - 1, [[6 * T, 2], [SUB, T // SUB], [0, SUB]]),
                           ALU.subtract).then_inc(diff_ready, 1)
                    if part < 3:
                        m = LEVELS[part]
                        for role, first, step in ((0, 0, 6 * T), (1, 6 * T, -6 * T)):
                            last = tt(both_ways(xb, (2 + part) * 2 * T + role * T, m, 0),
                                      both_ways(G, first + u * T, m, step),
                                      part_of(G, first + u * T + m - 1 + role,
                                              [[step + (1, -1)[role], 2], [2 * m, T // (2 * m)], [0, m]]),
                                      ALU.subtract)
                        last.then_inc(diff_ready, 1)
                    else:
                        tt(part_of(xb, 6 * 2 * T, [[T, 2], [CHUNK, 4], [1, CHUNK]]),
                           part_of(TOT, u * 4, [[24, 2], [1, 4], [0, CHUNK]]),
                           part_of(G, u * T, [[6 * T, 2], [CHUNK, 4], [1, CHUNK]]),
                           ALU.subtract).then_inc(diff_ready, 1)

                def diagonal(u):
                    n, xb = L * 6 + u, decayed(L, u)
                    dve.wait_ge(exp_ready, 10 * n + 2)
                    stt(xb[:, 0, :, :], xb[:, 0, :, :], SUB_SCALE, part_of(Q, u * T, [[0, 2], [1, T]]),
                        ALU.mult, ALU.mult).then_inc(diag_ready, 1)
                    stt(xb[:, 1, :, :], xb[:, 1, :, :], SUB_SCALE, K[:, :, u, :],
                        ALU.mult, ALU.mult).then_inc(diag_ready, 1)

                for part, piece, form, engine in PROJ:
                    if engine == "v":
                        bank = take((part, piece, L), PROJ_BANK[part, piece])
                        two = bank[:, :].rearrange("p (a n) -> p a n", a=2)
                    if part == "glr":
                        nc.vector.tensor_copy(GLT[:, :], bank[0:2 * RANK, 0:T]).then_inc(emptied["v"], 1)
                    elif part == "gq":
                        ts(Q[:, 0:2, :], two, float(P // 2) ** -0.5, None, ALU.mult).then_inc(emptied["v"], 1)
                    elif part == "gk":
                        nc.vector.tensor_copy(K[:, 0, 0:2, :], two)
                        nc.vector.tensor_copy(K[:, 1, 0:2, :], two).then_inc(emptied["v"], 1)
                    elif part == "z":
                        for u in range(2):
                            c = C_BG + 4 * L + 2 * piece + u
                            last = ts(G[:, piece, u, :], bank[:, u * T:(u + 1) * T], RC[:, c:c + 1], None, ALU.add)
                        last.then_inc(emptied["v"], 1)
                    elif part in ("gv", "hv"):
                        c = (0 if part == "gv" else 512) + piece * FG
                        nc.vector.tensor_copy(V[:, :, c:c + FG], two).then_inc(emptied["v"], 1)
                    if form != "decay" and U0[("in", L, part, piece)] + SPLIT_RING <= last_unit:
                        low(U0[("in", L, part, piece)] + SPLIT_RING)
                    if part == "gq":
                        data(dve, ("hq", 1, L))
                        ts(Q[:, 2:6, :], Q[:, 2:6, :], float(P) ** -0.5, None, ALU.mult)
                        data(dve, ("hfb", 1, L))
                        for d in range(2):
                            for u in range(4):
                                c = 4 * d + u
                                ts(K[:, d, 2 + u, :], K[:, d, 2 + u, :], LB[:, 2 + L, c:c + 1], None, ALU.mult)
                                last = ts(G[:, d, 2 + u, :], G[:, d, 2 + u, :], LB[:, 2 + L, c:c + 1],
                                          LB[:, L, c:c + 1], ALU.mult, ALU.add)
                        link(last)
                        ts(G[:, :, 2:6, :], G[:, :, 2:6, :], F_MIN, None, ALU.max).then_inc(forget_ready, 1)
                    if (part, piece) == ("z", 1):
                        dve.wait_ge(logf_ready, L + 1)
                        chunk_sums(range(2, 6))
                        dve.wait_ge(softplus_step, 3 * L + 3)
                        data(dve, ("z", 1, L))
                        link(stt(g2, g2, 0.0, soft, ALU.min, ALU.subtract))
                        link(ts(g2, g2, 1.0 / 16.0, LN_F_MIN, ALU.mult, ALU.max))
                        link(chunk_sums(range(2)))
                        nc.vector.tensor_copy(TOT[:, 0, :, :], G[:, 0, :, CHUNK - 1:T:CHUNK])
                        nc.vector.tensor_copy(TOT[:, 1, :, :], G[:, 1, :, 0:T:CHUNK]).then_inc(sums_ready, 1)
                        dve.wait_ge(sums_ready, L + 1)
                    if (part, piece) == ("gv", 1):
                        for i in range(4):
                            difference(0, i)
                    elif (part, piece) == ("hv", 0):
                        diagonal(0)
                        for i in range(4):
                            difference(1, i)
                def mask(g):
                    n = L * NGROUP + g
                    w = 384 if g % 2 else 512
                    dve.wait_ge(score_full, n + 1)
                    if n >= 4:
                        dve.wait_ge(av_done, n - 3)
                    tt(masked_scores(L, n)[:, 0:w], psum[4 + n % 4][:, 0:w], CST[:, O_MASK + (g % 2) * 512:][:, 0:w],
                       ALU.mult).then_inc(masked, 1)

                def add_up(g):
                    n = L * NGROUP + g
                    dve.wait_ge(masked, n + 1)
                    a = masked_scores(L, n)
                    tt(a[:, 0:256], a[:, 0:256], a[:, 256:512], ALU.add).then_inc(summed, 1)

                for u in range(6):
                    for g in range(GROUPS_OF[u]):
                        mask(GROUP0[u] + g)
                        if g % 2:
                            add_up(GROUP0[u] + g - 1)
                        if g == 1 and u < 5:
                            diagonal(u + 1)
                        if g < 4 and u < 4:
                            difference(u + 2, g)
                dve.wait_ge(osq, 16 * L + 16)
                ts(HST[:, 1, :], HST[:, 0, :], 1.0 / P, HEAD_EPS, ALU.mult, ALU.add).then_inc(omean, 1)
                dve.wait_ge(oroot, L + 1)
                link(nc.vector.reciprocal(HST[:, 0, :], HST[:, 2, :]))
                for g in range(2):
                    for t in range(NT):
                        for hd in range(4):
                            n, c = 8 * g + 4 * t + hd, 512 * g + hd * P
                            last = stt(hn[:, t, c:c + P], head_output(4 * g + hd, t),
                                       HST[:, 0, n:n + 1], SR[:, t, c:c + P], ALU.mult, ALU.mult)
                last.then_inc(y_ready, 1)
                low(last_unit + 1)
                low(last_unit + 2)
                scaled_low(("yT", L), 4, lambda k: (C_GON if k < 4 else C_HON) + L, 17 * L + 4)
                low(last_unit + 3)
                for n in range(4):
                    two = take(("mix", L, n), n)[:, :].rearrange("p (a n) -> p a n", a=2)
                    hv = h[:, :, n * FG:(n + 1) * FG]
                    tt(hv, two, hv, ALU.add).then_inc(emptied["v"], 1)
                    low(U0[("out", L, n)] + SPLIT_RING)
                data(dve, ("mix", L, 3))
                nc.vector.memset(LBX[:, 0, 0:1], 0.0).then_inc(h_ready, 1)

            def dense():
                first = U0[("dg", 0)]

                def step(f, half, further):
                    static = isinstance(f, int)
                    n = first + 3 * (f if static else 2 - half) + 2
                    if static and f == 0:
                        low(first + 3)
                    else:
                        low(n, further)
                    dve.wait_ge(silu_ready, f + 1)
                    dve.wait_ge(gu_full[1], f + 1)
                    tt(HS[:, half, :], psum[5 + 2 * half][:, :], SG[:, half, :], ALU.mult).then_inc(hs_ready, 1)
                    low(first + 4 if static and f == 0 else n + 1, further)
                    dve.wait_ge(hh_ready, f + 1)
                    tt(HL[:, half, :], HS[:, half, :], HH[:, half, :].bitcast(F32), ALU.subtract).then_inc(hidden_ready, 1)
                    if not (static and f == 0):
                        low(n + 2, further)

                step(0, 0, 0)
                step(1, 1, 0)
                step(2, 0, 0)
                with dve.Fori(1, ND // 2) as i:
                    step(2 * i + 1, 1, RING * i)
                    step(2 * i + 2, 0, RING * i)
                low(first + 3 * ND + 2)
                dve.wait_ge(down_done, ND)
                for t in range(NT):
                    for c in range(2):
                        hv = h[:, t, c * 512:(c + 1) * 512]
                        last = tt(hv, psum[2 * t + c][:, :], hv, ALU.add)
                last.then_inc(h_ready, 1)

            def route():
                lg, sh, pr = RT[:, 0, :], RT[:, 1, :], RT[:, 4, :]
                nc.vector.tensor_copy(lg, take("logits", 4)[:, 0:16]).then_inc(emptied["v"], 1)
                data(dve, "logits")
                for t in range(NT):
                    w = slice(8 * t, 8 * t + 8)
                    link(nc.vector.max(RT[:, 5, w], lg[:, w]))
                    ts(sh[:, w], lg[:, w], RT[:, 5, 8 * t:8 * t + 1], None, ALU.subtract).then_inc(rt_shift, 1)
                dve.wait_ge(rt_exp, 2)
                link(nc.vector.reciprocal(RT[:, 3, 2:4], RT[:, 3, 0:2]))
                for t in range(NT):
                    w = slice(8 * t, 8 * t + 8)
                    link(ts(pr[:, w], RT[:, 2, w], RT[:, 3, 2 + t:3 + t], None, ALU.mult))
                    link(nc.vector.max(RT[:, 6, w], pr[:, w]))
                    link(nc.vector.max_index(IDX[:, t, :], RT[:, 6, w], pr[:, w]))
                    link(nc.vector.tensor_copy(RT[:, 7, w], IDX[:, t, :]))
                    ts(RT[:, 9, w], iota8, RT[:, 7, 8 * t:8 * t + 1], None, ALU.is_equal)
                    link(ts(RT[:, 10, w], iota8, RT[:, 7, 8 * t + 1:8 * t + 2], None, ALU.is_equal))
                    link(tt(RT[:, 3, 4 + t:5 + t], RT[:, 6, 8 * t:8 * t + 1], RT[:, 6, 8 * t + 1:8 * t + 2], ALU.add))
                    link(nc.vector.reciprocal(RT[:, 3, 6 + t:7 + t], RT[:, 3, 4 + t:5 + t]))
                    link(ts(RT[:, 11, w], RT[:, 6, w], RT[:, 3, 6 + t:7 + t], None, ALU.mult))
                    link(ts(RT[:, 12, w], RT[:, 9, w], RT[:, 11, 8 * t:8 * t + 1], None, ALU.mult))
                    link(stt(RT[:, 13, w], RT[:, 10, w], RT[:, 11, 8 * t + 1:8 * t + 2], RT[:, 12, w],
                             ALU.mult, ALU.add))
                gates, picks = RT[:, 13, :], RT[:, 8, :]
                tt(picks, RT[:, 9, :], RT[:, 10, :], ALU.add).then_inc(rt_mask, 1)
                bank = take("rank", 5)
                nc.vector.tensor_copy(RT[:, 14, 0:8], bank[:, 16:24])
                link(stt(RT[:, 15, :], bank[:, 0:16], 1.0, picks, ALU.add, ALU.mult))
                nc.vector.memset(LBX[:, 0, 0:1], 0.0).then_inc(emptied["v"], 1)
                place = RT[:, 16, :]
                link(ts(place, RT[:, 15, :], -1.0, None, ALU.add))
                for t in range(NT):
                    nc.vector.tensor_copy(JC[:, 0:NE, t], place[:, 8 * t:8 * t + 8])
                    nc.vector.tensor_copy(JC[:, 0:NE, 2 + t], gates[:, 8 * t:8 * t + 8])
                over, upto, rank = RT[:, 17, 0:8], RT[:, 18, 0:8], RT[:, 19, 0:8]
                link(ts(over, RT[:, 14, 0:8], CAP + 0.5, None, ALU.is_gt))
                link(nc.vector.tensor_tensor_scan(upto, ones[:, 0:8], over, 0.0, ALU.mult, ALU.add))
                tt(rank, upto, over, ALU.subtract)
                nc.vector.tensor_copy(JF[:, 0:NE], iota8)
                link(nc.vector.tensor_copy(JF[:, 15:16], upto[:, 7:8]))
                for e in range(NJMAX - NE):
                    sel, scr = RT[:, 20, 0:8], RT[:, 21, 0:8]
                    link(stt(sel, rank, float(e), over, ALU.is_equal, ALU.mult))
                    link(stt(scr, sel, 1.0, iota8, ALU.mult, ALU.mult, accum_out=JF[:, NE + e:NE + e + 1]))
                    for t in range(NT):
                        w = slice(8 * t, 8 * t + 8)
                        link(stt(scr, sel, 1.0, place[:, w], ALU.mult, ALU.mult, accum_out=RT[:, 22, t:t + 1]))
                        link(stt(scr, sel, 1.0, gates[:, w], ALU.mult, ALU.mult, accum_out=JC[:, NE + e, 2 + t:3 + t]))
                    link(ts(JC[:, NE + e, 0:2], RT[:, 22, 0:2], -float(CAP), None, ALU.add))
                nc.vector.memset(LBX[:, 0, 0:1], 0.0).then_inc(scat_done, 4)
                nc.vector.tensor_copy(JT[:, :], JF[:, :]).then_inc(table_ready, 1)
                dve.wait_ge(table_ready, 1)

            def picks(j):
                nc.vector.tensor_copy(PLACE[:, :], JC[:, bass.ds(j, 1), 0:NT].rearrange("p a c -> p (a c)"))\
                    .then_inc(place_ready, 1)
                dve.wait_ge(place_ready, j + 1)
                for t in range(NT):
                    ts(PICK[:, t, :], iota, PLACE[:, t:t + 1], None, ALU.is_equal).then_inc(pick_ready, 1)

            def gather_low(j):
                for b in range(2):
                    dve.wait_ge(vh_ready, 2 * j + b + 1)
                    for k in range(4 * b, 4 * b + 4):
                        c = C_FFN + KD + k
                        last = stt(VL[:, k, :], psum[2 + b][:, (k % 4) * P:(k % 4 + 1) * P], RC[:, c:c + 1],
                                   VH[:, k, :].bitcast(F32), ALU.mult, ALU.subtract)
                    last.then_inc(gathered, 1)

            def job(j):
                base, further = NG * j, 3 * NG * j
                dve.wait_ge(scat_done, 4 * j + 4)
                nc.vector.tensor_copy(GATE[:, :], JC[:, bass.ds(j, 1), NT:2 * NT].rearrange("p a c -> p (a c)"))\
                    .then_inc(gate_ready, 1)

                def hidden(f, half, wait):
                    dve.wait_ge(e_silu, base + f + 1)
                    dve.wait_ge(e_up, base + f + 1)
                    if wait:
                        dve.wait_ge(e_ht_full, base + f - 1)
                    tt(HS[:, half, 0:FG], psum[5 + 2 * half][:, 0:FG], SG[:, half, 0:FG], ALU.mult).then_inc(e_hid, 1)

                def turned(f, half):
                    dve.wait_ge(e_hh, base + f + 1)
                    tt(HL[:, half, 0:FG], psum[2 + half][:, 0:FG], HH[:, half, 0:FG].bitcast(F32),
                       ALU.subtract).then_inc(e_ht, 1)

                def step(f, half, n, on, wait):
                    turned(f - 1, 1 - half)
                    low(UE + n, on)
                    hidden(f, half, wait)
                    low(UE + n + 1, on)
                    low(UE + n + 2, on)

                low(UE + 3, further)
                hidden(0, 0, False)
                low(UE + 4, further)
                step(1, 1, 5, further, False)
                step(2, 0, 8, further, True)
                with dve.Fori(1, NG // 2 - 1) as i:
                    step(2 * i + 1, 1, 5, further + RING * i, True)
                    step(2 * i + 2, 0, 8, further + RING * i, True)
                turned(NG - 2, 0)
                low(UE + 3 * NG - 1, further)
                hidden(NG - 1, 1, True)
                low(UE + 3 * NG, further)
                turned(NG - 1, 1)
                picks(j + 1)
                low(UE + 3 * NG + 1, further)
                for c in range(2):
                    cols_ = slice(c * 512, (c + 1) * 512)
                    dve.wait_ge(yh_ready, 2 * j + c + 1)
                    last = tt(YL[:, cols_], psum[c][:, :], YH[:, cols_].bitcast(F32), ALU.subtract)
                last.then_inc(ys_ready, 1)
                gather_low(j + 1)
                dve.wait_ge(gate_ready, j + 1)
                for t in range(NT):
                    for c in range(2):
                        dve.wait_ge(scat_full, 4 * j + 2 * t + c + 1)
                        hv = h[:, t, c * 512:(c + 1) * 512]
                        stt(hv, psum[4 + 2 * t + c][:, :], GATE[:, t:t + 1], hv,
                            ALU.mult, ALU.add).then_inc(scat_done, 1)
                low(UE + 3 * NG + 2, further)

            def ple(L, base, further):
                dve.wait_ge(xh_ready, 17 * L + 13)
                two = take(("pT", L), 7)[:, :].rearrange("p (a n) -> p a n", a=2)
                tt(PL[:, :, :], two, PH[:, :, :].bitcast(F32), ALU.subtract).then_inc(emptied["v"], 1)
                scaled_low(("normT", 3 * L + 2), 3, lambda k: C_PLE + KD * L + k, 17 * L + 13)
                low(base + SPLIT_RING, further)
                for n in range(4):
                    bank = take(("pp", L, n), n)
                    data(dve, ("pg", L, n))
                    tt(HS[:, n % 2, :], bank[:, :], SG[:, n % 2, :], ALU.mult).then_inc(emptied["v"], 1)
                    data(dve, ("pp", L, n))
                    hv = h[:, :, n * FG:(n + 1) * FG]
                    last = tt(hv, hv, HS[:, n % 2, :].rearrange("p (a n) -> p a n", a=2), ALU.add)
                    if n == 3:
                        last.then_inc(h_ready, 1)
                    if L == 0 or n < 1:
                        low(base + SPLIT_RING + 1 + n, further)

            for L in range(DEPTH):
                norm(3 * L, 0)
                scaled_low(("normT", 3 * L), 0, lambda k: C_MIX + KD * L + k, 17 * L)
                mixer(L)
                norm(3 * L + 1, 0)
                scaled_low(("normT", 3 * L + 1), 4, lambda k: C_FFN + KD * L + k, 17 * L + 8)
                if L == 0:
                    dense()
                    norm(2, 0)
                    ple(0, U0[("pp", 0)], 0)
                else:
                    route()
                    picks(0)
                    gather_low(0)
                    nj = NE + nc.vector.value_load(JT[0:1, 15:16], min_val=0, max_val=NJMAX - NE)
                    with dve.Fori(0, nj) as j:
                        job(j)
                    dve.wait_ge(scat_done, 4 * nj + 4)
                    nc.vector.memset(LBX[:, 0, 0:1], 0.0).then_inc(h_ready, 1)
                    norm(5, 0)
                    ple(1, UE, 3 * NG * nj)
            norm(6, None)


_INS = ["x", "p", "w_in", "gla_wg2", "gla_bg", "hg_lb_logits", "gla_onorm", "hg_onorm", "w_out", "norm_mix",
        "norm_ffn", "w_dense_gate", "w_dense_up", "w_dense_down", "w_router", "w_exp_gate", "w_exp_up",
        "w_exp_down", "w_ple_proj", "w_ple_gate", "norm_ple", "norm_final"]
_OUTS = [((1, T, D), "float32")]


def kernel(**inputs):
    import numpy as _np
    import concourse.bacc as _bacc
    from concourse import mybir as _mybir
    from concourse.bass_utils import run_bass_kernel_spmd as _run

    nc = _bacc.Bacc("TRN2", target_bir_lowering=False, num_devices=1)
    arrays, args = {}, []
    for name in _INS + ["consts"]:
        a = shape_constants(_np) if name == "consts" else _np.ascontiguousarray(inputs[name])
        arrays[f"in_{name}_dram"] = a
        args.append(nc.dram_tensor(f"in_{name}_dram", a.shape, _mybir.dt.from_np(a.dtype), kind="ExternalInput").ap())
    for i, (shape, dtype) in enumerate(_OUTS):
        dt = _mybir.dt.from_np(_np.dtype(dtype))
        args.append(nc.dram_tensor(f"out_{i}_dram", shape, dt, kind="ExternalOutput").ap())
    trunk_kernel(nc, *args)
    r = _run(nc, [arrays], core_ids=[0])
    got = tuple(r.results[0][f"out_{i}_dram"] for i in range(len(_OUTS)))
    return got[0]
```

```python
from contextlib import ExitStack

import concourse.bass as bass
import numpy as np
from concourse import mybir

F32 = mybir.dt.float32
BF16 = mybir.dt.bfloat16
F32R = mybir.dt.float32r
I32 = mybir.dt.int32
U32 = mybir.dt.uint32
ACT = mybir.ActivationFunctionType
ALU = mybir.AluOpType

P = 128
D = 1024
T = 256
NT = T // P
KD = D // P
DEPTH = 2
EPS, HEAD_EPS, F_MIN = 1e-6, 1e-5, 1e-6
LN_F_MIN = -13.815510557964274
CHUNK = 64
RANK = 16
FF_DENSE, FF_EXPERT, NE, PLE = 2816, 3584, 8, 256
CAP = 128
NJMAX = NE + 3
FG = 256
RING = 6
SLOT = 2048
SPLIT_RING = 3
SUB = 8
SUB_SCALE = 2.0 ** -14
LEVELS = (8, 16, 32)

SPLIT = dict(gq=0, gk=256, gv=512, gr=1024, glr=1536, hq=1568, hff=2080, hfb=2592, hv=3104, hr=3616)
PROJ = [("gr", 0, "tok", "a"), ("gr", 1, "tok", "a"), ("hr", 0, "tok", "a"), ("hr", 1, "tok", "a"),
        ("hq", 0, "col", "a"), ("hq", 1, "col", "a"), ("hff", 0, "col", "a"), ("hff", 1, "col", "a"),
        ("hfb", 0, "col", "a"), ("hfb", 1, "col", "a"), ("glr", 0, "low", "v"), ("gq", 0, "col", "v"),
        ("gk", 0, "col", "v"), ("z", 0, "decay", "v"), ("z", 1, "decay", "v"), ("gv", 0, "tok", "v"),
        ("gv", 1, "tok", "a"), ("hv", 0, "tok", "a"), ("hv", 1, "tok", "v")]
PROJ_BANK = {(s[0], s[1]): (4 + n) % 8 for n, s in enumerate(PROJ)}

C_MIX, C_FFN, C_PLE, C_BG, C_LB, C_GON, C_HON, NROW = 0, 16, 32, 48, 56, 72, 74, 76

O_MASK = 0
O_ID = O_MASK + 7 * P
O_IOTA = O_ID + P
O_TRI = O_IOTA + P
O_ONE = O_TRI + P
O_RST = O_ONE + P
NCONST = O_RST + T

HEADS = [[(u, 64 * hh, 64, 2 * u + hh) for hh in range(2)] for u in range(2)] + \
        [[(u, 0, P, 4 + u - 2)] for u in range(2, 6)]
PAIRS = [[(hd, t) for hd in heads for t in range(NT)] for heads in HEADS]
SCORES = [[(hd, t, i) for i in range(2) for hd, t in PAIRS[0]]] + \
         [[(hd, t, i) for hd, t in p for i in range(2)] for p in PAIRS[1:]]
GROUPS_OF = [len(p) for p in SCORES]
NGROUP = sum(GROUPS_OF)
PART_OF = [i for unit in SCORES for _, _, i in unit]
assert len(PAIRS[0]) == 4
TAKEN = [{0: (), 1: (), 2: (), 3: (0,), 4: (), 5: (4, 1), 6: (5, 2), 7: (6, 3), 8: ()}.get(g, (g - 2,))
         for g in range(NGROUP)] + [(NGROUP - 2, NGROUP - 1)]
TAKEN_AT = {g: n + 1 for n, g in enumerate(g for turn in TAKEN for g in turn)}
SUMS = [PART_OF[:g + 1].count(0) for g in range(NGROUP)]
GROUP0 = [sum(GROUPS_OF[:u]) for u in range(6)]


def shape_constants(np):
    c = np.zeros((P, NCONST), np.float32)
    s, t = np.arange(P)[:, None], np.arange(P)[None, :]
    same = lambda n: (s // n) == (t // n)
    masks = [same(SUB) * (s <= t) / SUB_SCALE ** 2, same(SUB) * (s >= t) / SUB_SCALE ** 2]
    for m in LEVELS + (CHUNK,):
        masks.append(same(2 * m) * ((s // m) != (t // m)))
    for n, m in enumerate(masks + [np.ones((P, P))]):
        c[:, O_MASK + n * P:O_MASK + (n + 1) * P] = m
    c[:, O_ID:O_ID + P] = np.eye(P)
    c[:, O_IOTA:O_IOTA + P] = t
    c[:, O_TRI:O_TRI + P] = s < t
    c[:, O_ONE:O_ONE + P] = 1.0
    c[:, O_RST:O_RST + T] = (np.arange(T) % CHUNK != 0)[None, :]
    return c


def product_order():
    order = [("rows", "v")]
    for L in range(DEPTH):
        order += [(("normT", 3 * L, b), "v") for b in range(4)]
        if L == 0:
            order += [(("pT", layer), "v") for layer in range(DEPTH)]
        order += [((part, piece, L), engine) for part, piece, _, engine in PROJ]
        order += [(("yT", L, b), "v") for b in range(4)]
        order += [(("mix", L, n), "v") for n in range(4)]
        order += [(("normT", 3 * L + 1, b), "v") for b in range(4)]
        if L == 1:
            order += [("logitsT", "v"), ("logits", "v"), ("rank", "v")]
        order += [(("pp", L, n), "v") for n in range(4)]
        order += [(("normT", 3 * L + 2, b), "v") for b in range(4)]
        order += [(("pg", L, n), "a") for n in range(4)]
    return order


def taking_order():
    order = product_order()
    for L in range(DEPTH):
        pp = [x for x in order if x[0][0] == "pp" and x[0][1] == L]
        order = [x for x in order if x not in pp]
        at = order.index((("pg", L, 0), "a"))
        order[at:at] = pp
    return order


def numbered(order, taking):
    taken, place = {"a": 0, "v": 0}, {}
    for name, engine in taking:
        taken[engine] += 1
        place[name] = taken[engine]
    return {name: (n + 1, engine, place[name]) for n, (name, engine) in enumerate(order)}


HIGH_ORDER = [("normT", 0, 4), ("pT", 0, 1), ("pT", 1, 1), ("yT", 0, 4), ("normT", 1, 4), ("normT", 2, 4),
              ("normT", 3, 4), ("yT", 1, 4), ("normT", 4, 4), ("normT", 5, 4)]
HIGH_BEFORE = {x[:2]: sum(y[2] for y in HIGH_ORDER[:i]) for i, x in enumerate(HIGH_ORDER)}

FIRST_PART = [D // 2, 3 * FG, D // 2, 3 * FG, 3 * FG, D // 2, 3 * FG]


def trunk_kernel(nc, x, p, w_in, gla_wg2, gla_bg, hg_lb_logits, gla_onorm, hg_onorm, w_out, norm_mix,
                 norm_ffn, w_dense_gate, w_dense_up, w_dense_down, w_router, w_exp_gate, w_exp_up,
                 w_exp_down, w_ple_proj, w_ple_gate, norm_ple, norm_final, consts, out):
    ctx = ExitStack()
    with ctx:
        def sb(name, shape, dt=F32):
            return ctx.enter_context(nc.sbuf_tensor(name, shape, dt))

        def sem(name):
            return ctx.enter_context(nc.semaphore(name))

        def shared(*sets):
            places = []
            for tiles in sets:
                with ExitStack() as scope:
                    places.append([scope.enter_context(nc.sbuf_tensor(name, shape, dt)) for name, shape, dt in tiles])
            size = max(sum(4 * int(np.prod(shape[1:])) for _, shape, _ in tiles) for tiles in sets)
            ctx.enter_context(nc.sbuf_tensor("place_of_" + sets[0][0][0], [P, size // 4], F32))
            return places

        ring = sb("ring", [P, RING, SLOT])
        h = sb("h", [P, NT, D])
        hn = sb("hn", [P, NT, D])
        (XH, XL), (X2,), (NH, NL) = shared([("XH", [P, KD, T], F32R), ("XL", [P, KD, T], F32R)],
                                           [("X2", [P, 8, 2, T], F32)],
                                           [("NH", [P, NT, D], F32R), ("NL", [P, NT, D], F32R)])
        (W,), (X,) = shared([("W", [P, SPLIT_RING, 2, SLOT], F32R)], [("X", [P, SPLIT_RING, 8, 2, T], F32)])
        assert 8 * 2 * T == 2 * SLOT
        (V, SR, Q, K, G), (SG, HS, HH, HL, VH, VL, YH, YL, PICK, PICKT) = shared(
            [("V", [P, NT, D], F32), ("SR", [P, NT, D], F32), ("Q", [P, 6, T], F32), ("K", [P, 2, 6, T], F32),
             ("G", [P, 2, 6, T], F32)],
            [("SG", [P, 2, 512], F32), ("HS", [P, 2, 512], F32), ("HH", [P, 2, 512], F32R),
             ("HL", [P, 2, 512], F32R), ("VH", [P, KD, CAP], F32R), ("VL", [P, KD, CAP], F32R),
             ("YH", [P, D], F32R), ("YL", [P, D], F32R), ("PICK", [P, NT, CAP], F32R), ("PICKT", [P, T], F32R)])
        NF = G[:, 0, 0:4, :].rearrange("p a b -> p (a b)")
        CST = sb("CST", [P, NCONST])
        RV = sb("RV", [NROW, P])
        RC = sb("RC", [P, NROW])
        LB = sb("LB", [P, 4, 8])
        LBX = sb("LBX", [P, 6, 8])
        TOT = sb("TOT", [P, 2, 6, 4])
        EF = sb("EF", [P, 2, 6, 4])
        WG2 = sb("WG2", [2 * RANK, DEPTH, 2, T])
        GLT = sb("GLT", [2 * RANK, T])
        PIN = sb("PIN", [P, DEPTH, NT, PLE])
        PH = sb("PH", [P, DEPTH, 2, T], F32R)
        PL = sb("PL", [P, DEPTH, 2, T], F32R)
        WR = sb("WR", [P, KD, NE])
        WRH = sb("WRH", [P, KD, NE], F32R)
        WRL = sb("WRL", [P, KD, NE], F32R)
        STAT = sb("STAT", [P, 5, 7, NT])
        SCALE = sb("SCALE", [P, NT, P])
        WARM = sb("WARM", [P, 2])
        HST = sb("HST", [P, 4, 16])
        ZB = sb("ZB", [1, 512], BF16)
        RT = sb("RT", [P, 24, 16])
        IDX = sb("IDX", [P, NT, 8], U32)
        JC = sb("JC", [P, NJMAX + 1, 4])
        JF = sb("JF", [P, 16])
        JT = sb("JT", [P, 16], I32)
        PLACE = sb("PLACE", [P, NT])
        GATE = sb("GATE", [P, NT])

        psum = [ctx.enter_context(nc.psum_tensor(f"bank{i}", [P, 512], F32)) for i in range(8)]

        ident = CST[:, O_ID:O_ID + P]
        iota = CST[:, O_IOTA:O_IOTA + P]
        iota8 = CST[:, O_IOTA:O_IOTA + NE]
        tri = CST[:, O_TRI:O_TRI + P]
        ones = CST[:, O_ONE:O_ONE + P]
        one_col = CST[:, O_ONE:O_ONE + 1]
        reset = CST[:, O_RST:O_RST + T]

        x_in = sem("x_in")
        small_in = sem("small_in")
        p_in = sem("p_in")
        masks_in = sem("masks_in")
        wg2_in = sem("wg2_in")
        last_in = sem("last_in")
        high_ready = sem("high_ready")
        split_ready = sem("split_ready")
        xh_ready = sem("xh_ready")
        router_high = sem("router_high")
        router_ready = sem("router_split")
        hh_ready = sem("hidden_high")
        slot_full = [sem(f"slot_full{i}") for i in range(RING)]
        filled = sem("filled")
        emptied = {"a": sem("emptied_by_scalar"), "v": sem("emptied_by_vector")}
        dve_step = sem("dve_step")
        zeroed = sem("zeroed")
        lb_shifted = sem("lb_shifted")
        lb_exp = sem("lb_exp")
        squares = sem("squares")
        rest_ready = sem("rest_of_mean_ready")
        root_ready = sem("root_ready")
        scale_ready = sem("scale_ready")
        nh_ready = sem("normalised_high")
        hn_ready = sem("normalised_split")
        h_first = sem("h_first_part")
        h_ready = sem("h_ready")
        out_ready = sem("out_ready")
        forget_ready = sem("forget_ready")
        logf_ready = sem("logf_ready")
        softplus_step = sem("softplus_step")
        sums_ready = sem("sums_ready")
        edge_ready = sem("edge_ready")
        diff_ready = sem("diff_ready")
        exp_ready = sem("exp_ready")
        diag_ready = sem("diag_ready")
        decayed_ready = sem("decayed_ready")
        score_full = sem("score_full")
        masked = sem("masked")
        summed = sem("summed")
        av_done = sem("av_done")
        osq = sem("head_squares")
        omean = sem("head_mean")
        oroot = sem("head_root")
        y_ready = sem("y_ready")
        gu_full = [sem("gate_full"), sem("up_full")]
        silu_ready = sem("silu_ready")
        hs_ready = sem("hidden_rows")
        hidden_ready = sem("hidden_ready")
        down_done = sem("down_done")
        rt_shift = sem("router_shifted")
        rt_exp = sem("router_exp")
        rt_mask = sem("router_mask")
        table_ready = sem("table_ready")
        place_ready = sem("place_ready")
        pick_ready = sem("pick_ready")
        gather_full = sem("gather_full")
        vh_ready = sem("gathered_high")
        gathered = sem("gathered")
        gate_ready = sem("gate_ready")
        pickT_full = sem("pickT_full")
        pickT_ready = sem("pickT_ready")
        e_gate = sem("exp_gate_full")
        e_up = sem("exp_up_full")
        e_silu = sem("exp_silu")
        e_hid = sem("exp_hidden")
        e_ht_full = sem("exp_hiddenT_full")
        e_hh = sem("exp_hiddenT_high")
        e_ht = sem("exp_hiddenT")
        e_down = sem("exp_down_done")
        yh_ready = sem("exp_y_high")
        ys_ready = sem("exp_y_split")
        scat_full = sem("scatter_full")
        scat_done = sem("scatter_done")
        out_done = sem("out_done")

        number = numbered(product_order(), taking_order())
        ND = FF_DENSE // FG
        NG = FF_EXPERT // FG
        assert ND % 2 == 1 and NG % 2 == 0 and (3 * NG) % RING == 0
        UNITS = []
        for L in range(DEPTH):
            UNITS += [("in", L, part, piece) for part, piece, form, _ in PROJ if form != "decay"]
            UNITS += [("out", L, n) for n in range(4)]
            if L == 0:
                UNITS += [("dg", 0), ("du", 0)]
                for f in range(1, ND):
                    UNITS += [("dg", f), ("du", f), ("dd", f - 1)]
                UNITS += [("dd", ND - 1), ("pp", L)] + [("pg", L, n) for n in range(4)]
        U0 = {u: n for n, u in enumerate(UNITS)}
        UE = len(UNITS)
        TAIL = [("pp", 1)] + [("pg", 1, n) for n in range(4)]
        NSMALL = 9

        def col_view(w):
            return w.rearrange("(k p) n -> p k n", p=P)

        def cols(s):
            return [W[:, s, i, :].rearrange("p (k n) -> p k n", k=KD) for i in range(2)]

        def rows(s):
            return [W[:, s, i, :].rearrange("p (k n) -> p k n", k=2) for i in range(2)]

        def decayed(L, u):
            last = U0[("in", L, "hv", 1)]
            return X2[:, :, :, :] if u % 3 == 2 else X[:, (last - 2 + u % 3) % SPLIT_RING, :, :, :]

        def masked_scores(L, n):
            slot = U0[("in", L, "hv", 1)] % SPLIT_RING
            return X[:, slot, 0:4, :, :].rearrange("p a d t -> p a (d t)")[:, n % 4, :]

        def head_output(head, t):
            c = 2 * t + head % 2
            return psum[head // 2][:, c * P:(c + 1) * P]

        def part_of(t, offset, dims):
            a = t[(slice(None),) * len(t.shape)]
            return bass.AP(a.tensor, a.offset + offset, [a.ap[0]] + [[s, n] for s, n in dims])

        block = ctx.enter_context(nc.Block())

        @block.sync
        def _(sp):
            sp.dma_start(h[:, :, :], x[0].rearrange("(t p) d -> p t d", p=P)).then_inc(x_in, 16)
            small = [
                (CST[:, O_ID:], consts[:, O_ID:]),
                (RV[C_MIX:C_MIX + 16, :], norm_mix.rearrange("l (k p) -> (l k) p", p=P)),
                (RV[C_FFN:C_FFN + 16, :], norm_ffn.rearrange("l (k p) -> (l k) p", p=P)),
                (RV[C_PLE:C_PLE + 16, :], norm_ple.rearrange("l (k p) -> (l k) p", p=P)),
                (RV[C_BG:C_BG + 8, :], gla_bg.rearrange("l d (u p) -> (l d u) p", p=P)),
                (RV[C_LB:C_LB + 16, :], hg_lb_logits.rearrange("l d (u p) -> (l d u) p", p=P)),
                (RV[C_GON:C_GON + 2, :], gla_onorm),
                (RV[C_HON:C_HON + 2, :], hg_onorm),
                (WR[:, :, :], w_router[0].rearrange("(k p) e -> p k e", p=P)),
            ]
            for dst, src in small:
                sp.dma_start(dst, src).then_inc(small_in, 16)

            def load(n, src, further=0):
                if not isinstance(further, int) or n + further >= RING:
                    sp.wait_ge(split_ready, further + n - RING + 1)
                dst = ring[:, n % RING, :].rearrange("p (k n) -> p k n", k=src.shape[1])
                sp.dma_start(dst, src).then_inc(slot_full[n % RING], 16)

            def source(u):
                if u[0] == "in":
                    c = SPLIT[u[2]] + u[3] * FG
                    return col_view(w_in[u[1]])[:, :, c:c + FG]
                if u[0] == "out":
                    return col_view(w_out[u[1]])[:, :, u[2] * FG:(u[2] + 1) * FG]
                if u[0] in ("dg", "du"):
                    w = w_dense_gate if u[0] == "dg" else w_dense_up
                    return col_view(w[0])[:, :, u[1] * FG:(u[1] + 1) * FG]
                if u[0] == "dd":
                    return w_dense_down[0, u[1] * FG:(u[1] + 1) * FG, :].rearrange("(k p) n -> p k n", p=P)
                if u[0] == "pp":
                    return w_ple_proj[u[1]].rearrange("(k p) n -> p k n", p=P)
                return col_view(w_ple_gate[u[1]])[:, :, u[2] * FG:(u[2] + 1) * FG]

            for n, u in enumerate(UNITS):
                load(n, source(u))
                if n == 0:
                    for L in range(DEPTH):
                        sp.dma_start(PIN[:, L, :, :], p[L, 0].rearrange("(t p) d -> p t d", p=P)).then_inc(p_in, 16)
                if n == RING - 1:
                    sp.dma_start(CST[:, 0:O_ID], consts[:, 0:O_ID]).then_inc(masks_in, 16)
                    sp.wait_ge(zeroed, 1)
                    for L in range(DEPTH):
                        for d in range(2):
                            sp.dma_start(WG2[RANK * d:RANK * (d + 1), L, d, :], gla_wg2[L, d]).then_inc(wg2_in, 16)

            gate_v = w_exp_gate[0].rearrange("e (k p) f -> p e k f", p=P)
            up_v = w_exp_up[0].rearrange("e (k p) f -> p e k f", p=P)
            down_v = w_exp_down[0].rearrange("e (g k p) n -> p e g k n", p=P, k=2)

            def job_loads(e, j):
                def gate(f, n, i):
                    load(UE + n, gate_v[:, bass.ds(e, 1), :, bass.ds(f * FG, FG)].rearrange("p e k f -> p (e k) f"),
                         3 * NG * j + RING * i)

                def up(f, n, i):
                    load(UE + n, up_v[:, bass.ds(e, 1), :, bass.ds(f * FG, FG)].rearrange("p e k f -> p (e k) f"),
                         3 * NG * j + RING * i)

                def down(f, n, i):
                    load(UE + n, down_v[:, bass.ds(e, 1), bass.ds(f, 1), :, :].rearrange("p e g k n -> p (e g k) n"),
                         3 * NG * j + RING * i)

                gate(0, 0, 0)
                up(0, 1, 0)
                with sp.Fori(0, NG // 2 - 1) as i:
                    for c in range(2):
                        f = 2 * i + 1 + c
                        gate(f, 2 + 3 * c, i)
                        up(f, 3 + 3 * c, i)
                        down(f - 1, 4 + 3 * c, i)
                gate(NG - 1, 3 * NG - 4, 0)
                up(NG - 1, 3 * NG - 3, 0)
                down(NG - 2, 3 * NG - 2, 0)
                down(NG - 1, 3 * NG - 1, 0)

            job_loads(0, 0)
            sp.wait_ge(table_ready, 1)
            nj = NE + nc.sync.value_load(JT[0:1, 15:16], min_val=0, max_val=NJMAX - NE)
            with sp.Fori(1, nj) as j:
                job_loads(nc.sync.value_load(JT[0:1, bass.ds(j, 1)], min_val=0, max_val=NE - 1), j)
            for n, u in enumerate(TAIL):
                load(UE + n, source(u), 3 * NG * nj)
            sp.dma_start(NF, norm_final.rearrange("(a d) -> a d", a=1).to_broadcast([P, D])).then_inc(last_in, 16)
            for t in range(NT):
                sp.wait_ge(out_ready, t + 1)
                sp.dma_start(out[0, t * P:(t + 1) * P, :], hn[:, t, :]).then_inc(out_done, 16)
            sp.wait_ge(out_done, 16 * NT)

        def used(eng, u):
            if u[0] in ("dg", "du"):
                eng.wait_ge(gu_full[u[0] == "du"], u[1] + 1)
            elif u[0] == "dd":
                eng.wait_ge(down_done, u[1] + 1)
            else:
                name = {"in": lambda: (u[2], u[3], u[1]), "out": lambda: ("mix", u[1], u[2]),
                        "pp": lambda: ("pp", u[1], 3), "pg": lambda: ("pg", u[1], u[2])}[u[0]]()
                eng.wait_ge(filled, number[name][0])

        def data(eng, name):
            _, engine, n = number[name]
            eng.wait_ge(emptied[engine], n)

        @block.tensor
        def _(pe):
            mm = nc.tensor.matmul

            def split(n, further=0):
                pe.wait_ge(split_ready, n + 1 + further)
                return n % SPLIT_RING

            def three(out, left, right, start, stop):
                mm(out, left[0], right[0], start=start, stop=False, skip_group_check=True)
                mm(out, left[0], right[1], start=False, stop=False, skip_group_check=True)
                return mm(out, left[1], right[0], start=False, stop=stop, skip_group_check=True)

            def parts(pair, *at):
                return [x[at] for x in pair]

            ALL = slice(None)
            def transposes(bank, src):
                for kk in range(2):
                    for t in range(NT):
                        last = nc.tensor.transpose(bank[:, kk * T + t * P:kk * T + (t + 1) * P], src(kk, t), ident)
                last.then_inc(filled, 1)

            def turn_norm(r, first_bank, before=None):
                pe.wait_ge(scale_ready, r + 1)
                for b in range(4):
                    if before is not None:
                        data(pe, before[b])
                    for kk in range(2):
                        k = 2 * b + kk
                        for t in range(NT):
                            last = mm(psum[first_bank + b][:, kk * T + t * P:kk * T + (t + 1) * P],
                                      h[:, t, k * P:(k + 1) * P], SCALE[:, t, :], start=True, stop=True)
                    last.then_inc(filled, 1)

            def columns(bank, w, count=2, arrival=None):
                for c in range(count):
                    for k in range(KD):
                        if arrival is not None and c == 0 and k % 2 == 0:
                            data(pe, arrival + (k // 2,))
                        last = three(bank[:, c * T:(c + 1) * T], parts(w, ALL, k, slice(c * P, (c + 1) * P)),
                                     [XH[:, k, :], XL[:, k, :]], k == 0, k == KD - 1)
                return last

            def tokens(bank, w, act, kt=KD, at=slice(0, FG), arrival=None):
                for t in range(NT):
                    for k in range(kt):
                        if arrival is not None and t == 0 and k % 2 == 0:
                            data(pe, arrival + (k // 2,))
                        last = three(bank[:, t * FG:(t + 1) * FG], parts(act, ALL, k, slice(t * P, (t + 1) * P)),
                                     parts(w, ALL, k, at), k == 0, k == kt - 1)
                return last

            pe.wait_ge(small_in, 16 * NSMALL)
            nc.tensor.transpose(psum[7][:, 0:NROW], RV[:, :], ident[0:NROW, 0:NROW]).then_inc(filled, 1)

            def project(L):
                turn_norm(3 * L, 0, [("pg", 0, b) for b in range(4)] if L else None)
                if L == 0:
                    pe.wait_ge(p_in, 16 * DEPTH)
                    for layer in range(DEPTH):
                        transposes(psum[5 + layer], lambda kk, t: PIN[:, layer, t, kk * P:(kk + 1) * P])
                held = [("pp", 0, b) for b in range(4)] if L else [None, ("pT", 0), ("pT", 1), "rows"]
                held += [("normT", 3 * L, b) for b in range(4)]
                for i, (part, piece, form, _) in enumerate(PROJ):
                    before = held[i] if i < 8 else PROJ[i - 8][:2] + (L,)
                    if before is not None:
                        data(pe, before)
                    bank = psum[PROJ_BANK[part, piece]]
                    if form == "low":
                        last = columns(bank, cols(split(U0[("in", L, part, piece)])), 1)
                    elif form == "decay":
                        data(pe, ("glr", 0, L))
                        pe.wait_ge(wg2_in, 16 * 2 * DEPTH)
                        for u in range(2):
                            last = mm(bank[:, u * T:(u + 1) * T], WG2[:, L, piece, u * P:(u + 1) * P], GLT[:, :],
                                      start=True, stop=True)
                    else:
                        w = cols(split(U0[("in", L, part, piece)]))
                        arrival = ("normT", 3 * L) if i == 0 else None
                        last = columns(bank, w) if form == "col" else tokens(bank, w, (XH, XL), arrival=arrival)
                    last.then_inc(filled, 1)

            def scan(L):
                data(pe, ("hv", 0, L))
                data(pe, ("hv", 1, L))

                def scores(g, ins):
                    n = L * NGROUP + g
                    if n >= 4:
                        pe.wait_ge(masked, n - 3)
                    for c, (k_ap, q_ap) in enumerate(ins):
                        last = mm(psum[4 + n % 4][:, c * P:(c + 1) * P], k_ap, q_ap, start=True, stop=True)
                    last.then_inc(score_full, 1)

                def weighted(g):
                    (_, _, _, head), t, part = [x for unit in SCORES for x in unit][g]
                    n = L * NGROUP + g
                    if part:
                        pe.wait_ge(masked, n + 1)
                    else:
                        pe.wait_ge(summed, L * SUMS[-1] + SUMS[g])
                    sources = [[t, t], [t, t, 1 - t]][part]
                    o = head_output(head, t)
                    for c, s in enumerate(sources):
                        last = mm(o, masked_scores(L, n)[:, c * P:(c + 1) * P], V[:, s, head * P:(head + 1) * P],
                                  start=(part == 0 and c == 0), stop=(part == 1 and c == 2),
                                  skip_group_check=True)
                    last.then_inc(av_done, 1)

                g = 0
                for u in range(6):
                    xb, n = decayed(L, u), L * 6 + u
                    pe.wait_ge(diag_ready, 2 * n + 2)
                    pe.wait_ge(decayed_ready, 10 * n + 4)
                    for (_, p0, kd, head), t, i in SCORES[u]:
                        dims, at = slice(p0, p0 + kd), slice(t * P, (t + 1) * P)

                        cross = 1 - t
                        groups = [[(xb[dims, 1, d, at], xb[dims, 0, d, at]) for d in range(2)] +
                                  [(xb[dims, s, 0, at], xb[dims, s, 1, at]) for s in (2, 3)],
                                  [(xb[dims, 4, 0, at], xb[dims, 4, 1, at]),
                                   (xb[dims, 6, 0, at], xb[dims, 5, 1, at]),
                                   (xb[dims, 7, cross, 0:P], xb[dims, 7, cross, P:2 * P])]]
                        if i == 1:
                            pe.wait_ge(decayed_ready, 10 * n + 10)
                        scores(g, groups[i])
                        for taken in TAKEN[g]:
                            weighted(taken)
                        g += 1
                for taken in TAKEN[NGROUP]:
                    weighted(taken)

            def mix_out(L):
                for b in range(4):
                    pe.wait_ge(y_ready, 3 * L + max(b, 1))
                    transposes(psum[4 + b], lambda kk, t: hn[:, t, (2 * b + kk) * P:(2 * b + kk + 1) * P])
                for n in range(4):
                    tokens(psum[n], cols(split(U0[("out", L, n)])), (XH, XL),
                           arrival=("yT", L) if n == 0 else None).then_inc(filled, 1)

            def dense():
                for n in range(4):
                    data(pe, ("mix", 0, n))
                for b in range(4):
                    mm(psum[b][:, :], ZB[0:1, 0:P], ZB[0:1, :], start=True, stop=False, skip_group_check=True)
                first = U0[("dg", 0)]

                def gate_up(half, n, further, free, arrival=None):
                    for c in range(2):
                        if free is not None:
                            pe.wait_ge((silu_ready, hs_ready)[c], free)
                        columns(psum[4 + c + 2 * half], cols(split(n + c, further)),
                                arrival=arrival if c == 0 else None).then_inc(gu_full[c], 1)

                def down(half, n, further, ready, final=False):
                    pe.wait_ge(hidden_ready, ready)
                    w = rows(split(n, further))
                    for k in range(2):
                        for t in range(NT):
                            for c in range(2):
                                last = three(psum[2 * t + c][:, :],
                                             parts((HH, HL), ALL, half, slice(k * T + t * P, k * T + (t + 1) * P)),
                                             parts(w, ALL, k, slice(c * 512, (c + 1) * 512)), False, final and k == 1)
                    last.then_inc(down_done, 1)

                gate_up(0, first, 0, None, ("normT", 1))
                gate_up(1, first + 2, 0, None)
                down(0, first + 4, 0, 1)
                gate_up(0, first + 5, 0, 1)
                down(1, first + 7, 0, 2)
                with pe.Fori(1, ND // 2) as i:
                    gate_up(1, first + 2, RING * i, 2 * i)
                    down(0, first + 4, RING * i, 2 * i + 1)
                    gate_up(0, first + 5, RING * i, 2 * i + 1)
                    down(1, first + 7, RING * i, 2 * i + 2)
                down(0, first + 3 * ND - 1, 0, ND, final=True)

            def route():
                for k in range(KD):
                    if k % 2 == 0:
                        data(pe, ("normT", 4, k // 2))
                    if k == 0:
                        pe.wait_ge(router_ready, 1)
                    last = three(psum[4][0:NE, 0:T], parts((WRH, WRL), ALL, k), [XH[:, k, :], XL[:, k, :]],
                                 k == 0, k == KD - 1)
                last.then_inc(filled, 1)
                data(pe, "logitsT")
                for t in range(NT):
                    last = nc.tensor.transpose(psum[4][:, t * NE:(t + 1) * NE], GLT[0:NE, t * P:(t + 1) * P],
                                               ident[0:NE, 0:NE])
                last.then_inc(filled, 1)
                bank = psum[5]
                pe.wait_ge(rt_mask, 1)
                m = RT[:, 8, :]
                mm(bank[:, 0:8], tri, m[:, 0:8], start=True, stop=True)
                mm(bank[:, 8:16], ones, m[:, 0:8], start=True, stop=False)
                mm(bank[:, 8:16], tri, m[:, 8:16], start=False, stop=True)
                mm(bank[:, 16:24], ones, m[:, 0:8], start=True, stop=False)
                mm(bank[:, 16:24], ones, m[:, 8:16], start=False, stop=True).then_inc(filled, 1)

            def gather(j):
                pe.wait_ge(hn_ready, 2)
                pe.wait_ge(pick_ready, 2 * j + 2)
                for k in range(KD):
                    for t in range(NT):
                        for part in (NH, NL):
                            last = mm(psum[2 + k // 4][:, (k % 4) * P:(k % 4 + 1) * P],
                                      part[:, t, k * P:(k + 1) * P], PICK[:, t, :],
                                      start=(t == 0 and part is NH), stop=(t == NT - 1 and part is NL))
                    if k % 4 == 3:
                        last.then_inc(gather_full, 1)

            def job(j):
                base = NG * j
                further = 3 * NG * j
                pe.wait_ge(gathered, 2 * j + 1)
                for t in range(NT):
                    last = nc.tensor.transpose(psum[2][:, t * P:(t + 1) * P], PICK[:, t, :].bitcast(F32), ident)
                last.then_inc(pickT_full, 1)

                def gate_or_up(f, half, which, n, on, wait, gathering=False):
                    if wait:
                        pe.wait_ge((e_silu, e_hid)[which], base + f - 1)
                    w = cols(split(n, on))
                    for k in range(KD):
                        if gathering and k == KD // 2:
                            pe.wait_ge(gathered, 2 * j + 2)
                        last = three(psum[4 + 2 * half + which][:, 0:FG], parts((VH, VL), ALL, k), parts(w, ALL, k),
                                     k == 0, k == KD - 1)
                    last.then_inc((e_gate, e_up)[which], 1)

                def turn(f, half, wait):
                    pe.wait_ge(e_hid, base + f + 1)
                    if wait:
                        pe.wait_ge(e_ht, base + f - 1)
                    for k in range(2):
                        last = nc.tensor.transpose(psum[2 + half][:, k * P:(k + 1) * P],
                                                   HS[:, half, k * P:(k + 1) * P], ident)
                    last.then_inc(e_ht_full, 1)

                def down(f, half, n, on, first=False, final=False):
                    pe.wait_ge(e_ht, base + f + 1)
                    w = rows(split(n, on))
                    for k in range(2):
                        for c in range(2):
                            last = three(psum[c][:, :], parts((HH, HL), ALL, half, slice(k * P, (k + 1) * P)),
                                         parts(w, ALL, k, slice(c * 512, (c + 1) * 512)),
                                         first and k == 0, final and k == 1)
                    last.then_inc(e_down, 1)

                def step(f, half, n, on, wait, turn_wait=True, first=False):
                    gate_or_up(f, half, 0, n, on, wait)
                    turn(f - 1, 1 - half, turn_wait)
                    gate_or_up(f, half, 1, n + 1, on, wait)
                    down(f - 1, 1 - half, n + 2, on, first)

                pe.wait_ge(scat_done, 4 * j + 1)
                gate_or_up(0, 0, 0, UE, further, False, gathering=True)
                pe.wait_ge(scat_done, 4 * j + 2)
                gate_or_up(0, 0, 1, UE + 1, further, False)
                pe.wait_ge(scat_done, 4 * j + 4)
                pe.wait_ge(pickT_ready, j + 1)
                step(1, 1, UE + 2, further, False, turn_wait=False, first=True)
                step(2, 0, UE + 5, further, True, turn_wait=False)
                with pe.Fori(1, NG // 2 - 1) as i:
                    step(2 * i + 1, 1, UE + 2, further + RING * i, True)
                    step(2 * i + 2, 0, UE + 5, further + RING * i, True)
                gate_or_up(NG - 1, 1, 0, UE + 3 * NG - 4, further, True)
                turn(NG - 2, 0, True)
                gate_or_up(NG - 1, 1, 1, UE + 3 * NG - 3, further, True)
                down(NG - 2, 0, UE + 3 * NG - 2, further)
                turn(NG - 1, 1, True)
                down(NG - 1, 1, UE + 3 * NG - 1, further, final=True)
                gather(j + 1)
                pe.wait_ge(ys_ready, j + 1)
                for t in range(NT):
                    for c in range(2):
                        bank, place = psum[4 + 2 * t + c][:, :], PICKT[:, t * P:(t + 1) * P]
                        mm(bank, place, YH[:, c * 512:(c + 1) * 512], start=True, stop=False)
                        mm(bank, place, YL[:, c * 512:(c + 1) * 512], start=False, stop=True).then_inc(scat_full, 1)

            def ple(L, base, further, jobs=0):
                first = 0 if L else 4
                if L:
                    pe.wait_ge(gathered, 2 * jobs + 2)
                w = rows(split(base, further))
                for n in range(4):
                    tokens(psum[first + n], w, (PH[:, L, :, :], PL[:, L, :, :]), 2,
                           slice(n * FG, (n + 1) * FG)).then_inc(filled, 1)
                turn_norm(3 * L + 2, 4 - first)
                for n in range(4):
                    if n:
                        data(pe, ("normT", 3 * L + 2, n))
                    tokens(psum[4 - first + n], cols(split(base + 1 + n, further)), (XH, XL),
                           arrival=None if n else ("normT", 3 * L + 2)).then_inc(filled, 1)

            for L in range(DEPTH):
                project(L)
                scan(L)
                mix_out(L)
                turn_norm(3 * L + 1, 4, [("yT", L, b) for b in range(4)])
                if L == 0:
                    dense()
                    ple(0, U0[("pp", 0)], 0)
                else:
                    route()
                    gather(0)
                    pe.wait_ge(table_ready, 1)
                    nj = NE + nc.tensor.value_load(JT[0:1, 15:16], min_val=0, max_val=NJMAX - NE)
                    with pe.Fori(0, nj) as j:
                        job(j)
                    ple(1, UE, 3 * NG * nj, nj)

        def both_ways(t, offset, m, step):
            return part_of(t, offset, [[step + m, 2], [2 * m, T // (2 * m)], [1, m]])

        def by_chunk(t, u, turn):
            return both_ways(t, (6 * turn + u) * T, CHUNK, -6 * T if turn else 6 * T)

        @block.scalar
        def _(act):
            fn = nc.scalar.activation

            def take(name, bank):
                act.wait_ge(filled, number[name][0])
                return psum[bank]

            def high(n, turns=0):
                act.wait_ge(slot_full[n % RING], 16 * (n // RING + 1) + 16 * turns)
                fn(W[:, n % SPLIT_RING, 0, :], ring[:, n % RING, :], ACT.Copy).then_inc(high_ready, 1)

            def follow(u):
                used(act, u)
                high(U0[u] + SPLIT_RING)

            def scaled_high(name, first_bank, column):
                for b in range(4):
                    bank = take(name + (b,), first_bank + b)
                    for c in range(2):
                        col = column(2 * b + c)
                        last = fn(XH[:, 2 * b + c, :], bank[:, c * T:(c + 1) * T], ACT.Copy, scale=RC[:, col:col + 1])
                    last.then_inc(xh_ready, 1)

            def squares_of(r, part):
                c = (0, FIRST_PART[r], D)[part:part + 2]
                for t in range(NT):
                    fn(hn[:, t, c[0]:c[1]], h[:, t, c[0]:c[1]], ACT.Square,
                       accum_out=STAT[:, part, r, t:t + 1]).then_inc(squares, 1)

            def root(r):
                act.wait_ge(squares, 4 * r + 4)
                act.wait_ge(rest_ready, r + 1)
                for t in range(NT):
                    last = fn(STAT[:, 4, r, t:t + 1], STAT[:, 1, r, t:t + 1], ACT.Sqrt, scale=1.0 / D,
                              bias=STAT[:, 3, r, t:t + 1])
                last.then_inc(root_ready, 1)

            def norm_first(r):
                act.wait_ge(h_first, r)
                squares_of(r, 0)

            def norm_last(r):
                fn(WARM[:, 1:2], WARM[:, 0:1], ACT.Sqrt)
                act.wait_ge(h_ready, r)
                squares_of(r, 1)
                root(r)

            def norm_whole(r, semaphore, value):
                fn(WARM[:, 1:2], WARM[:, 0:1], ACT.Sqrt)
                act.wait_ge(semaphore, value)
                squares_of(r, 0)
                squares_of(r, 1)
                root(r)

            def head_squares(L, bank, unit):
                act.wait_ge(av_done, L * NGROUP + GROUP0[unit] + GROUPS_OF[unit])
                for head in (2 * bank, 2 * bank + 1):
                    for t in range(NT):
                        n = 4 * bank + 2 * t + head % 2
                        fn(hn[:, t, head * P:(head + 1) * P], head_output(head, t), ACT.Square,
                           accum_out=HST[:, 0, n:n + 1]).then_inc(osq, 1)

            def mixer(L):
                last_unit = U0[("in", L, "hv", 1)]
                for part, piece, form, engine in PROJ:
                    if engine == "a":
                        bank = take((part, piece, L), PROJ_BANK[part, piece])
                        two = bank[:, :].rearrange("p (a n) -> p a n", a=2)
                        if part in ("gv", "hv"):
                            c = (0 if part == "gv" else 512) + piece * FG
                            fn(V[:, :, c:c + FG], two, ACT.Copy).then_inc(emptied["a"], 1)
                        elif form == "tok":
                            c = piece * FG + (512 if part == "hr" else 0)
                            fn(SR[:, :, c:c + FG], two, ACT.Silu).then_inc(emptied["a"], 1)
                        elif part == "hq":
                            fn(Q[:, 2 + 2 * piece:4 + 2 * piece, :], two, ACT.Silu).then_inc(emptied["a"], 1)
                        else:
                            d, u = (0 if part == "hff" else 1), 2 + 2 * piece
                            fn(G[:, d, u:u + 2, :], two, ACT.Sigmoid)
                            fn(K[:, d, u:u + 2, :], two, ACT.Sigmoid, scale=-1.0).then_inc(emptied["a"], 1)
                    if form != "decay" and U0[("in", L, part, piece)] + SPLIT_RING <= last_unit:
                        follow(("in", L, part, piece))
                    if part == "gq":
                        act.wait_ge(forget_ready, 2 * L + 2)
                        fn(G[:, :, 2:6, :], G[:, :, 2:6, :], ACT.Ln).then_inc(logf_ready, 1)
                    soft = hn[:, 0, :].rearrange("p (d u t) -> p d u t", d=2, u=2)
                    if (part, piece) == ("z", 1):
                        data(act, ("z", 1, L))
                        fn(soft, G[:, :, 0:2, :], ACT.Abs).then_inc(softplus_step, 1)
                        act.wait_ge(softplus_step, 3 * L + 1)
                        fn(soft, soft, ACT.Exp, scale=-1.0).then_inc(softplus_step, 1)
                    if (part, piece) == ("gv", 0):
                        act.wait_ge(softplus_step, 3 * L + 2)
                        fn(soft, soft, ACT.Ln, bias=1.0).then_inc(softplus_step, 1)
                act.wait_ge(sums_ready, L + 1)
                for d, place, c in ((0, 0, 1), (0, 3, 2), (1, 1, 2), (1, 2, 1)):
                    fn(EF[:, d, :, place], TOT[:, d, :, c], ACT.Exp).then_inc(edge_ready, 1)
                for u in range(6):
                    n, xb = L * 6 + u, decayed(L, u)
                    for i in range(len(LEVELS)):
                        act.wait_ge(diff_ready, 5 * n + (1, 3, 4)[i])
                        for role in range(2):
                            v = xb[:, 2 + i, role, :]
                            fn(v, v, ACT.Exp, scale=1.0 if role else -1.0).then_inc(exp_ready, 1)
                        if i == 0:
                            act.wait_ge(diff_ready, 5 * n + 2)
                            fn(xb[:, 1, :, :], xb[:, 0, :, :], ACT.Exp, scale=-1.0).then_inc(exp_ready, 1)
                            fn(xb[:, 0, :, :], xb[:, 0, :, :], ACT.Exp).then_inc(exp_ready, 1)
                    for turn in range(2):
                        last = fn(both_ways(xb, (5 * 2 + turn) * T, CHUNK, 0), by_chunk(G, u, turn), ACT.Exp)
                    last.then_inc(exp_ready, 1)
                    act.wait_ge(diff_ready, 5 * n + 5)
                    fn(xb[:, 6, :, :], xb[:, 6, :, :], ACT.Exp).then_inc(exp_ready, 1)
                    if u > 3:
                        head_squares(L, u - 4, u - 4)
                head_squares(L, 2, 3)
                act.wait_ge(omean, 2 * L + 1)
                fn(HST[:, 2, 0:12], HST[:, 1, 0:12], ACT.Sqrt).then_inc(oroot, 1)
                act.wait_ge(score_full, L * NGROUP + GROUP0[4])
                high(last_unit + 1)
                act.wait_ge(score_full, L * NGROUP + GROUP0[5])
                high(last_unit + 2)
                head_squares(L, 3, 5)
                act.wait_ge(omean, 2 * L + 2)
                fn(HST[:, 2, 12:16], HST[:, 1, 12:16], ACT.Sqrt).then_inc(oroot, 1)
                scaled_high(("yT", L), 4, lambda k: (C_GON if k < 4 else C_HON) + L)
                high(last_unit + 3)
                for n in range(4):
                    if n == 3:
                        norm_first(3 * L + 1)
                        norm_last(3 * L + 1)
                    follow(("out", L, n))

            def dense():
                first = U0[("dg", 0)]

                def step(f, half, turns, wait):
                    n = first + 3 * (f if isinstance(f, int) else 2 - half) + 2
                    act.wait_ge(gu_full[0], f + 1)
                    if wait:
                        act.wait_ge(hs_ready, f - 1)
                    fn(SG[:, half, :], psum[4 + 2 * half][:, :], ACT.Silu).then_inc(silu_ready, 1)
                    if not isinstance(f, int) or f:
                        high(n, turns)
                    else:
                        high(first + 3)
                    act.wait_ge(gu_full[1], f + 1)
                    high(n + 1 if not isinstance(f, int) or f else first + 4, turns)
                    act.wait_ge(hs_ready, f + 1)
                    if wait:
                        act.wait_ge(down_done, f - 1)
                    fn(HH[:, half, :], HS[:, half, :], ACT.Copy).then_inc(hh_ready, 1)
                    if not isinstance(f, int) or f:
                        act.wait_ge(down_done, f)
                        high(n + 2, turns)

                step(0, 0, 0, False)
                step(1, 1, 0, False)
                step(2, 0, 0, True)
                with act.Fori(1, ND // 2) as i:
                    step(2 * i + 1, 1, i, True)
                    step(2 * i + 2, 0, i, True)
                norm_first(2)
                norm_last(2)
                act.wait_ge(down_done, ND)
                high(first + 3 * ND + 2)

            def gather_high(j):
                for b in range(2):
                    act.wait_ge(gather_full, 2 * j + b + 1)
                    for k in range(4 * b, 4 * b + 4):
                        c = C_FFN + KD + k
                        last = fn(VH[:, k, :], psum[2 + b][:, (k % 4) * P:(k % 4 + 1) * P], ACT.Copy,
                                  scale=RC[:, c:c + 1])
                    last.then_inc(vh_ready, 1)

            def job(j):
                base, jt = NG * j, 3 * NG // RING * j

                def silu(f, half, wait):
                    act.wait_ge(e_gate, base + f + 1)
                    if wait:
                        act.wait_ge(e_hid, base + f - 1)
                    fn(SG[:, half, 0:FG], psum[4 + 2 * half][:, 0:FG], ACT.Silu).then_inc(e_silu, 1)

                def turned(f, half, wait):
                    act.wait_ge(e_ht_full, base + f + 1)
                    if wait:
                        act.wait_ge(e_down, base + f - 1)
                    fn(HH[:, half, 0:FG], psum[2 + half][:, 0:FG], ACT.Copy).then_inc(e_hh, 1)

                def step(f, half, n, turns, wait, turned_wait):
                    silu(f, half, wait)
                    turned(f - 1, 1 - half, turned_wait)
                    high(UE + n, turns)
                    act.wait_ge(e_up, base + f + 1)
                    high(UE + n + 1, turns)
                    act.wait_ge(e_down, base + f)
                    high(UE + n + 2, turns)

                act.wait_ge(pickT_full, j + 1)
                fn(PICKT[:, :], psum[2][:, 0:T], ACT.Copy).then_inc(pickT_ready, 1)
                silu(0, 0, False)
                high(UE + 3, jt)
                act.wait_ge(e_up, base + 1)
                high(UE + 4, jt)
                step(1, 1, 5, jt, False, False)
                step(2, 0, 8, jt, True, False)
                with act.Fori(1, NG // 2 - 1) as i:
                    step(2 * i + 1, 1, 5, jt + i, True, True)
                    step(2 * i + 2, 0, 8, jt + i, True, True)
                silu(NG - 1, 1, True)
                turned(NG - 2, 0, True)
                high(UE + 3 * NG - 1, jt)
                act.wait_ge(e_up, base + NG)
                high(UE + 3 * NG, jt)
                turned(NG - 1, 1, True)
                act.wait_ge(e_down, base + NG - 1)
                high(UE + 3 * NG + 1, jt)
                act.wait_ge(e_down, base + NG)
                for c in range(2):
                    fn(YH[:, c * 512:(c + 1) * 512], psum[c][:, :], ACT.Copy).then_inc(yh_ready, 1)
                gather_high(j + 1)
                high(UE + 3 * NG + 2, jt)

            def ple(L, base, turns):
                act.wait_ge(filled, number[("pp", L, 3)][0])
                high(base + SPLIT_RING, turns)
                scaled_high(("normT", 3 * L + 2), 4 if L else 0, lambda k: C_PLE + KD * L + k)
                for n in range(4):
                    if n == 3:
                        norm_first(3 * L + 3)
                    bank = take(("pg", L, n), (4 if L else 0) + n)
                    if n >= 2:
                        data(act, ("pp", L, n - 2))
                    fn(SG[:, n % 2, :], bank[:, :], ACT.Sigmoid).then_inc(emptied["a"], 1)
                    if n < (1 if L else 3):
                        high(base + SPLIT_RING + 1 + n, turns)

            act.wait_ge(zeroed, 1)
            norm_whole(0, x_in, 16)
            high(0)
            data(act, "rows")
            for L in range(DEPTH):
                if L:
                    norm_last(3 * L)
                    follow(("pg", 0, 3))
                scaled_high(("normT", 3 * L), 0, lambda k: C_MIX + KD * L + k)
                if L == 0:
                    for layer in range(DEPTH):
                        fn(PH[:, layer, :, :], take(("pT", layer), 5 + layer)[:, :].rearrange("p (a n) -> p a n", a=2),
                           ACT.Copy).then_inc(xh_ready, 1)
                    for n in range(1, SPLIT_RING):
                        high(n)
                    act.wait_ge(lb_shifted, 1)
                    fn(LBX[:, 3:5, :], LBX[:, 1:3, :], ACT.Exp).then_inc(lb_exp, 1)
                    fn(WRH[:, :, :], WR[:, :, :], ACT.Copy).then_inc(router_high, 1)
                mixer(L)
                scaled_high(("normT", 3 * L + 1), 4, lambda k: C_FFN + KD * L + k)
                if L == 0:
                    dense()
                    further = 0
                else:
                    act.wait_ge(filled, number["logitsT"][0])
                    for t in range(NT):
                        fn(NH[:, t, :], h[:, t, :], ACT.Copy, scale=STAT[:, 2, 4, t:t + 1]).then_inc(nh_ready, 1)
                    act.wait_ge(rt_shift, 1)
                    for t in range(NT):
                        fn(RT[:, 2, t * 8:(t + 1) * 8], RT[:, 1, t * 8:(t + 1) * 8], ACT.Exp,
                           accum_out=RT[:, 3, t:t + 1]).then_inc(rt_exp, 1)
                    gather_high(0)
                    act.wait_ge(table_ready, 1)
                    nj = NE + nc.scalar.value_load(JT[0:1, 15:16], min_val=0, max_val=NJMAX - NE)
                    with act.Fori(0, nj) as j:
                        job(j)
                    further = 3 * NG // RING * nj
                if L:
                    norm_whole(5, scat_done, 4 * nj + 4)
                ple(L, U0[("pp", 0)] if L == 0 else UE, further)
            norm_last(6)

        @block.gpsimd
        def _(pool):
            for L in range(DEPTH):
                for u in range(6):
                    n, xb = L * 6 + u, decayed(L, u)

                    def times(dst, src, other, ready):
                        pool.wait_ge(exp_ready, 10 * n + ready)
                        nc.gpsimd.tensor_tensor(dst, src, other, ALU.mult).then_inc(decayed_ready, 1)

                    for i, m in enumerate(LEVELS):
                        v = both_ways(xb, (2 + i) * 2 * T, m, 0)
                        times(v, v, both_ways(K, u * T, m, 6 * T), (1, 5, 7)[i])
                        v = xb[:, 2 + i, 1, :]
                        times(v, v, Q[:, u, :], (2, 6, 8)[i])
                    times(xb[:, 5, :, :], xb[:, 5, :, :], part_of(Q, u * T, [[0, 2], [1, T]]), 9)
                    pool.wait_ge(exp_ready, 10 * n + 10)
                    v = both_ways(xb, 6 * 2 * T, CHUNK, 0)
                    nc.gpsimd.tensor_tensor(v, v, by_chunk(K, u, 0), ALU.mult)
                    v = both_ways(xb, 6 * 2 * T + T, CHUNK, 0)
                    times(v, v, by_chunk(K, u, 1), 10)
                    pool.wait_ge(edge_ready, 4 * L + 4)
                    pool.wait_ge(decayed_ready, 10 * n + 8)
                    o5, o6, o7 = (a * 2 * T for a in (5, 6, 7))
                    ef = u * 4
                    on, back = [[T + CHUNK, 2], [1, CHUNK]], [[CHUNK - T, 2], [1, CHUNK]]
                    near, edge = [[CHUNK, 2], [1, CHUNK]], [[1, 2], [0, CHUNK]]
                    nc.gpsimd.tensor_tensor(part_of(xb, o7, near), part_of(xb, o6, on), part_of(EF, ef, edge), ALU.mult)
                    times(part_of(xb, o7 + T, near), part_of(xb, o6 + T + P, back), part_of(EF, ef + 24, edge), 10)
                    nc.gpsimd.tensor_tensor(part_of(xb, o7 + P, near), part_of(xb, o5 + P, on),
                                            part_of(EF, ef + 2, edge), ALU.mult)
                    times(part_of(xb, o7 + T + P, near), part_of(xb, o5 + T, back), part_of(EF, ef + 26, edge), 10)

        @block.vector
        def _(dve):
            tt, ts, stt = nc.vector.tensor_tensor, nc.vector.tensor_scalar, nc.vector.scalar_tensor_tensor
            steps = [0]

            def link(ins):
                steps[0] += 1
                ins.then_inc(dve_step, 1)
                dve.wait_ge(dve_step, steps[0])

            def take(name, bank):
                dve.wait_ge(filled, number[name][0])
                return psum[bank]

            def low(n, further=0):
                dve.wait_ge(high_ready, n + 1 + further)
                s = n % SPLIT_RING
                tt(W[:, s, 1, :], ring[:, n % RING, :], W[:, s, 0, :].bitcast(F32), ALU.subtract).then_inc(split_ready, 1)

            def reciprocal_root(r):
                dve.wait_ge(squares, 4 * r + 2)
                ts(STAT[:, 3, r, :], STAT[:, 0, r, :], 1.0 / D, EPS, ALU.mult, ALU.add).then_inc(rest_ready, 1)
                dve.wait_ge(root_ready, r + 1)
                link(nc.vector.reciprocal(STAT[:, 2, r, :], STAT[:, 4, r, :]))
                if r < 6:
                    for t in range(NT):
                        last = ts(SCALE[:, t, :], ident, STAT[:, 2, r, t:t + 1], None, ALU.mult)
                    last.then_inc(scale_ready, 1)

            nc.vector.memset(WARM[:, :], 0.0)
            nc.vector.memset(WG2[:, :, :, :], 0.0).then_inc(zeroed, 1)
            nc.vector.memset(ZB[:, :], 0.0)
            nc.vector.memset(JF[:, :], 0.0)
            nc.vector.memset(JC[:, :, :], 0.0)
            link(nc.vector.memset(EF[:, :, :, :], 1.0))
            dve.wait_ge(small_in, 16 * NSMALL)
            reciprocal_root(0)
            nc.vector.tensor_copy(RC[:, :], take("rows", 7)[:, 0:NROW]).then_inc(emptied["v"], 1)
            low(0)
            data(dve, "rows")
            def scaled_low(name, first_bank, column):
                for b in range(4):
                    dve.wait_ge(xh_ready, HIGH_BEFORE[name] + b + 1)
                    bank = take(name + (b,), first_bank + b)
                    for c in range(2):
                        col = column(2 * b + c)
                        last = stt(XL[:, 2 * b + c, :], bank[:, c * T:(c + 1) * T], RC[:, col:col + 1],
                                   XH[:, 2 * b + c, :].bitcast(F32), ALU.mult, ALU.subtract)
                    last.then_inc(emptied["v"], 1)

            def bounds_and_router():
                l0, l1 = RC[:, C_LB:C_LB + 8], RC[:, C_LB + 8:C_LB + 16]
                link(tt(LBX[:, 0, :], l0, l1, ALU.max))
                tt(LBX[:, 1, :], l0, LBX[:, 0, :], ALU.subtract)
                tt(LBX[:, 2, :], l1, LBX[:, 0, :], ALU.subtract).then_inc(lb_shifted, 1)
                dve.wait_ge(lb_exp, 1)
                link(tt(LBX[:, 5, :], LBX[:, 3, :], LBX[:, 4, :], ALU.add))
                link(nc.vector.reciprocal(LBX[:, 0, :], LBX[:, 5, :]))
                tt(LBX[:, 1, :], LBX[:, 3, :], LBX[:, 0, :], ALU.mult)
                link(tt(LBX[:, 2, :], LBX[:, 4, :], LBX[:, 0, :], ALU.mult))
                tt(LB[:, 0, :], LBX[:, 1, :], LBX[:, 1, :], ALU.subtract)
                link(tt(LBX[:, 5, :], LBX[:, 1, :], LBX[:, 2, :], ALU.add))
                link(tt(LB[:, 1, :], LBX[:, 5, :], LBX[:, 1, :], ALU.subtract))
                link(ts(LB[:, 2:4, :], LB[:, 0:2, :], -1.0, 1.0, ALU.mult, ALU.add))

                dve.wait_ge(router_high, 1)
                tt(WRL[:, :, :], WR[:, :, :], WRH[:, :, :].bitcast(F32), ALU.subtract).then_inc(router_ready, 1)

            def mixer(L):
                last_unit = U0[("in", L, "hv", 1)]
                g2 = G[:, :, 0:2, :].rearrange("p d u t -> p d (u t)")
                soft = hn[:, 0, :].rearrange("p (d n) -> p d n", d=2)

                def chunk_sums(units):
                    for u in units:
                        nc.vector.tensor_tensor_scan(G[:, 0, u, :], reset, G[:, 0, u, :], 0.0, ALU.mult, ALU.add)
                        back = part_of(G, (6 + u) * T + T - 1, [[-1, T]])
                        last = nc.vector.tensor_tensor_scan(back, reset, back, 0.0, ALU.mult, ALU.add)
                    return last

                def difference(u, part):
                    n, xb = L * 6 + u, decayed(L, u)
                    if part == 0:
                        if u >= 3:
                            dve.wait_ge(score_full, L * NGROUP + GROUP0[u - 2])
                        elif u < 2:
                            used(dve, ("in", L, *(("gv", 1), ("hv", 0))[u]))
                    if part < 3:
                        m = LEVELS[part]
                        for role, first, step in ((0, 0, 6 * T), (1, 6 * T, -6 * T)):
                            last = tt(both_ways(xb, (2 + part) * 2 * T + role * T, m, 0),
                                      both_ways(G, first + u * T, m, step),
                                      part_of(G, first + u * T + m - 1 + role,
                                              [[step + (1, -1)[role], 2], [2 * m, T // (2 * m)], [0, m]]),
                                      ALU.subtract)
                        last.then_inc(diff_ready, 1)
                    if part == 0:
                        tt(part_of(xb, 0, [[T, 2], [SUB, T // SUB], [1, SUB]]),
                           part_of(G, u * T, [[6 * T, 2], [SUB, T // SUB], [1, SUB]]),
                           part_of(G, u * T + SUB // 2 - 1, [[6 * T, 2], [SUB, T // SUB], [0, SUB]]),
                           ALU.subtract).then_inc(diff_ready, 1)
                    if part == 3:
                        for turn in range(2):
                            last = tt(both_ways(xb, (6 * 2 + turn) * T, CHUNK, 0),
                                      part_of(TOT, turn * 24 + u * 4, [[(25, -23)[turn], 2], [2, 2], [0, CHUNK]]),
                                      by_chunk(G, u, turn), ALU.subtract)
                        last.then_inc(diff_ready, 1)

                def diagonal(u):
                    n, xb = L * 6 + u, decayed(L, u)
                    dve.wait_ge(exp_ready, 10 * n + 4)
                    stt(xb[:, 0, :, :], xb[:, 0, :, :], SUB_SCALE, part_of(Q, u * T, [[0, 2], [1, T]]),
                        ALU.mult, ALU.mult).then_inc(diag_ready, 1)
                    stt(xb[:, 1, :, :], xb[:, 1, :, :], SUB_SCALE, K[:, :, u, :],
                        ALU.mult, ALU.mult).then_inc(diag_ready, 1)

                for part, piece, form, engine in PROJ:
                    if engine == "v":
                        bank = take((part, piece, L), PROJ_BANK[part, piece])
                        two = bank[:, :].rearrange("p (a n) -> p a n", a=2)
                    if part == "glr":
                        nc.vector.tensor_copy(GLT[:, :], bank[0:2 * RANK, 0:T]).then_inc(emptied["v"], 1)
                    elif part == "gq":
                        ts(Q[:, 0:2, :], two, float(P // 2) ** -0.5, None, ALU.mult).then_inc(emptied["v"], 1)
                    elif part == "gk":
                        nc.vector.tensor_copy(K[:, 0, 0:2, :], two)
                        nc.vector.tensor_copy(K[:, 1, 0:2, :], two).then_inc(emptied["v"], 1)
                    elif part == "z":
                        for u in range(2):
                            c = C_BG + 4 * L + 2 * piece + u
                            last = ts(G[:, piece, u, :], bank[:, u * T:(u + 1) * T], RC[:, c:c + 1], None, ALU.add)
                        last.then_inc(emptied["v"], 1)
                    elif part in ("gv", "hv") and engine == "v":
                        c = (0 if part == "gv" else 512) + piece * FG
                        nc.vector.tensor_copy(V[:, :, c:c + FG], two).then_inc(emptied["v"], 1)
                    if form != "decay" and U0[("in", L, part, piece)] + SPLIT_RING <= last_unit:
                        low(U0[("in", L, part, piece)] + SPLIT_RING)
                    if (part, piece) == ("hff", 0):
                        data(dve, ("hq", 1, L))
                        ts(Q[:, 2:6, :], Q[:, 2:6, :], float(P) ** -0.5, None, ALU.mult)
                    if (part, piece) in (("hfb", 0), ("glr", 0)):
                        d = 0 if part == "hfb" else 1
                        data(dve, (("hff", "hfb")[d], 1, L))
                        for u in range(4):
                            c = 4 * d + u
                            ts(K[:, d, 2 + u, :], K[:, d, 2 + u, :], LB[:, 2 + L, c:c + 1], None, ALU.mult)
                            last = ts(G[:, d, 2 + u, :], G[:, d, 2 + u, :], LB[:, 2 + L, c:c + 1],
                                      LB[:, L, c:c + 1], ALU.mult, ALU.add)
                        link(last)
                        ts(G[:, d, 2:6, :], G[:, d, 2:6, :], F_MIN, None, ALU.max).then_inc(forget_ready, 1)
                    if (part, piece) in (("gk", 0), ("z", 0)):
                        dve.wait_ge(logf_ready, L + 1)
                        chunk_sums(range(2, 4) if part == "gk" else range(4, 6))
                    if (part, piece) == ("gv", 0):
                        dve.wait_ge(softplus_step, 3 * L + 3)
                        data(dve, ("z", 1, L))
                        link(stt(g2, g2, 0.0, soft, ALU.min, ALU.subtract))
                        link(ts(g2, g2, 1.0 / 16.0, LN_F_MIN, ALU.mult, ALU.max))
                        link(chunk_sums(range(2)))
                        nc.vector.tensor_copy(TOT[:, 0, :, :], G[:, 0, :, CHUNK - 1:T:CHUNK])
                        nc.vector.tensor_copy(TOT[:, 1, :, :], G[:, 1, :, 0:T:CHUNK]).then_inc(sums_ready, 1)
                        dve.wait_ge(sums_ready, L + 1)
                    if (part, piece) == ("gv", 1):
                        for i in range(4):
                            difference(0, i)
                    elif (part, piece) == ("hv", 0):
                        diagonal(0)
                def head_means(a, b):
                    dve.wait_ge(osq, 16 * L + b)
                    ts(HST[:, 1, a:b], HST[:, 0, a:b], 1.0 / P, HEAD_EPS, ALU.mult, ALU.add).then_inc(omean, 1)

                def gated(bank):
                    for head in (2 * bank, 2 * bank + 1):
                        for t in range(NT):
                            n, c = 4 * bank + 2 * t + head % 2, head * P
                            last = stt(hn[:, t, c:c + P], head_output(head, t), HST[:, 3, n:n + 1],
                                       SR[:, t, c:c + P], ALU.mult, ALU.mult)
                    return last

                def mask(g):
                    n = L * NGROUP + g
                    if g == 0:
                        dve.wait_ge(masks_in, 16)
                    w = 384 if PART_OF[g] else 512
                    dve.wait_ge(score_full, n + 1)
                    if g >= 4:
                        dve.wait_ge(av_done, L * NGROUP + TAKEN_AT[g - 4])
                    elif L:
                        dve.wait_ge(av_done, L * NGROUP)
                    tt(masked_scores(L, n)[:, 0:w], psum[4 + n % 4][:, 0:w], CST[:, O_MASK + PART_OF[g] * 512:][:, 0:w],
                       ALU.mult).then_inc(masked, 1)

                def add_up(g):
                    n = L * NGROUP + g
                    dve.wait_ge(masked, n + 1)
                    a = masked_scores(L, n)
                    tt(a[:, 0:256], a[:, 0:256], a[:, 256:512], ALU.add).then_inc(summed, 1)

                for u in range(6):
                    for g in range(GROUPS_OF[u]):
                        mask(GROUP0[u] + g)
                        if g and PART_OF[GROUP0[u] + g - 1] == 0:
                            add_up(GROUP0[u] + g - 1)
                        if u == 0:
                            difference(1 + g // 4, g % 4)
                        elif g < 4 and u < 4:
                            difference(u + 2, g)
                        if g == (5 if u == 0 else 1) and u < 5:
                            diagonal(u + 1)
                        if u == 5 and g == 2:
                            head_means(0, 12)
                dve.wait_ge(oroot, 2 * L + 1)
                link(nc.vector.reciprocal(HST[:, 3, 0:12], HST[:, 2, 0:12]))
                gated(0)
                gated(1).then_inc(y_ready, 1)
                gated(2).then_inc(y_ready, 1)
                head_means(12, 16)
                dve.wait_ge(oroot, 2 * L + 2)
                link(nc.vector.reciprocal(HST[:, 3, 12:16], HST[:, 2, 12:16]))
                gated(3).then_inc(y_ready, 1)
                low(last_unit + 1)
                scaled_low(("yT", L), 4, lambda k: (C_GON if k < 4 else C_HON) + L)
                low(last_unit + 2)
                low(last_unit + 3)
                for n in range(4):
                    two = take(("mix", L, n), n)[:, :].rearrange("p (a n) -> p a n", a=2)
                    hv = h[:, :, n * FG:(n + 1) * FG]
                    tt(hv, two, hv, ALU.add).then_inc(emptied["v"], 1)
                    if n > 1:
                        data(dve, ("mix", L, n))
                        nc.vector.memset(LBX[:, 0, 0:1], 0.0).then_inc((h_first, h_ready)[n - 2], 1)
                    if n < 3:
                        low(U0[("out", L, n)] + SPLIT_RING)
                reciprocal_root(3 * L + 1)
                low(U0[("out", L, 3)] + SPLIT_RING)

            def dense():
                first = U0[("dg", 0)]

                def step(f, half, further):
                    static = isinstance(f, int)
                    n = first + 3 * (f if static else 2 - half) + 2
                    if static and f == 0:
                        low(first + 3)
                    else:
                        low(n, further)
                    dve.wait_ge(silu_ready, f + 1)
                    dve.wait_ge(gu_full[1], f + 1)
                    tt(HS[:, half, :], psum[5 + 2 * half][:, :], SG[:, half, :], ALU.mult).then_inc(hs_ready, 1)
                    low(first + 4 if static and f == 0 else n + 1, further)
                    dve.wait_ge(hh_ready, f + 1)
                    tt(HL[:, half, :], HS[:, half, :], HH[:, half, :].bitcast(F32), ALU.subtract).then_inc(hidden_ready, 1)
                    if not (static and f == 0):
                        low(n + 2, further)

                step(0, 0, 0)
                step(1, 1, 0)
                step(2, 0, 0)
                with dve.Fori(1, ND // 2) as i:
                    step(2 * i + 1, 1, RING * i)
                    step(2 * i + 2, 0, RING * i)
                dve.wait_ge(down_done, ND)
                for c in range(2):
                    for t in range(NT):
                        hv = h[:, t, c * 512:(c + 1) * 512]
                        last = tt(hv, psum[2 * t + c][:, :], hv, ALU.add)
                    last.then_inc((h_first, h_ready)[c], 1)
                reciprocal_root(2)
                low(first + 3 * ND + 2)

            def route():
                both = lambda row, w=NE: RT[:, row, 0:NT * NE].rearrange("p (t e) -> p t e", t=NT)[:, :, 0:w]
                wide = lambda a: a.to_broadcast([P, NT, NE])
                iotas = iota8.unsqueeze(1).to_broadcast([P, NT, NE])
                row = lambda n, t: RT[:, n, NE * t:NE * (t + 1)]
                nc.vector.tensor_copy(GLT[0:NE, :], take("logitsT", 4)[0:NE, 0:T]).then_inc(emptied["v"], 1)
                nc.vector.tensor_copy(RT[:, 0, :], take("logits", 4)[:, 0:16]).then_inc(emptied["v"], 1)
                data(dve, "logits")
                nc.vector.max(row(5, 0), row(0, 0))
                link(nc.vector.max(row(5, 1), row(0, 1)))
                tt(both(1), both(0), wide(both(5, 1)), ALU.subtract).then_inc(rt_shift, 1)
                dve.wait_ge(rt_exp, 2)
                link(nc.vector.reciprocal(RT[:, 3, 2:4], RT[:, 3, 0:2]))
                link(tt(both(4), both(2), wide(RT[:, 3, 2:4].unsqueeze(2)), ALU.mult))
                nc.vector.max(row(6, 0), row(4, 0))
                link(nc.vector.max(row(6, 1), row(4, 1)))
                nc.vector.max_index(IDX[:, 0, :], row(6, 0), row(4, 0))
                link(nc.vector.max_index(IDX[:, 1, :], row(6, 1), row(4, 1)))
                link(nc.vector.tensor_copy(both(7), IDX[:, :, :]))
                tt(both(9), iotas, wide(both(7, 1)), ALU.is_equal)
                link(tt(both(10), iotas, wide(both(7, 2)[:, :, 1:2]), ALU.is_equal))
                gates, picks = RT[:, 13, :], RT[:, 8, :]
                tt(picks, RT[:, 9, :], RT[:, 10, :], ALU.add).then_inc(rt_mask, 1)
                first, second = both(6, 1), both(6, 2)[:, :, 1:2]
                link(tt(RT[:, 3, 4:6].unsqueeze(2), first, second, ALU.add))
                link(nc.vector.reciprocal(RT[:, 3, 6:8], RT[:, 3, 4:6]))
                link(tt(both(11), both(6), wide(RT[:, 3, 6:8].unsqueeze(2)), ALU.mult))
                tt(both(12), both(9), wide(both(11, 1)), ALU.mult)
                link(tt(both(15), both(10), wide(both(11, 2)[:, :, 1:2]), ALU.mult))
                link(tt(gates, RT[:, 12, :], RT[:, 15, :], ALU.add))
                for t in range(NT):
                    dve.wait_ge(nh_ready, t + 1)
                    stt(NL[:, t, :], h[:, t, :], STAT[:, 2, 4, t:t + 1], NH[:, t, :].bitcast(F32),
                        ALU.mult, ALU.subtract).then_inc(hn_ready, 1)
                bank = take("rank", 5)
                nc.vector.tensor_copy(RT[:, 14, 0:8], bank[:, 16:24])
                link(stt(RT[:, 15, :], bank[:, 0:16], 1.0, picks, ALU.add, ALU.mult))
                nc.vector.memset(LBX[:, 0, 0:1], 0.0).then_inc(emptied["v"], 1)
                place = RT[:, 16, :]
                link(ts(place, RT[:, 15, :], -1.0, None, ALU.add))
                for t in range(NT):
                    nc.vector.tensor_copy(JC[:, 0:NE, t], place[:, 8 * t:8 * t + 8])
                    last = nc.vector.tensor_copy(JC[:, 0:NE, 2 + t], gates[:, 8 * t:8 * t + 8])
                link(last)

            def further_jobs():
                gates, place = RT[:, 13, :], RT[:, 16, :]
                over, upto, rank = RT[:, 17, 0:8], RT[:, 18, 0:8], RT[:, 19, 0:8]
                link(ts(over, RT[:, 14, 0:8], CAP + 0.5, None, ALU.is_gt))
                link(nc.vector.tensor_tensor_scan(upto, ones[:, 0:8], over, 0.0, ALU.mult, ALU.add))
                tt(rank, upto, over, ALU.subtract)
                nc.vector.tensor_copy(JF[:, 0:NE], iota8)
                link(nc.vector.tensor_copy(JF[:, 15:16], upto[:, 7:8]))
                for e in range(NJMAX - NE):
                    sel, scr = RT[:, 20, 0:8], RT[:, 21, 0:8]
                    link(stt(sel, rank, float(e), over, ALU.is_equal, ALU.mult))
                    link(stt(scr, sel, 1.0, iota8, ALU.mult, ALU.mult, accum_out=JF[:, NE + e:NE + e + 1]))
                    for t in range(NT):
                        w = slice(8 * t, 8 * t + 8)
                        link(stt(scr, sel, 1.0, place[:, w], ALU.mult, ALU.mult, accum_out=RT[:, 22, t:t + 1]))
                        link(stt(scr, sel, 1.0, gates[:, w], ALU.mult, ALU.mult, accum_out=JC[:, NE + e, 2 + t:3 + t]))
                    link(ts(JC[:, NE + e, 0:2], RT[:, 22, 0:2], -float(CAP), None, ALU.add))
                nc.vector.memset(LBX[:, 0, 0:1], 0.0).then_inc(scat_done, 4)
                nc.vector.tensor_copy(JT[:, :], JF[:, :]).then_inc(table_ready, 1)
                dve.wait_ge(table_ready, 1)

            def picks(j):
                nc.vector.tensor_copy(PLACE[:, :], JC[:, bass.ds(j, 1), 0:NT].rearrange("p a c -> p (a c)"))\
                    .then_inc(place_ready, 1)
                dve.wait_ge(place_ready, j + 1)
                for t in range(NT):
                    ts(PICK[:, t, :], iota, PLACE[:, t:t + 1], None, ALU.is_equal).then_inc(pick_ready, 1)

            def gather_low(j):
                for b in range(2):
                    dve.wait_ge(vh_ready, 2 * j + b + 1)
                    for k in range(4 * b, 4 * b + 4):
                        c = C_FFN + KD + k
                        last = stt(VL[:, k, :], psum[2 + b][:, (k % 4) * P:(k % 4 + 1) * P], RC[:, c:c + 1],
                                   VH[:, k, :].bitcast(F32), ALU.mult, ALU.subtract)
                    last.then_inc(gathered, 1)

            def job(j):
                base, further = NG * j, 3 * NG * j
                dve.wait_ge(scat_done, 4 * j + 4)
                nc.vector.tensor_copy(GATE[:, :], JC[:, bass.ds(j, 1), NT:2 * NT].rearrange("p a c -> p (a c)"))\
                    .then_inc(gate_ready, 1)

                def hidden(f, half, wait):
                    dve.wait_ge(e_silu, base + f + 1)
                    dve.wait_ge(e_up, base + f + 1)
                    if wait:
                        dve.wait_ge(e_ht_full, base + f - 1)
                    tt(HS[:, half, 0:FG], psum[5 + 2 * half][:, 0:FG], SG[:, half, 0:FG], ALU.mult).then_inc(e_hid, 1)

                def turned(f, half):
                    dve.wait_ge(e_hh, base + f + 1)
                    tt(HL[:, half, 0:FG], psum[2 + half][:, 0:FG], HH[:, half, 0:FG].bitcast(F32),
                       ALU.subtract).then_inc(e_ht, 1)

                def step(f, half, n, on, wait):
                    turned(f - 1, 1 - half)
                    low(UE + n, on)
                    hidden(f, half, wait)
                    low(UE + n + 1, on)
                    low(UE + n + 2, on)

                low(UE + 3, further)
                hidden(0, 0, False)
                low(UE + 4, further)
                step(1, 1, 5, further, False)
                step(2, 0, 8, further, True)
                with dve.Fori(1, NG // 2 - 1) as i:
                    step(2 * i + 1, 1, 5, further + RING * i, True)
                    step(2 * i + 2, 0, 8, further + RING * i, True)
                dve.wait_ge(pickT_full, j + 1)
                picks(j + 1)
                turned(NG - 2, 0)
                low(UE + 3 * NG - 1, further)
                hidden(NG - 1, 1, True)
                turned(NG - 1, 1)
                low(UE + 3 * NG, further)
                low(UE + 3 * NG + 1, further)
                for c in range(2):
                    cols_ = slice(c * 512, (c + 1) * 512)
                    dve.wait_ge(yh_ready, 2 * j + c + 1)
                    last = tt(YL[:, cols_], psum[c][:, :], YH[:, cols_].bitcast(F32), ALU.subtract)
                last.then_inc(ys_ready, 1)
                gather_low(j + 1)
                dve.wait_ge(gate_ready, j + 1)
                for t in range(NT):
                    for c in range(2):
                        dve.wait_ge(scat_full, 4 * j + 2 * t + c + 1)
                        hv = h[:, t, c * 512:(c + 1) * 512]
                        stt(hv, psum[4 + 2 * t + c][:, :], GATE[:, t:t + 1], hv,
                            ALU.mult, ALU.add).then_inc(scat_done, 1)
                low(UE + 3 * NG + 2, further)

            def ple(L, base, further):
                low(base + SPLIT_RING, further)
                scaled_low(("normT", 3 * L + 2), 4 if L else 0, lambda k: C_PLE + KD * L + k)
                for n in range(4):
                    bank = take(("pp", L, n), (0 if L else 4) + n)
                    data(dve, ("pg", L, n))
                    tt(HS[:, n % 2, :], bank[:, :], SG[:, n % 2, :], ALU.mult).then_inc(emptied["v"], 1)
                    data(dve, ("pp", L, n))
                    hv = h[:, :, n * FG:(n + 1) * FG]
                    last = tt(hv, hv, HS[:, n % 2, :].rearrange("p (a n) -> p a n", a=2), ALU.add)
                    if n > 1:
                        last.then_inc((h_first, h_ready)[n - 2], 1)
                    if n < (1 if L else 3):
                        low(base + SPLIT_RING + 1 + n, further)

            for L in range(DEPTH):
                if L:
                    reciprocal_root(3 * L)
                    low(U0[("pg", 0, 3)] + SPLIT_RING)
                scaled_low(("normT", 3 * L), 0, lambda k: C_MIX + KD * L + k)
                if L == 0:
                    for layer in range(DEPTH):
                        dve.wait_ge(xh_ready, HIGH_BEFORE[("pT", layer)] + 1)
                        two = take(("pT", layer), 5 + layer)[:, :].rearrange("p (a n) -> p a n", a=2)
                        tt(PL[:, layer, :, :], two, PH[:, layer, :, :].bitcast(F32),
                           ALU.subtract).then_inc(emptied["v"], 1)
                    for n in range(1, SPLIT_RING):
                        low(n)
                    bounds_and_router()
                mixer(L)
                scaled_low(("normT", 3 * L + 1), 4, lambda k: C_FFN + KD * L + k)
                if L == 0:
                    dense()
                    ple(0, U0[("pp", 0)], 0)
                else:
                    route()
                    picks(0)
                    further_jobs()
                    gather_low(0)
                    nj = NE + nc.vector.value_load(JT[0:1, 15:16], min_val=0, max_val=NJMAX - NE)
                    with dve.Fori(0, nj) as j:
                        job(j)
                    dve.wait_ge(scat_done, 4 * nj + 4)
                    nc.vector.memset(LBX[:, 0, 0:1], 0.0).then_inc(h_first, 1)
                    nc.vector.memset(LBX[:, 0, 1:2], 0.0).then_inc(h_ready, 1)
                    reciprocal_root(5)
                    ple(1, UE, 3 * NG * nj)
            reciprocal_root(6)
            dve.wait_ge(last_in, 16)
            for t in range(NT):
                stt(hn[:, t, :], h[:, t, :], STAT[:, 2, 6, t:t + 1], NF[:, :], ALU.mult, ALU.mult).then_inc(out_ready, 1)


_INS = ["x", "p", "w_in", "gla_wg2", "gla_bg", "hg_lb_logits", "gla_onorm", "hg_onorm", "w_out", "norm_mix",
        "norm_ffn", "w_dense_gate", "w_dense_up", "w_dense_down", "w_router", "w_exp_gate", "w_exp_up",
        "w_exp_down", "w_ple_proj", "w_ple_gate", "norm_ple", "norm_final"]
_OUTS = [((1, T, D), "float32")]


def kernel(**inputs):
    import numpy as _np
    import concourse.bacc as _bacc
    from concourse import mybir as _mybir
    from concourse.bass_utils import run_bass_kernel_spmd as _run

    nc = _bacc.Bacc("TRN2", target_bir_lowering=False, num_devices=1)
    arrays, args = {}, []
    for name in _INS + ["consts"]:
        a = shape_constants(_np) if name == "consts" else _np.ascontiguousarray(inputs[name])
        arrays[f"in_{name}_dram"] = a
        args.append(nc.dram_tensor(f"in_{name}_dram", a.shape, _mybir.dt.from_np(a.dtype), kind="ExternalInput").ap())
    for i, (shape, dtype) in enumerate(_OUTS):
        dt = _mybir.dt.from_np(_np.dtype(dtype))
        args.append(nc.dram_tensor(f"out_{i}_dram", shape, dt, kind="ExternalOutput").ap())
    trunk_kernel(nc, *args)
    r = _run(nc, [arrays], core_ids=[0])
    got = tuple(r.results[0][f"out_{i}_dram"] for i in range(len(_OUTS)))
    return got[0]
```
